# Optimizing a Trainium2 kernel written in Bass

```python
import jax
import jax.numpy as jnp
from jax import lax
import numpy as np

D_MODEL = 2048
BATCH = 1
SEQ = 256
DEPTH = 2

CHUNK = 64
LN_EPS = 1e-5
ALPHA = (2 * DEPTH) ** 0.25
BETA = (8 * DEPTH) ** -0.25
N_EVEN = (DEPTH + 1) // 2
N_ODD = DEPTH // 2

CONV_CH = D_MODEL // 2
CONV_WIDTH = 31
HGRN_HEADS = 8
HGRN_DK = 128
HGRN_DV = (D_MODEL // 2) // HGRN_HEADS
HGRN_KDIM = HGRN_HEADS * HGRN_DK
HGRN_VDIM = HGRN_HEADS * HGRN_DV
FOX_HEADS = 8
FOX_DH = 128
FOX_WIDTH = FOX_HEADS * FOX_DH
FOX_QBLOCK = 128
CA_HEADS = 8
CA_DH = 128
CA_WIDTH = CA_HEADS * CA_DH
CA_LEFT_CHUNKS = 8
CA_BAND = (CA_LEFT_CHUNKS + 1) * CHUNK
REL_CLIP = 256
REL_TABLE = (CHUNK - 1) + REL_CLIP + 1
D_FF = 4 * D_MODEL

EVEN_IN = 2 * CONV_CH + 2 * HGRN_KDIM + 2 * HGRN_VDIM
ODD_IN = 3 * FOX_WIDTH + FOX_HEADS + 3 * CA_WIDTH

kernel_name = 'hybrid_conv_hgrn2_fox_chunkattn_trunk'

def layer_norm(x, g, b):
    xf = x.astype(jnp.float32)
    mu = jnp.mean(xf, axis=-1, keepdims=True)
    var = jnp.mean(jnp.square(xf - mu), axis=-1, keepdims=True)
    return ((xf - mu) * lax.rsqrt(var + LN_EPS) * g + b).astype(x.dtype)

def conformer_conv(u, conv_w, conv_b, ln_g, ln_b):
    a, gate = jnp.split(u, 2, axis=-1)
    h = a * jax.nn.sigmoid(gate)
    h = lax.conv_general_dilated(
        h, conv_w[:, None, :].astype(h.dtype), window_strides=(1,),
        padding=[(CONV_WIDTH - 1, 0)],
        dimension_numbers=('NWC', 'WIO', 'NWC'),
        feature_group_count=CONV_CH) + conv_b
    return jax.nn.silu(layer_norm(h, ln_g, ln_b))

def hgrn2(q, f_logit, i, g, lb, gnorm_g):
    B, S, _ = q.shape
    nc = S // CHUNK
    f32 = jnp.float32
    f = lb + (1.0 - lb) * jax.nn.sigmoid(f_logit.astype(f32))
    log_f = jnp.log(f)
    k = 1.0 - f

    def to_chunks(t, d):
        return t.astype(f32).reshape(B, nc, CHUNK, HGRN_HEADS, d).transpose(1, 0, 3, 2, 4)

    qc = to_chunks(jax.nn.silu(q), HGRN_DK)
    kc = to_chunks(k, HGRN_DK)
    vc = to_chunks(i, HGRN_DV)
    lc = to_chunks(log_f, HGRN_DK)
    causal = jnp.tril(jnp.ones((CHUNK, CHUNK), dtype=bool))[:, :, None]

    def step(state, inp):
        qb, kb, vb, lfb = inp
        L = jnp.cumsum(lfb, axis=2)
        diff = L[:, :, :, None, :] - L[:, :, None, :, :]
        decay = jnp.exp(jnp.where(causal, diff, -jnp.inf))
        scores = jnp.einsum('bhtk,bhsk,bhtsk->bhts', qb, kb, decay)
        o = (jnp.einsum('bhts,bhsv->bhtv', scores, vb)
             + jnp.einsum('bhtk,bhkv->bhtv', qb * jnp.exp(L), state))
        L_end = L[:, :, -1, :]
        state = (jnp.exp(L_end)[..., None] * state
                 + jnp.einsum('bhsk,bhsv->bhkv', kb * jnp.exp(L_end[:, :, None, :] - L), vb))
        return state, o

    s0 = jnp.zeros((B, HGRN_HEADS, HGRN_DK, HGRN_DV), f32)
    _, o = lax.scan(step, s0, (qc, kc, vc, lc))
    o = o.transpose(1, 0, 3, 2, 4).reshape(B, S, HGRN_HEADS, HGRN_DV)
    o = o * lax.rsqrt(jnp.mean(jnp.square(o), axis=-1, keepdims=True) + LN_EPS)
    o = o.reshape(B, S, HGRN_VDIM) * gnorm_g * jax.nn.silu(g.astype(f32))
    return o.astype(q.dtype)

def forgetting_attention(q, k, v, f_logit):
    B, S, _ = q.shape
    nb = S // FOX_QBLOCK
    heads = lambda t: t.reshape(B, S, FOX_HEADS, FOX_DH).transpose(0, 2, 1, 3)
    qh, kh, vh = heads(q), heads(k), heads(v)
    F = jnp.cumsum(jax.nn.log_sigmoid(f_logit.astype(jnp.float32)), axis=1).transpose(0, 2, 1)
    q_blocks = qh.reshape(B, FOX_HEADS, nb, FOX_QBLOCK, FOX_DH).transpose(2, 0, 1, 3, 4)
    F_blocks = F.reshape(B, FOX_HEADS, nb, FOX_QBLOCK).transpose(2, 0, 1, 3)
    kpos = jnp.arange(S)
    scale = FOX_DH ** -0.5

    def block(args):
        qb, Fb, bidx = args
        s = jnp.einsum('bhqd,bhkd->bhqk', qb, kh).astype(jnp.float32) * scale
        s = s + Fb[..., None] - F[:, :, None, :]
        qpos = bidx * FOX_QBLOCK + jnp.arange(FOX_QBLOCK)
        s = jnp.where(kpos[None, :] <= qpos[:, None], s, -jnp.inf)
        p = jax.nn.softmax(s, axis=-1).astype(vh.dtype)
        return jnp.einsum('bhqk,bhkd->bhqd', p, vh)

    out = lax.map(block, (q_blocks, F_blocks, jnp.arange(nb)))
    return out.transpose(1, 0, 3, 2, 4).reshape(B, S, FOX_WIDTH)

def chunked_relpos_attention(q, k, v, rel_bias):
    B, S, _ = q.shape
    nc = S // CHUNK
    left = CA_LEFT_CHUNKS * CHUNK
    qc = q.reshape(B, nc, CHUNK, CA_HEADS, CA_DH).transpose(1, 0, 3, 2, 4)
    pad = lambda t: jnp.pad(t.reshape(B, S, CA_HEADS, CA_DH),
                            ((0, 0), (left, 0), (0, 0), (0, 0))).transpose(0, 2, 1, 3)
    kp, vp = pad(k), pad(v)
    qi = jnp.arange(CHUNK)
    km = jnp.arange(CA_BAND)
    rel = (left + qi[:, None]) - km[None, :]
    bias = rel_bias[:, jnp.minimum(rel, REL_CLIP) + (CHUNK - 1)].astype(jnp.float32)
    scale = CA_DH ** -0.5

    def chunk(args):
        qb, c = args
        start = c * CHUNK
        kb = lax.dynamic_slice_in_dim(kp, start, CA_BAND, axis=2)
        vb = lax.dynamic_slice_in_dim(vp, start, CA_BAND, axis=2)
        s = jnp.einsum('bhqd,bhkd->bhqk', qb, kb).astype(jnp.float32) * scale + bias
        s = jnp.where(start + km >= left, s, -jnp.inf)
        p = jax.nn.softmax(s, axis=-1).astype(vb.dtype)
        return jnp.einsum('bhqk,bhkd->bhqd', p, vb)

    out = lax.map(chunk, (qc, jnp.arange(nc)))
    return out.transpose(1, 0, 3, 2, 4).reshape(B, S, CA_WIDTH)

def setup_inputs(seed: int = 0) -> dict:
    key = jax.random.key(seed)
    ks = jax.random.split(key, 19)
    f32 = jnp.float32

    def nrm(k, shape, scale):
        return scale * jax.random.normal(k, shape, f32)

    return {
        'x': nrm(ks[0], (BATCH, SEQ, D_MODEL), 1.0),
        'ev_w_in': nrm(ks[1], (N_EVEN, D_MODEL, EVEN_IN), D_MODEL ** -0.5),
        'ev_conv_w': nrm(ks[2], (N_EVEN, CONV_WIDTH, CONV_CH), CONV_WIDTH ** -0.5),
        'ev_conv_b': nrm(ks[3], (N_EVEN, CONV_CH), 0.02),
        'ev_conv_ln_g': 1.0 + nrm(ks[4], (N_EVEN, CONV_CH), 0.1),
        'ev_conv_ln_b': nrm(ks[5], (N_EVEN, CONV_CH), 0.02),
        'hgrn_lb_logits': nrm(ks[6], (N_EVEN + 1, HGRN_KDIM), 0.1),
        'ev_gnorm_g': 1.0 + nrm(ks[7], (N_EVEN, HGRN_VDIM), 0.1),
        'ev_w_out': nrm(ks[8], (N_EVEN, CONV_CH + HGRN_VDIM, D_MODEL), (CONV_CH + HGRN_VDIM) ** -0.5 * BETA),
        'od_w_in': nrm(ks[9], (N_ODD, D_MODEL, ODD_IN), D_MODEL ** -0.5),
        'fox_b_f': 3.0 + nrm(ks[10], (N_ODD, FOX_HEADS), 0.5),
        'rel_bias': nrm(ks[11], (N_ODD, CA_HEADS, REL_TABLE), 0.5),
        'od_w_out': nrm(ks[12], (N_ODD, FOX_WIDTH + CA_WIDTH, D_MODEL), (FOX_WIDTH + CA_WIDTH) ** -0.5 * BETA),
        'ln_mix_g': 1.0 + nrm(ks[13], (DEPTH, D_MODEL), 0.1),
        'ln_mix_b': nrm(ks[14], (DEPTH, D_MODEL), 0.02),
        'mlp_w1': nrm(ks[15], (DEPTH, D_MODEL, D_FF), D_MODEL ** -0.5),
        'mlp_w2': nrm(ks[16], (DEPTH, D_FF, D_MODEL), D_FF ** -0.5 * BETA),
        'ln_mlp_g': 1.0 + nrm(ks[17], (DEPTH, D_MODEL), 0.1),
        'ln_mlp_b': nrm(ks[18], (DEPTH, D_MODEL), 0.02),
    }

def reference(x, ev_w_in, ev_conv_w, ev_conv_b, ev_conv_ln_g, ev_conv_ln_b, hgrn_lb_logits,
              ev_gnorm_g, ev_w_out, od_w_in, fox_b_f, rel_bias, od_w_out, ln_mix_g, ln_mix_b,
              mlp_w1, mlp_w2, ln_mlp_g, ln_mlp_b):
    lower_bounds = jnp.cumsum(jax.nn.softmax(hgrn_lb_logits.astype(jnp.float32), axis=0), axis=0)
    for l in range(DEPTH):
        j = l // 2
        if l % 2 == 0:
            u = x @ ev_w_in[j]
            conv_in, hq, hf, hi, hg = jnp.split(
                u, [2 * CONV_CH, 2 * CONV_CH + HGRN_KDIM, 2 * CONV_CH + 2 * HGRN_KDIM,
                    2 * CONV_CH + 2 * HGRN_KDIM + HGRN_VDIM], axis=-1)
            a_out = conformer_conv(conv_in, ev_conv_w[j], ev_conv_b[j], ev_conv_ln_g[j], ev_conv_ln_b[j])
            b_out = hgrn2(hq, hf, hi, hg, lower_bounds[j], ev_gnorm_g[j])
            mix = jnp.concatenate([a_out, b_out], axis=-1) @ ev_w_out[j]
        else:
            u = x @ od_w_in[j]
            c_q, c_k, c_v, c_f, d_q, d_k, d_v = jnp.split(
                u, [FOX_WIDTH, 2 * FOX_WIDTH, 3 * FOX_WIDTH, 3 * FOX_WIDTH + FOX_HEADS,
                    3 * FOX_WIDTH + FOX_HEADS + CA_WIDTH, 3 * FOX_WIDTH + FOX_HEADS + 2 * CA_WIDTH], axis=-1)
            c_out = forgetting_attention(c_q, c_k, c_v, c_f + fox_b_f[j])
            d_out = chunked_relpos_attention(d_q, d_k, d_v, rel_bias[j])
            mix = jnp.concatenate([c_out, d_out], axis=-1) @ od_w_out[j]
        x = layer_norm(ALPHA * x + mix, ln_mix_g[l], ln_mix_b[l])
        h = jnp.square(jax.nn.relu(x @ mlp_w1[l])) @ mlp_w2[l]
        x = layer_norm(ALPHA * x + h, ln_mlp_g[l], ln_mlp_b[l])
    return x


_drawn_inputs = setup_inputs


def setup_inputs(seed=0):
    import zlib

    import numpy as np

    out = dict(_drawn_inputs(seed))
    spreads = {}
    factors = {'ev_conv_b': 8.0,
     'ev_conv_ln_g': 3.05,
     'ev_conv_ln_b': 8.0,
     'hgrn_lb_logits': 8.0,
     'ev_gnorm_g': 3.743,
     'fox_b_f': 36.92,
     'rel_bias': 3.23}
    for name, (base, spread) in spreads.items():
        noise = np.random.default_rng([zlib.crc32(name.encode()), seed]).standard_normal(out[name].shape)
        drawn = base * np.exp(spread * noise) if base else spread * noise
        out[name] = jnp.asarray(drawn.astype(out[name].dtype))
    for name, factor in factors.items():
        out[name] = (out[name] * factor).astype(out[name].dtype)
    return out
```

```python
from contextlib import ExitStack

import concourse.bass as bass
from concourse import mybir

F32, F32R, I8 = mybir.dt.float32, mybir.dt.float32r, mybir.dt.int8
ACT, ALU, AX = mybir.ActivationFunctionType, mybir.AluOpType, mybir.AxisListType

D = 2048
S = 256
P = 128
RT = S // P
KT = D // P
N = 512
CK = 2
CPT = KT // CK
DEPTH = 2
ALPHA = float((2 * DEPTH) ** 0.25)
EPS = 1e-5
CONV_CH, CONV_W = D // 2, 31
HEADS, DH = 8, 128
HG = 4
KDIM = HEADS * DH
REL_TABLE = 320
CHUNK = 64
D_FF = 4 * D
FB = D_FF // D
SCALE = float(DH) ** -0.5
NEG = -3.0e38
LEVELS = 7
F_MIN = 2.0 ** -63

F_COL, Q_COL, I_COL, G_COL = 2 * CONV_CH + KDIM, 2 * CONV_CH, 2 * CONV_CH + 2 * KDIM, 2 * CONV_CH + 3 * KDIM
EVEN_TILES = [F_COL, Q_COL, CONV_CH, 0, CONV_CH + N, N, I_COL, G_COL,
              F_COL + N, Q_COL + N, I_COL + N, G_COL + N]
FOX_F = 3 * KDIM
ODD_TILES = [base + third * KDIM for base in (0, N, FOX_F + HEADS, FOX_F + HEADS + N) for third in range(3)]
EVEN_OUT = [[8, 9, 10, 11, 0, 1, 2, 3, 4, 5, 6, 7], [12, 13, 14, 15]]
ODD_OUT = [list(range(12)), list(range(12, 16))]
NT = D // N
IN_SLOTS = 12 * CPT
OUT_A, OUT_B = 12 // CK, 4 // CK
LAYER_SLOTS = IN_SLOTS + NT * (OUT_A + OUT_B)
MLP_SLOTS = FB * 2 * NT * CPT
LAYER_TILES, MLP_TILES = 12 + 2 * NT, FB * 2 * NT
SLOT0 = [0, LAYER_SLOTS + MLP_SLOTS]
SLOT_MLP = [LAYER_SLOTS, 2 * LAYER_SLOTS + MLP_SLOTS]
TILE0 = [0, LAYER_TILES + MLP_TILES]
TILE_MLP = [LAYER_TILES, 2 * LAYER_TILES + MLP_TILES]
SLOTS = 2 * (LAYER_SLOTS + MLP_SLOTS)
RING = 4

P0_X = [0, 1]
P0 = {n: 2 + i for i, n in enumerate(["F0", "Q0", "C0", "C1", "O0", "F1", "Q1", "MEAN", "VAR", "O1"])}
P0_LN1 = [12, 13]
P0_MLP = [14, 54]
P0_LN2 = [30, 31]
P0_ATT = 32
P0_LN3 = [52, 53]
P1_CONST = 0
P1_X = [1, 2]
P1_HG = [3, 13]
P1_LN1 = [23, 24]
P1_LN2 = [25, 26]
P1 = {n: 27 + i for i, n in enumerate(["FL", "FC", "FB0", "S0", "P0", "FB1", "S1", "P1", "S2", "P2", "S3", "P3"])}
P1_LN3 = [39, 40]
LN0 = [P0_X, P0_LN1, P0_LN2, P0_LN3]
LN1 = [P1_X, P1_LN1, P1_LN2, P1_LN3]


def trunk(nc, x, ev_w_in, ev_conv_w, ev_conv_b, ev_conv_ln_g, ev_conv_ln_b, hgrn_lb_logits, ev_gnorm_g, ev_w_out,
          od_w_in, fox_b_f, rel_bias, od_w_out, ln_mix_g, ln_mix_b, mlp_w1, mlp_w2, ln_mlp_g, ln_mlp_b, out):
    w_in, w_out = [ev_w_in[0], od_w_in[0]], [ev_w_out[0], od_w_out[0]]
    with ExitStack() as ctx:
        def sb(name, shape, dt):
            return ctx.enter_context(nc.sbuf_tensor(name, shape, dt))

        def sem(name):
            return ctx.enter_context(nc.semaphore(name))

        raw = sb("raw", [P, RING, CK, N], F32)
        w_hi = sb("w_hi", [P, RING, CK, N], F32R)
        w_lo = sb("w_lo", [P, RING, CK, N], F32R)
        x_hi = sb("x_hi", [P, KT, S], F32R)
        x_lo = sb("x_lo", [P, KT, S], F32R)
        c_hi = sb("c_hi", [P, KT, S], F32R)
        c_lo = sb("c_lo", [P, KT, S], F32R)
        X = sb("X", [P, RT, D], F32)
        lnp = sb("lnp", [P, 2, D], F32)
        ident = sb("ident", [P, P], F32)
        stats = sb("stats", [P, RT, NT, 6], F32)
        mv = sb("mv", [P, RT, 2], F32)
        rstd = sb("rstd", [P, RT, 1], F32)
        mhalf = sb("mhalf", [P, S], F32)
        scr = sb("scr", [P, 14800], F32)
        used = [0]

        def cut(n):
            used[0] += n
            assert used[0] <= 14800, used[0]
            return scr[:, used[0] - n:used[0]]

        urow = [cut(RT * N).rearrange("p (r n) -> p r n", r=RT) for _ in range(2)]
        qT = cut(HG * S).rearrange("p (h t) -> p h t", h=HG)
        kT = cut(HG * S).rearrange("p (h t) -> p h t", h=HG)
        vrow = cut(RT * N).rearrange("p (r n) -> p r n", r=RT)
        both = used[0]
        L = cut(HG * S)
        Dm = cut(HG * S)
        Z = [cut(HG * S) for _ in range(2)]
        A = cut(HG * RT * P)
        Ax = cut(HG * P)
        G = cut(RT * N)
        PADW = CONV_W - 1 + S
        hpad = [cut(4 * PADW).rearrange("p (c t) -> p c t", c=4) for _ in range(2)]
        cw = cut(8 * CONV_W).rearrange("p (c j) -> p c j", c=8)
        small = cut(40)
        cpar = small[:, 0:24].rearrange("p (w c) -> p w c", w=3)
        lbl = small[:, 24:40].rearrange("p (w h) -> p w h", w=2)
        cw_rows, small_rows = Z[0], L[:, 0:P]
        lb = cut(8)
        oml = cut(8)
        ss = cut(8)
        crs = cut(S)
        meanw = cut(P)
        cv = lnp[:, 0, :].rearrange("p (c t) -> p c t", c=8)
        orow = lnp[:, 1, 0:RT * N]
        gn = lnp[:, 1, RT * N:RT * N + KDIM]
        reset = w = None
        csq = scr[:, both + 6 * 1024 + 512:both + 6 * 1024 + 512 + 2048].rearrange("p (c t) -> p c t", c=8)
        even_end = used[0]
        used[0] = both
        sm = cut(HG * (P + S))
        pT = cut(HG * (P + S))
        fbias = cut(HG * (P + S))
        rel = cut(HEADS * S).rearrange("p (h j) -> p h j", h=HEADS)
        U2 = cut(S)
        tri = cut(S)
        lsb = cut(RT * HG * P).rearrange("p (r h t) -> p r h t", r=RT, h=HG)
        wf = cut(KT * HEADS).rearrange("p (k h) -> p k h", k=KT)
        bf = cut(HEADS)
        zf = cut(RT * HEADS)
        za = cut(RT * HEADS)
        ls = cut(RT * HEADS)
        Fc = cut(RT * HEADS)
        mx = cut(RT * HG)
        sums = cut(RT * HG)
        rs = cut(RT * HG)
        wf_hi = sb("wf_hi", [P, KT, HEADS], F32R)
        wf_lo = sb("wf_lo", [P, KT, HEADS], F32R)
        rstm = sb("rstm", [P, HG * S], mybir.dt.bfloat16)
        masks = sb("masks", [P, LEVELS, CHUNK], I8)
        imask = sb("imask", [P, P], I8)

        gemm = [ctx.enter_context(nc.psum_tensor(f"gemm{i}", [P, RT, N], F32)) for i in range(2)]
        pair = [ctx.enter_context(nc.psum_tensor(f"pair{i}", [P, RT * N], F32)) for i in range(2)]
        quad = [p[:, :].rearrange("p (k t) -> p k t", k=4) for p in pair]

        raw_full = [sem(f"raw_full{i}") for i in range(RING)]
        hi_ready, lo_ready = sem("hi_ready"), sem("lo_ready")
        chunk_used = sem("chunk_used")
        relu_done = sem("relu_done")
        pair_full = [sem(f"pair_full{i}") for i in range(2)]
        params_ready = sem("params_ready")
        x_loaded, const_loaded, consts = sem("x_loaded"), sem("const_loaded"), sem("consts")
        odd_loaded, odd_consts, lnp_loaded = sem("odd_loaded"), sem("odd_consts"), sem("lnp_loaded")
        xt_hi, xt_ready = sem("xt_hi"), sem("xt_ready")
        cat_hi, cat_ready = sem("cat_hi"), sem("cat_ready")
        h_row, h_hi, h_ready = sem("h_row"), sem("h_hi"), sem("h_ready")
        act_link, dve_link, pool_link = sem("act_link"), sem("dve_link"), sem("pool_link")
        row_ready = sem("row_ready")
        x_sum, normed, x_scaled = sem("x_sum"), sem("normed"), sem("x_scaled")
        var_ready, rstd_ready = sem("var_ready"), sem("rstd_ready")
        gate_ready, h_ready_row, pad_ready = sem("gate_ready"), sem("h_ready_row"), sem("pad_ready")
        taps_done = sem("taps_done")
        lb_exp, lb_ready, f_ready, lnf_ready, L_ready = (sem("lb_exp"), sem("lb_ready"), sem("f_ready"),
                                                         sem("lnf_ready"), sem("L_ready"))
        sig_ready, q_ready, g_sig = sem("sig_ready"), sem("q_ready"), sem("g_sig")
        diff_ready, exp_ready, z_ready = sem("diff_ready"), sem("exp_ready"), sem("z_ready")
        scores_in, scores_clear, o_row, o_ready = sem("scores_in"), sem("scores_clear"), sem("o_row"), sem("o_ready")
        cen_ready, csq_ready, cn_ready, csig_ready, conv_ready = (sem("cen_ready"), sem("csq_ready"), sem("cn_ready"),
                                                                  sem("csig_ready"), sem("conv_ready"))
        wf_hi_ready, wf_ready, za_ready, zl_ready, ls_ready = (sem("wf_hi_ready"), sem("wf_ready"), sem("za_ready"),
                                                               sem("zl_ready"), sem("ls_ready"))
        max_ready, prob_exp, prob_ready, pT_act, pT_dve = (sem("max_ready"), sem("prob_exp"), sem("prob_ready"),
                                                           sem("pT_act"), sem("pT_dve"))
        qk_ready = sem("qk_ready")
        g_silu, z_sum, Fc_ready, fb_ready, scores_read = (sem("g_silu"), sem("z_sum"), sem("Fc_ready"), sem("fb_ready"),
                                                          sem("scores_read"))
        stored = sem("stored")

        block = ctx.enter_context(nc.Block())

        def tile_done(eng, layer, i):
            part_a, part_b = min(max(i - 12, 0), NT), max(i - 12 - NT, 0)
            end = CPT * min(i, 12) + OUT_A * part_a + OUT_B * part_b
            end += CPT if i < 12 else OUT_A if i < 12 + NT else OUT_B
            eng.wait_ge(chunk_used, SLOT0[layer] + end)

        def raw_wait(eng, s):
            eng.wait_ge(raw_full[s % RING], 16 * (s // RING + 1))

        @block.sync
        def _(sp):
            for r in range(RT):
                sp.dma_start(X[:, r, :], x[0, r * P:(r + 1) * P, :]).then_inc(x_loaded, 16)

            def load(s, wmat, k0, c0):
                if s >= RING:
                    sp.wait_ge(lo_ready, s - RING + 1)
                sp.dma_start(raw[:, s % RING], wmat[k0 * P:(k0 + CK) * P, c0:c0 + N].rearrange("(k p) n -> p k n", p=P)
                             ).then_inc(raw_full[s % RING], 16)

            for layer in range(DEPTH):
                s = SLOT0[layer]
                for c0 in (EVEN_TILES, ODD_TILES)[layer]:
                    for c in range(CPT):
                        load(s, w_in[layer], CK * c, c0)
                        s += 1
                for part in (EVEN_OUT, ODD_OUT)[layer]:
                    for j in range(NT):
                        for k in part[::CK]:
                            load(s, w_out[layer], k, j * N)
                            s += 1
                base = SLOT_MLP[layer]
                assert s == base and base % RING == 0
                w1, w2 = mlp_w1[layer], mlp_w2[layer]
                with sp.Fori(0, FB) as b:
                    with sp.Fori(0, NT) as j:
                        for c in range(CPT):
                            sp.wait_ge(lo_ready, b * (2 * NT * CPT) + j * CPT + (base + c - RING + 1))
                            sp.dma_start(raw[:, c % RING],
                                         w1[CK * c * P:CK * (c + 1) * P, bass.ds(b * D + j * N, N)].rearrange(
                                             "(k p) n -> p k n", p=P)).then_inc(raw_full[c % RING], 16)
                    with sp.Fori(0, NT) as j:
                        for c in range(CPT):
                            sp.wait_ge(lo_ready, b * (2 * NT * CPT) + j * CPT + (base + NT * CPT + c - RING + 1))
                            sp.dma_start(raw[:, c % RING],
                                         w2[bass.ds(b * D + CK * c * P, CK * P), bass.ds(j * N, N)].rearrange(
                                             "(k p) n -> p k n", p=P)).then_inc(raw_full[c % RING], 16)
            for g in range(NT):
                sp.wait_ge(normed, 3 * NT + g + 1)
                for r in range(RT):
                    sp.dma_start(out[0, r * P:(r + 1) * P, g * N:(g + 1) * N], X[:, r, g * N:(g + 1) * N]
                                 ).then_inc(stored, 16)
            sp.wait_ge(stored, 16 * NT * RT)

        @block.gpsimd
        def _(pool):
            n = [0]

            def link(ins):
                n[0] += 1
                ins.then_inc(pool_link, 1)
                pool.wait_ge(pool_link, n[0])

            def row(dst, src, width, s):
                pool.dma_start(dst, src.rearrange("(o n) -> o n", o=1).broadcast_to([P, width])).then_inc(s, 16)

            def ln_params(which):
                g, b = [(ln_mix_g[0], ln_mix_b[0]), (ln_mlp_g[0], ln_mlp_b[0]),
                        (ln_mix_g[1], ln_mix_b[1]), (ln_mlp_g[1], ln_mlp_b[1])][which]
                row(lnp[:, 0, :], g, D, lnp_loaded)
                row(lnp[:, 1, :], b, D, lnp_loaded)

            def inverse_root(which):
                pool.wait_ge(var_ready, which + 1)
                pool.tensor_tensor(rstd[:, :, 0], mv[:, :, 1], mhalf[:, 0:RT], ALU.pow).then_inc(rstd_ready, 1)

            link(pool.memset(ident[:, :], 0.0))
            pool.affine_select(out=ident[:, :], in_=ident[:, :], compare_op=ALU.not_equal, fill=1.0, base=0,
                               pattern=[[-1, P]], channel_multiplier=1).then_inc(consts, 1)
            link(pool.memset(imask[:, :], 0))
            link(pool.affine_select(out=imask[:, :], in_=imask[:, :], compare_op=ALU.not_equal, fill=1.0, base=0,
                                    pattern=[[-1, P]], channel_multiplier=1))
            link(pool.memset(masks[:, :, :], 1))
            for lv in range(LEVELS):
                h = CHUNK >> lv
                m = masks[:, lv, :].rearrange("p (g r) -> p g r", r=h)
                link(pool.affine_select(out=m, in_=m, compare_op=ALU.is_ge, fill=0.0, base=0,
                                        pattern=[[-2 * h, CHUNK // h], [0, h]], channel_multiplier=1))
                link(pool.affine_select(out=m, in_=m, compare_op=ALU.is_ge, fill=0.0, base=h - 1,
                                        pattern=[[2 * h, CHUNK // h], [0, h]], channel_multiplier=-1))
            link(pool.memset(rstm[:, :], 1.0))
            link(pool.memset(rstm[:, :].rearrange("p (g t) -> p g t", t=P)[:, :, 0:1], 0.0))
            pool.memset(mhalf[:, :], -0.5)
            pool.memset(meanw, 1.0 / CONV_CH)
            for hp in hpad:
                pool.memset(hp[:, :, 0:CONV_W - 1], 0.0)
            link(pool.memset(A, 0.0))
            pool.dma_start(cw_rows[0:CONV_W, :], ev_conv_w[0]).then_inc(const_loaded, 16)
            for i, v in enumerate((ev_conv_b, ev_conv_ln_g, ev_conv_ln_b)):
                pool.dma_start(small_rows[8 * i:8 * i + 8, :], v[0].rearrange("(c p) -> c p", p=P)
                               ).then_inc(const_loaded, 16)
            pool.dma_start(small_rows[24:40, :], hgrn_lb_logits.rearrange("w (h k) -> (w h) k", k=DH)
                           ).then_inc(const_loaded, 16)
            row(gn, ev_gnorm_g[0], KDIM, const_loaded)
            pool.nop().then_inc(consts, 1)
            for half in range(2):
                if half == 1:
                    pool.wait_ge(pair_full[1], P1_HG[0] + 10)
                    pool.memset(A, 0.0).then_inc(scores_clear, 1)
                    pool.wait_ge(var_ready, 2)
                    pool.tensor_tensor(crs, crs, mhalf[:, 0:S], ALU.pow).then_inc(rstd_ready, 1)
                pool.wait_ge(var_ready, 1 if half == 0 else 3)
                pool.tensor_tensor(ss, ss, mhalf[:, 0:8], ALU.pow).then_inc(rstd_ready, 1)
            pool.wait_ge(pair_full[0], P0["O1"] + 1)
            pool.wait_ge(cat_ready, 2)
            ln_params(0)
            pool.wait_ge(cat_ready, 3)
            pool.dma_start(wf, od_w_in[0, :, FOX_F:FOX_F + HEADS].rearrange("(k p) h -> p k h", p=P)
                           ).then_inc(odd_loaded, 16)
            row(bf, fox_b_f[0], HEADS, odd_loaded)
            for lo in range(2):
                j0 = CHUNK if lo == 0 else 0
                base = rel_bias[0, 0:1, lo * CHUNK - CHUNK + j0:lo * CHUNK - CHUNK + j0 + 1]
                pool.dma_start(rel[lo * CHUNK:(lo + 1) * CHUNK, :, j0:S],
                               bass.AP(base.tensor, base.offset, [[1, CHUNK], [REL_TABLE, HEADS], [1, S - j0]])
                               ).then_inc(odd_loaded, 16)
            pool.memset(rel[0:CHUNK, :, 0:CHUNK], NEG)
            link(pool.memset(U2, 1.0))
            link(pool.memset(tri, 0.0))
            pool.affine_select(out=U2[:, 0:P], in_=U2[:, 0:P], compare_op=ALU.is_ge, fill=0.0, base=0,
                               pattern=[[1, P]], channel_multiplier=-1).then_inc(odd_consts, 1)
            pool.affine_select(out=tri[:, P:S], in_=tri[:, P:S], compare_op=ALU.is_ge, fill=NEG, base=0,
                               pattern=[[-1, P]], channel_multiplier=1).then_inc(odd_consts, 1)
            inverse_root(3)
            for which in range(1, 4):
                pool.wait_ge(normed, NT * which)
                ln_params(which)
                inverse_root(3 + which)

        @block.scalar
        def _(act):
            at = [0]
            n = [0]

            def link(ins):
                n[0] += 1
                ins.then_inc(act_link, 1)
                act.wait_ge(act_link, n[0])

            def split(s):
                raw_wait(act, s)
                if s >= RING:
                    act.wait_ge(chunk_used, s - RING + 1)
                act.activation(w_hi[:, s % RING], raw[:, s % RING], ACT.Copy).then_inc(hi_ready, 1)

            def upto(s):
                while at[0] <= s:
                    split(at[0])
                    at[0] += 1

            def evac(layer, i, dst, func, done):
                tile_done(act, layer, i)
                act.activation(dst, gemm[(TILE0[layer] + i) % 2][:, :, :], func).then_inc(done, 1)

            def hi_of(p, use, dst, done):
                act.wait_ge(pair_full[p], use + 1)
                act.activation(dst, quad[p], ACT.Copy).then_inc(done, 1)

            def layer_norm(which):
                for g in range(NT):
                    hi_of(g % 2, (LN0, LN1)[g % 2][which][g // 2], x_hi[:, 4 * g:4 * g + 4, :], xt_hi)

            def scale_residual(which):
                for r in range(RT):
                    ins = act.activation(X[:, r, :], X[:, r, :], ACT.Copy, scale=ALPHA)
                ins.then_inc(x_scaled, 1)

            upto(RING - 1)
            layer_norm(0)
            scale_residual(0)
            act.wait_ge(lb_exp, 1)
            act.activation(lbl, lbl, ACT.Exp).then_inc(lb_exp, 1)

            def forget(half, s0, i):
                upto(s0 + 11)
                if half == 1:
                    act.wait_ge(h_ready_row, 2)
                evac(0, i, urow[0], ACT.Copy, row_ready)
                upto(s0 + 13)
                if half == 1:
                    act.wait_ge(z_ready, 8)
                act.wait_ge(pair_full[0], P0[f"F{half}"] + 1)
                act.activation(Dm, pair[0][:, :], ACT.Sigmoid).then_inc(sig_ready, 1)
                upto(s0 + 16)
                act.wait_ge(f_ready, half + 1)
                act.activation(Dm, L, ACT.Ln).then_inc(lnf_ready, 1)

            def query(half, s0, i):
                upto(s0 + 11)
                if half == 1:
                    act.wait_ge(pair_full[0], P0["C1"] + 1)
                evac(0, i, urow[1], ACT.Copy, row_ready)
                upto(s0 + 13)
                act.wait_ge(L_ready, half + 1)
                act.wait_ge(pair_full[0], P0[f"Q{half}"] + 1)
                act.activation(Dm, pair[0][:, :], ACT.Sigmoid).then_inc(sig_ready, 1)

            def exps(half, k):
                act.wait_ge(diff_ready, 8 * half + k + 1)
                if k < LEVELS:
                    h = CHUNK >> k
                    v = Dm.rearrange("p (g u r) -> p g u r", u=2, r=h)
                    act.activation(v[:, :, 0, :], v[:, :, 0, :], ACT.Exp, scale=-1.0)
                    act.activation(v[:, :, 1, :], v[:, :, 1, :], ACT.Exp).then_inc(exp_ready, 1)
                else:
                    v = Dm.rearrange("p (h b t) -> p h b t", b=2, t=P)
                    act.activation(v, v, ACT.Exp).then_inc(exp_ready, 1)

            def out_rows(half):
                act.wait_ge(pair_full[1], P1_HG[half] + 10)
                if half == 1:
                    act.wait_ge(pair_full[0], P0["O0"] + 1)
                act.activation(orow, pair[1][:, :], ACT.Copy).then_inc(o_row, 1)

            def group_hi(use, k0):
                hi_of(0, use, c_hi[:, k0:k0 + 4, :], cat_hi)

            forget(0, 0, 0)
            query(0, 8, 1)
            upto(23)
            exps(0, 0)
            upto(25)
            exps(0, 1)
            upto(27)
            act.wait_ge(pair_full[0], P0["F0"] + 1)
            evac(0, 2, urow[0], ACT.Sigmoid, gate_ready)
            exps(0, 2)
            for k in range(3, 8):
                upto(23 + 2 * k)
                exps(0, k)
            upto(38)
            act.wait_ge(pair_full[0], P0["C0"] + 1)
            act.activation(hpad[0][:, :, CONV_W - 1:], quad[0], ACT.Copy).then_inc(pad_ready, 1)
            upto(43)
            act.wait_ge(h_ready_row, 1)
            evac(0, 4, urow[0], ACT.Sigmoid, gate_ready)
            upto(54)
            act.wait_ge(pair_full[0], P0["C1"] + 1)
            act.activation(hpad[1][:, :, CONV_W - 1:], quad[0], ACT.Copy).then_inc(pad_ready, 1)
            upto(59)
            evac(0, 6, vrow, ACT.Copy, row_ready)
            upto(64)
            out_rows(0)
            upto(67)
            evac(0, 7, G.rearrange("p (r n) -> p r n", r=RT), ACT.Sigmoid, g_sig)
            upto(71)
            group_hi(P0["O0"], 8)
            forget(1, 64, 8)
            query(1, 72, 9)
            upto(89)
            exps(1, 0)
            upto(91)
            exps(1, 1)
            act.wait_ge(pair_full[1], P1_HG[0] + 10)
            evac(0, 10, vrow, ACT.Copy, row_ready)
            upto(93)
            exps(1, 2)
            upto(94)
            act.wait_ge(cen_ready, 1)
            act.activation(csq, cv, ACT.Square).then_inc(csq_ready, 1)
            upto(95)
            exps(1, 3)
            upto(97)
            exps(1, 4)
            upto(99)
            exps(1, 5)
            act.wait_ge(o_ready, 1)
            evac(0, 11, G.rearrange("p (r n) -> p r n", r=RT), ACT.Sigmoid, g_sig)
            act.wait_ge(cn_ready, 1)
            act.wait_ge(pair_full[0], P0["VAR"] + 1)
            for c in range(8):
                ins = act.activation(csq[:, c, :], cv[:, c, :], ACT.Sigmoid, scale=cpar[:, 1, c:c + 1],
                                     bias=cpar[:, 2, c:c + 1])
            ins.then_inc(csig_ready, 1)
            upto(101)
            exps(1, 6)
            act.wait_ge(conv_ready, 1)
            act.activation(c_hi[:, 0:8, :], cv, ACT.Copy).then_inc(cat_hi, 1)
            upto(103)
            exps(1, 7)
            upto(112)
            out_rows(1)
            upto(118)
            group_hi(P0["O1"], 12)
            upto(SLOT_MLP[0] + RING - 1)

            def mlp_tile(base, tbase, p0base, layer, b, i, last=False):
                first = base + i * CPT + RING
                for c in range(CPT):
                    s = first + c
                    if last and b * (2 * NT * CPT) + s >= SLOTS:
                        break
                    act.wait_ge(raw_full[s % RING], b * (16 * 2 * NT * CPT // RING) + 16 * (s // RING + 1))
                    act.wait_ge(chunk_used, b * (2 * NT * CPT) + (s - RING + 1))
                    act.activation(w_hi[:, s % RING], raw[:, s % RING], ACT.Copy).then_inc(hi_ready, 1)
                    if c == 1 and 1 <= i <= NT:
                        act.wait_ge(pair_full[0], b * NT + (p0base + i))
                        act.activation(c_hi[:, 4 * (i - 1):4 * i, :], quad[0], ACT.Copy).then_inc(h_hi, 1)
                if i < NT:
                    t = tbase + i
                    act.wait_ge(chunk_used, b * (2 * NT * CPT) + (base + (i + 1) * CPT))
                    act.activation(urow[i % 2], gemm[t % 2][:, :, :], ACT.Relu).then_inc(relu_done, 1)
                    act.wait_ge(relu_done, b * NT + (layer * FB * NT + i + 1))
                    act.activation(urow[i % 2], urow[i % 2], ACT.Square).then_inc(h_row, 1)

            def mlp(layer):
                base, tbase, p0base = SLOT_MLP[layer], TILE_MLP[layer], P0_MLP[layer]
                whole = FB if layer == 0 else FB - 1
                with act.Fori(0, whole) as b:
                    for i in range(2 * NT):
                        mlp_tile(base, tbase, p0base, layer, b, i)
                if layer == 1:
                    for i in range(2 * NT):
                        mlp_tile(base, tbase, p0base, layer, whole, i, last=True)
                at[0] = base + MLP_SLOTS + RING

            layer_norm(1)
            scale_residual(1)
            mlp(0)

            layer_norm(2)
            scale_residual(2)
            o = SLOT0[1]
            act.wait_ge(odd_loaded, 16 * 4)
            act.activation(wf_hi[:, :, :], wf, ACT.Copy).then_inc(wf_hi_ready, 1)
            for g in range(4):
                s0, use = o + 24 * g, P0_ATT + 5 * g
                upto(s0 + 6 if g else s0 + 3)
                if g:
                    act.wait_ge(pair_full[0], P0_ATT + 5 * (g - 1) + 5)
                    act.activation(c_hi[:, 4 * (g - 1):4 * g, :], quad[0], ACT.Copy).then_inc(cat_hi, 1)
                upto(s0 + 11)
                evac(1, 3 * g, urow[0], ACT.Copy, row_ready)
                if g == 0:
                    upto(s0 + 12)
                    act.wait_ge(za_ready, 1)
                    link(act.activation(za, za, ACT.Exp, scale=-1.0))
                    act.activation(za, za, ACT.Ln, bias=1.0).then_inc(zl_ready, 1)
                upto(s0 + 13)
                act.wait_ge(pair_full[0], use + 1)
                act.activation(qT, quad[0], ACT.Copy).then_inc(qk_ready, 1)
                upto(s0 + 19)
                evac(1, 3 * g + 1, urow[1], ACT.Copy, row_ready)
                upto(s0 + 21)
                act.wait_ge(pair_full[0], use + 2)
                act.activation(kT, quad[0], ACT.Copy).then_inc(qk_ready, 1)
                upto(s0 + 25)
                act.wait_ge(max_ready, g + 1)
                for q in range(RT):
                    width = (q + 1) * P
                    v = sm[:, q * HG * P:q * HG * P + HG * width].rearrange("p (h k) -> p h k", h=HG)
                    for h in range(HG):
                        i = q * HG + h
                        ins = act.activation(v[:, h, :], v[:, h, :], ACT.Exp, bias=mx[:, i:i + 1],
                                             accum_out=sums[:, i:i + 1])
                ins.then_inc(prob_exp, 1)
                upto(s0 + 27)
                evac(1, 3 * g + 2, vrow, ACT.Copy, row_ready)
                upto(s0 + 28)
                act.wait_ge(pair_full[0], use + 4)
                act.activation(pT[:, 0:HG * S], pair[0][:, :], ACT.Copy).then_inc(pT_act, 1)
            upto(o + 72 + 30)
            act.wait_ge(pair_full[0], P0_ATT + 20)
            act.activation(c_hi[:, 12:16, :], quad[0], ACT.Copy).then_inc(cat_hi, 1)
            upto(SLOT_MLP[1] + RING - 1)
            layer_norm(3)
            scale_residual(3)
            mlp(1)

        @block.vector
        def _(dve):
            at = [0]
            n = [0]

            def mark(ins):
                n[0] += 1
                ins.then_inc(dve_link, 1)
                return n[0]

            def link(ins):
                dve.wait_ge(dve_link, mark(ins))

            def split(s):
                dve.wait_ge(hi_ready, s + 1)
                raw_wait(dve, s)
                if s >= RING:
                    dve.wait_ge(chunk_used, s - RING + 1)
                dve.tensor_tensor(w_lo[:, s % RING], raw[:, s % RING], w_hi[:, s % RING].bitcast(F32), ALU.subtract
                                  ).then_inc(lo_ready, 1)

            def upto(s):
                while at[0] <= s:
                    split(at[0])
                    at[0] += 1

            def lo_of(p, hi, lo, hi_sem, value, ready):
                dve.wait_ge(hi_sem, value)
                dve.tensor_tensor(lo, quad[p], hi.bitcast(F32), ALU.subtract).then_inc(ready, 1)

            def add_tile(layer, i, j):
                tile_done(dve, layer, i)
                Xj = X[:, :, j * N:(j + 1) * N]
                dve.tensor_tensor(Xj, gemm[(TILE0[layer] + i) % 2][:, :, :], Xj, ALU.add).then_inc(x_sum, 1)

            def tile_stats(j):
                for r in range(RT):
                    dve.bn_stats(stats[:, r, j, :], X[:, r, j * N:(j + 1) * N]).then_inc(dve_link, 1)
                n[0] += RT

            def x_transposed(which, g):
                lo_of(g % 2, x_hi[:, 4 * g:4 * g + 4, :], x_lo[:, 4 * g:4 * g + 4, :], xt_hi, NT * which + g + 1, xt_ready)

            def layer_norm(which):
                dve.wait_ge(dve_link, n[0])
                for r in range(RT):
                    link(dve.bn_aggr(mv[:, r, :], stats[:, r, :, :]))
                dve.tensor_scalar(mv[:, :, 1], mv[:, :, 1], EPS, None, ALU.add).then_inc(var_ready, 1)
                dve.wait_ge(lnp_loaded, 32 * which)
                dve.wait_ge(rstd_ready, 3 + which)

                def norm(g):
                    cols = slice(g * N, (g + 1) * N)
                    for r in range(RT):
                        k = mark(dve.tensor_scalar(X[:, r, cols], X[:, r, cols], mv[:, r, 0:1], rstd[:, r, :],
                                                   ALU.subtract, ALU.mult))
                    dve.wait_ge(dve_link, k)
                    gb = lnp[:, 0, cols].unsqueeze(1).broadcast_to([P, RT, N])
                    bb = lnp[:, 1, cols].unsqueeze(1).broadcast_to([P, RT, N])
                    link(dve.tensor_tensor(X[:, :, cols], X[:, :, cols], gb, ALU.mult))
                    dve.tensor_tensor(X[:, :, cols], X[:, :, cols], bb, ALU.add).then_inc(normed, 1)

                if which == 4:
                    for g in range(NT):
                        norm(g)
                    return
                norm(0)
                norm(1)
                x_transposed(which, 0)
                norm(2)
                x_transposed(which, 1)
                norm(3)
                x_transposed(which, 2)
                x_transposed(which, 3)

            upto(RING - 1)
            dve.wait_ge(pair_full[1], P1_CONST + 1)
            dve.tensor_copy(cw, pair[1][:, 0:8 * 32].rearrange("p (c j) -> p c j", c=8)[:, :, 0:CONV_W]
                            ).then_inc(dve_link, 1)
            n[0] += 1
            dve.tensor_copy(small, pair[1][:, 8 * 32:8 * 32 + 40]).then_inc(params_ready, 1)
            dve.wait_ge(params_ready, 1)
            for g in range(NT):
                x_transposed(0, g)
            dve.wait_ge(consts, 2)
            link(dve.tensor_tensor(lb, lbl[:, 0, :], lbl[:, 1, :], ALU.max))
            k = mark(dve.tensor_tensor(lbl[:, 0, :], lbl[:, 0, :], lb, ALU.subtract))
            dve.tensor_tensor(lbl[:, 1, :], lbl[:, 1, :], lb, ALU.subtract).then_inc(lb_exp, 1)
            dve.wait_ge(lb_exp, 2)
            link(dve.tensor_tensor(lb, lbl[:, 0, :], lbl[:, 1, :], ALU.add))
            link(dve.reciprocal(oml, lb))
            link(dve.tensor_tensor(lb, lbl[:, 0, :], oml, ALU.mult))
            link(dve.tensor_scalar(oml, lb, -1.0, 1.0, ALU.mult, ALU.add))

            def forget(half, s0):
                upto(s0 + 14)
                dve.wait_ge(sig_ready, 2 * half + 1)
                if half == 1:
                    dve.wait_ge(pair_full[1], P1_HG[0] + 9)
                for h in range(HG):
                    c = HG * half + h
                    k = mark(dve.tensor_scalar(L[:, h * S:(h + 1) * S], Dm[:, h * S:(h + 1) * S],
                                               oml[:, c:c + 1], lb[:, c:c + 1], ALU.mult, ALU.add))
                dve.wait_ge(dve_link, k)
                link(dve.tensor_scalar(kT.rearrange("p h t -> p (h t)"), L, -1.0, 1.0, ALU.mult, ALU.add))
                dve.tensor_scalar(L, L, F_MIN, None, ALU.max).then_inc(f_ready, 1)
                upto(s0 + 17)
                dve.wait_ge(lnf_ready, half + 1)
                dve.tensor_tensor_scan(L, rstm[:, :], Dm, 0.0, ALU.mult, ALU.add).then_inc(L_ready, 1)

            def query(half, s0):
                upto(s0 + 13)
                dve.wait_ge(sig_ready, 2 * half + 2)
                dve.tensor_tensor(qT.rearrange("p h t -> p (h t)"), pair[0][:, :], Dm, ALU.mult
                                  ).then_inc(q_ready, 1)

            def diff(half, k):
                if k == 0:
                    dve.wait_ge(q_ready, half + 1)
                    dve.wait_ge(L_ready, half + 1)
                else:
                    dve.wait_ge(z_ready, 8 * half + k)
                if k < LEVELS:
                    h = CHUNK >> k
                    Lv = L.rearrange("p (g t) -> p g t", t=2 * h)
                    mid = Lv[:, :, h - 1:h].broadcast_to([P, HG * S // (2 * h), 2 * h])
                    dve.tensor_tensor(Dm.rearrange("p (g t) -> p g t", t=2 * h), Lv, mid, ALU.subtract
                                      ).then_inc(diff_ready, 1)
                else:
                    Lv = L.rearrange("p (h b t) -> p h b t", b=2, t=P)
                    Dv = Dm.rearrange("p (h b t) -> p h b t", b=2, t=P)
                    end = Lv[:, :, 0, P - 1:P].broadcast_to([P, HG, P])
                    k = mark(dve.tensor_tensor(Dv[:, :, 0, :], end, Lv[:, :, 0, :], ALU.subtract))
                    dve.tensor_copy(Dv[:, :, 1, :], Lv[:, :, 1, :]).then_inc(diff_ready, 1)

            def weigh(half, k):
                dve.wait_ge(exp_ready, 8 * half + k + 1)
                use = P1_HG[half] + k
                if 8 * half + k >= 2:
                    dve.wait_ge(pair_full[1], use - 1 if k >= 2 else P1_HG[0] + 7 + k)
                h = CHUNK >> k if k < LEVELS else P
                z = Z[k % 2].rearrange("p (g u r) -> p g u r", u=2, r=h)
                e = Dm.rearrange("p (g u r) -> p g u r", u=2, r=h)
                kv = kT.rearrange("p h t -> p (h t)").rearrange("p (g u r) -> p g u r", u=2, r=h)
                qv = qT.rearrange("p h t -> p (h t)").rearrange("p (g u r) -> p g u r", u=2, r=h)
                dve.tensor_tensor(z[:, :, 0, :], e[:, :, 0, :], kv[:, :, 0, :], ALU.mult)
                dve.tensor_tensor(z[:, :, 1, :], e[:, :, 1, :], qv[:, :, 1, :], ALU.mult).then_inc(z_ready, 1)

            def take(half, k):
                use = P1_HG[half] + k
                dve.wait_ge(pair_full[1], use + 1)
                if k == 0:
                    dve.wait_ge(scores_clear, half)
                Av = A.rearrange("p (b t) -> p b t", t=P)
                if k < LEVELS:
                    h = CHUNK >> k
                    o_ = A.rearrange("p (b g u r) -> p b g u r", b=2 * HG, u=2, r=h)[:, :, :, 1, :]
                    m_ = masks[:, k, :].rearrange("p (g r) -> p g r", r=h).unsqueeze(1).broadcast_to(
                        [P, 2 * HG, CHUNK // h, h])
                    d_ = pair[1][:, 0:N].rearrange("p (b g r) -> p b g r", b=2 * HG, r=h)
                    ins = dve.copy_predicated(o_, m_, d_)
                elif k == LEVELS:
                    ins = dve.tensor_copy(Ax, pair[1][:, 0:N])
                else:
                    ins = dve.copy_predicated(Av, imask[:, :].unsqueeze(1).broadcast_to([P, 2 * HG, P]),
                                              pair[1][:, :].rearrange("p (b t) -> p b t", t=P))
                ins.then_inc(scores_in, 1)

            def gates(half, i):
                dve.wait_ge(g_sig, half + 1)
                gv = G.rearrange("p (r n) -> p r n", r=RT)
                dve.tensor_tensor(gv, gv, gemm[(TILE0[0] + i) % 2][:, :, :], ALU.mult).then_inc(g_silu, 1)
                dve.wait_ge(g_silu, half + 1)
                link(dve.tensor_tensor(gv, gv, gn[:, half * N:(half + 1) * N].unsqueeze(1).broadcast_to([P, RT, N]),
                                       ALU.mult))

            def mean_square(half):
                dve.wait_ge(o_row, half + 1)
                sq = Dm
                link(dve.tensor_tensor(sq, orow, orow, ALU.mult))
                link(dve.tensor_reduce(ss, sq.rearrange("p (b v) -> p b v", v=DH), AX.X, ALU.add))
                dve.tensor_scalar(ss, ss, 1.0 / DH, EPS, ALU.mult, ALU.add).then_inc(var_ready, 1)

            def norm_out(half):
                dve.wait_ge(rstd_ready, 1 if half == 0 else 3)
                ov = orow.rearrange("p (b v) -> p b v", v=DH)
                link(dve.tensor_tensor(ov, ov, ss.unsqueeze(2).broadcast_to([P, 2 * HG, DH]), ALU.mult))
                dve.tensor_tensor(orow, orow, G, ALU.mult).then_inc(o_ready, 1)

            def group_lo(k0, value):
                lo_of(0, c_hi[:, k0:k0 + 4, :], c_lo[:, k0:k0 + 4, :], cat_hi, value, cat_ready)

            tap_mark = {}
            taps = [0]

            def conv(count):
                for _ in range(count):
                    if taps[0] == 8 * CONV_W:
                        return
                    half, rest = divmod(taps[0], 4 * CONV_W)
                    j, c = divmod(rest, 4)
                    if rest == 0:
                        dve.wait_ge(pad_ready, half + 1)
                    ch = 4 * half + c
                    src = hpad[half][:, c, j:j + S]
                    if j == 0:
                        ins = dve.tensor_scalar(cv[:, ch, :], src, cw[:, ch, 0:1], cpar[:, 0, ch:ch + 1], ALU.mult, ALU.add)
                    else:
                        dve.wait_ge(dve_link, tap_mark[ch])
                        ins = dve.scalar_tensor_tensor(out=cv[:, ch, :], in0=src, scalar=cw[:, ch, j:j + 1],
                                                       in1=cv[:, ch, :], op0=ALU.mult, op1=ALU.add)
                    tap_mark[ch] = mark(ins)
                    taps[0] += 1
                    if taps[0] == 8 * CONV_W:
                        dve.wait_ge(dve_link, n[0])
                        dve.nop().then_inc(taps_done, 1)

            def gated(i, half):
                dve.wait_ge(gate_ready, half + 1)
                tile_done(dve, 0, i)
                dve.wait_ge(pair_full[0], P0["Q0" if half == 0 else "C0"] + 1)
                dve.tensor_tensor(urow[1], gemm[(TILE0[0] + i) % 2][:, :, :], urow[0], ALU.mult
                                  ).then_inc(h_ready_row, 1)

            forget(0, 0)
            query(0, 8)
            conv_from, conv_each = 40, 5
            for s in range(22, SLOT_MLP[0]):
                upto(s)
                k0, k1 = s - 22, s - 88
                for half, k in ((0, k0), (1, k1)):
                    if k >= 0 and k % 2 == 0 and k // 2 <= 10:
                        k //= 2
                        if 1 <= k <= 8:
                            weigh(half, k - 1)
                        if k <= 7:
                            diff(half, k)
                        if 2 <= k:
                            take(half, k - 2)
                if s == 35:
                    gated(3, 0)
                if s == 51:
                    gated(5, 1)
                if s == 64:
                    mean_square(0)
                if s == 67:
                    gates(0, 7)
                if s == 68:
                    norm_out(0)
                if s == 71:
                    group_lo(8, 1)
                if s == 78:
                    forget(1, 64)
                if s == 81:
                    pass
                if s == 85:
                    query(1, 72)
                if s == 93:
                    conv(8 * CONV_W)
                    dve.wait_ge(pair_full[0], P0["MEAN"] + 1)
                    dve.tensor_tensor(cv, cv, pair[0][:, 0:S].unsqueeze(1).broadcast_to([P, 8, S]), ALU.subtract
                                      ).then_inc(cen_ready, 1)
                if s == 97:
                    dve.wait_ge(pair_full[0], P0["VAR"] + 1)
                    dve.tensor_scalar(crs, pair[0][:, 0:S], EPS, None, ALU.add
                                      ).then_inc(var_ready, 1)
                if s == 98:
                    dve.wait_ge(rstd_ready, 2)
                    dve.tensor_tensor(cv, cv, crs.unsqueeze(1).broadcast_to([P, 8, S]), ALU.mult).then_inc(cn_ready, 1)
                if s == 99:
                    gates(1, 11)
                if s == 100:
                    dve.wait_ge(csig_ready, 1)
                    for c in range(8):
                        k = mark(dve.tensor_scalar(cv[:, c, :], cv[:, c, :], cpar[:, 1, c:c + 1], cpar[:, 2, c:c + 1],
                                                   ALU.mult, ALU.add))
                    dve.wait_ge(dve_link, k)
                    dve.tensor_tensor(cv, cv, csq, ALU.mult).then_inc(conv_ready, 1)
                if s == 101:
                    dve.wait_ge(cat_hi, 2)
                    dve.tensor_tensor(c_lo[:, 0:8, :], cv, c_hi[:, 0:8, :].bitcast(F32), ALU.subtract
                                      ).then_inc(cat_ready, 1)
                if s == 112:
                    mean_square(1)
                if s == 114:
                    norm_out(1)
                if s == 118:
                    group_lo(12, 3)
                if s >= conv_from and s < 93:
                    conv(conv_each)
                for j in range(NT):
                    if s == 96 + OUT_A * j + OUT_A - 1 + RING:
                        if j == 0:
                            dve.wait_ge(x_scaled, 1)
                        add_tile(0, 12 + j, j)

            def second_part(layer):
                o = SLOT0[layer] + IN_SLOTS + NT * OUT_A
                for j in range(NT):
                    upto(o + OUT_B * j + OUT_B - 1 + RING)
                    add_tile(layer, 12 + NT + j, j)
                    dve.wait_ge(x_sum, x_sums[0] + NT + j + 1)
                    tile_stats(j)
                x_sums[0] += 2 * NT

            x_sums = [0]
            second_part(0)

            def mlp_tile(layer, b, i, last=False):
                base, tbase = SLOT_MLP[layer], TILE_MLP[layer]
                first = base + i * CPT + RING
                for c in range(CPT):
                    s = first + c
                    if last and b * (2 * NT * CPT) + s >= SLOTS:
                        break
                    dve.wait_ge(hi_ready, b * (2 * NT * CPT) + (s + 1))
                    dve.wait_ge(raw_full[s % RING], b * (16 * 2 * NT * CPT // RING) + 16 * (s // RING + 1))
                    dve.wait_ge(chunk_used, b * (2 * NT * CPT) + (s - RING + 1))
                    dve.tensor_tensor(w_lo[:, s % RING], raw[:, s % RING], w_hi[:, s % RING].bitcast(F32), ALU.subtract
                                      ).then_inc(lo_ready, 1)
                    if c == 1 and 1 <= i <= NT:
                        dve.wait_ge(h_hi, b * NT + (layer * NT * FB + i))
                        dve.tensor_tensor(c_lo[:, 4 * (i - 1):4 * i, :], quad[0],
                                          c_hi[:, 4 * (i - 1):4 * i, :].bitcast(F32), ALU.subtract
                                          ).then_inc(h_ready, 1)
                if i >= NT:
                    j, t = i - NT, tbase + i
                    if j == 0:
                        dve.wait_ge(x_scaled, 2 + 2 * layer)
                    dve.wait_ge(chunk_used, b * (2 * NT * CPT) + (base + (i + 1) * CPT))
                    Xj = X[:, :, j * N:(j + 1) * N]
                    dve.tensor_tensor(Xj, gemm[t % 2][:, :, :], Xj, ALU.add).then_inc(x_sum, 1)
                    dve.wait_ge(x_sum, b * NT + (x_sums[0] + j + 1))
                    for r in range(RT):
                        dve.bn_stats(stats[:, r, j, :], X[:, r, j * N:(j + 1) * N]).then_inc(dve_link, 1)

            def mlp(layer):
                whole = FB if layer == 0 else FB - 1
                with dve.Fori(0, whole) as b:
                    for i in range(2 * NT):
                        mlp_tile(layer, b, i)
                if layer == 1:
                    for i in range(2 * NT):
                        mlp_tile(layer, whole, i, last=True)
                n[0] += RT * NT * FB
                x_sums[0] += NT * FB
                at[0] = SLOT_MLP[layer] + MLP_SLOTS + RING

            layer_norm(1)
            mlp(0)
            layer_norm(2)

            o = SLOT0[1]
            dve.wait_ge(wf_hi_ready, 1)
            dve.tensor_tensor(wf_lo[:, :, :], wf, wf_hi[:, :, :].bitcast(F32), ALU.subtract).then_inc(wf_ready, 1)

            def spread(g):
                v = ls.rearrange("p (r h) -> p r h", r=RT)[:, :, HG * g:HG * (g + 1)]
                dve.tensor_copy(lsb, v.unsqueeze(3).broadcast_to([P, RT, HG, P])).then_inc(ls_ready, 1)

            def forget_bias(g):
                dve.wait_ge(pair_full[1], P1[f"FB{g}"] + 1)
                for q in range(RT):
                    width = (q + 1) * P
                    for h in range(HG):
                        o_ = fbias[:, q * HG * P + h * width:q * HG * P + (h + 1) * width]
                        ins = dve.scalar_tensor_tensor(out=o_, in0=tri[:, S - width:S],
                                                       scalar=Fc[:, q * HEADS + HG * g + h:q * HEADS + HG * g + h + 1],
                                                       in1=quad[1][:, h, 0:width], op0=ALU.add, op1=ALU.subtract)
                        ins.then_inc(fb_ready, 1)

            def softmax_in(g):
                dve.wait_ge(pair_full[0], P0_ATT + 5 * g + 3)
                dve.wait_ge(pair_full[1], P1[f"S{g}"] + 1)
                if g < 2:
                    dve.wait_ge(fb_ready, RT * HG * (g + 1))
                for q in range(RT):
                    width = (q + 1) * P
                    o_ = sm[:, q * HG * P:q * HG * P + HG * width].rearrange("p (h k) -> p h k", h=HG)
                    src = (pair[0][:, 0:N], pair[1][:, :])[q].rearrange("p (h k) -> p h k", h=HG)
                    if g < 2:
                        bias = fbias[:, q * HG * P:q * HG * P + HG * width].rearrange("p (h k) -> p h k", h=HG)
                    else:
                        last = P * q + 2 * CHUNK - 1
                        lo = last - width
                        heads = rel[:, HG * (g - 2):HG * (g - 1), :]
                        bias = heads[:, :, last::-1] if lo < 0 else heads[:, :, last:lo:-1]
                    dve.scalar_tensor_tensor(out=o_, in0=src, scalar=SCALE, in1=bias, op0=ALU.mult, op1=ALU.add
                                             ).then_inc(scores_read, 1)
                    dve.wait_ge(scores_read, 2 * g + q + 1)
                    link(dve.tensor_reduce(mx[:, q * HG:(q + 1) * HG], o_, AX.X, ALU.max))
                dve.tensor_scalar(mx, mx, -1.0, None, ALU.mult).then_inc(max_ready, 1)

            def softmax_out(g):
                dve.wait_ge(prob_exp, g + 1)
                link(dve.reciprocal(rs, sums))
                for q in range(RT):
                    width = (q + 1) * P
                    v = sm[:, q * HG * P:q * HG * P + HG * width].rearrange("p (h k) -> p h k", h=HG)
                    ins = dve.tensor_tensor(v, v, rs[:, q * HG:(q + 1) * HG].unsqueeze(2).broadcast_to([P, HG, width]),
                                            ALU.mult)
                ins.then_inc(prob_ready, 1)

            for g in range(4):
                s0 = o + 24 * g
                if g:
                    upto(s0 + 6)
                    lo_of(0, c_hi[:, 4 * (g - 1):4 * g, :], c_lo[:, 4 * (g - 1):4 * g, :], cat_hi, 3 + g, cat_ready)
                if g == 0:
                    upto(s0 + 12)
                    dve.wait_ge(pair_full[1], P1["FL"] + 1)
                    zv = zf.rearrange("p (r h) -> p r h", r=RT)
                    ins = dve.tensor_tensor(zv, pair[1][:, :].rearrange("p (r n) -> p r n", r=RT)[:, :, 0:HEADS],
                                            bf.unsqueeze(1).broadcast_to([P, RT, HEADS]), ALU.add)
                    ins.then_inc(z_sum, 1)
                    dve.wait_ge(z_sum, 1)
                    dve.scalar_tensor_tensor(out=za, in0=zf, scalar=-1.0, in1=zf, op0=ALU.mult, op1=ALU.max
                                             ).then_inc(za_ready, 1)
                    upto(s0 + 13)
                    dve.wait_ge(zl_ready, 1)
                    link(dve.scalar_tensor_tensor(out=ls, in0=zf, scalar=0.0, in1=za, op0=ALU.min, op1=ALU.subtract))
                    spread(0)
                    upto(s0 + 16)
                    dve.wait_ge(pair_full[1], P1["FC"] + 1)
                    ins = dve.tensor_copy(Fc.rearrange("p (r h) -> p r h", r=RT),
                                          pair[1][:, :].rearrange("p (r n) -> p r n", r=RT)[:, :, 0:HEADS])
                    ins.then_inc(Fc_ready, 1)
                    dve.wait_ge(Fc_ready, 1)
                    upto(s0 + 18)
                    forget_bias(0)
                if g == 1:
                    upto(s0 + 10)
                    dve.wait_ge(pair_full[1], P1["FB0"] + 1)
                    spread(1)
                    upto(s0 + 14)
                    forget_bias(1)
                upto(s0 + 24)
                softmax_in(g)
                upto(s0 + 26)
                softmax_out(g)
                upto(s0 + 28)
                dve.wait_ge(pair_full[1], P1[f"P{g}"] + 1)
                dve.tensor_copy(pT[:, HG * S:], pair[1][:, 0:N]).then_inc(pT_dve, 1)
            upto(o + 102)
            lo_of(0, c_hi[:, 12:16, :], c_lo[:, 12:16, :], cat_hi, 7, cat_ready)
            for j in range(NT):
                upto(o + 96 + OUT_A * j + OUT_A - 1 + RING)
                if j == 0:
                    dve.wait_ge(x_scaled, 3)
                add_tile(1, 12 + j, j)
            second_part(1)
            layer_norm(3)
            mlp(1)
            layer_norm(4)

        @block.tensor
        def _(pe):
            def products(acc, hi, lo, k, c, slot, first, last):
                for r in range(RT):
                    rows = slice(r * P, (r + 1) * P)
                    pe.matmul(acc[:, r, :], hi[:, k, rows], w_hi[:, slot, c, :], start=first, stop=False)
                    pe.matmul(acc[:, r, :], hi[:, k, rows], w_lo[:, slot, c, :], start=False, stop=False)
                    ins = pe.matmul(acc[:, r, :], lo[:, k, rows], w_hi[:, slot, c, :], start=False, stop=last)
                return ins

            def chunk(acc, act_, ks, s, first, last):
                pe.wait_ge(lo_ready, s + 1)
                for c, k in enumerate(ks):
                    ins = products(acc, act_[0], act_[1], k, c, s % RING, first and c == 0, last and c == CK - 1)
                ins.then_inc(chunk_used, 1)
                return ins

            tile_out = [[(row_ready, 1), (row_ready, 2), (gate_ready, 1), (h_ready_row, 1), (gate_ready, 2),
                         (h_ready_row, 2), (row_ready, 3), (g_silu, 1), (row_ready, 4), (row_ready, 5), (row_ready, 6),
                         (g_silu, 2)] + [(x_sum, j + 1) for j in range(2 * NT)],
                        [(row_ready, 7 + i) for i in range(12)] +
                        [(x_sum, 2 * NT + FB * NT + j + 1) for j in range(2 * NT)]]
            mlp_h = [[(h_ready, 16 * layer + i + 1) for i in range(FB * NT)] for layer in range(DEPTH)]
            x_g = [[(xt_ready, NT * which + g + 1) for g in range(NT)] for which in range(4)]
            pair_out = [
                x_g[0][0::2] + [(sig_ready, 1), (q_ready, 1), (pad_ready, 1), (pad_ready, 2), (cat_ready, 1),
                                (sig_ready, 3), (q_ready, 2), (cen_ready, 1), (var_ready, 2), (cat_ready, 3)]
                + x_g[1][0::2] + mlp_h[0] + x_g[2][0::2]
                + [u for g in range(4) for u in ((qk_ready, 2 * g + 1), (qk_ready, 2 * g + 2), (scores_read, 2 * g + 1),
                                                 (pT_act, g + 1), (cat_ready, 4 + g))]
                + x_g[3][0::2] + mlp_h[1],
                [(params_ready, 1)] + x_g[0][1::2]
                + [u for half in range(2) for u in [(scores_in, 9 * half + k + 1) for k in range(9)] + [(o_row, half + 1)]]
                + x_g[1][1::2] + x_g[2][1::2]
                + [(z_sum, 1), (Fc_ready, 1), (fb_ready, RT * HG), (scores_read, 2), (pT_dve, 1), (fb_ready, 2 * RT * HG)]
                + [u for g in range(1, 4) for u in ((scores_read, 2 * g + 2), (pT_dve, g + 1))]
                + x_g[3][1::2],
            ]

            def acquire(layer, i):
                if i >= 2:
                    pe.wait_ge(*tile_out[layer][i - 2])
                elif layer:
                    pe.wait_ge(x_sum, 2 * NT + NT * FB - 1 + i)
                return gemm[(TILE0[layer] + i) % 2]

            def pair_free(p, use):
                if use:
                    pe.wait_ge(*pair_out[p][use - 1])

            def transposes(p, use, src):
                pair_free(p, use)
                for c in range(4):
                    for r in range(RT):
                        ins = pe.transpose(quad[p][:, c, r * P:(r + 1) * P], src[:, r, c * P:(c + 1) * P], ident[:, :])
                ins.then_inc(pair_full[p], 1)

            def x_group(which, g):
                if which:
                    pe.wait_ge(normed, NT * (which - 1) + g + 1)
                transposes(g % 2, (LN0, LN1)[g % 2][which][g // 2], X[:, :, g * N:(g + 1) * N])

            X_ = (x_hi, x_lo)
            C_ = (c_hi, c_lo)
            at = [0, 0]

            def first_tile(which, base_wait=None):
                s, t = at
                acc = acquire(which // 2, 0)
                x_group(which, 0)
                x_group(which, 1)
                for c in range(CPT):
                    if c % 2 == 0:
                        pe.wait_ge(xt_ready, NT * which + c // 2 + 1)
                    ins = chunk(acc, X_, (CK * c, CK * c + 1), s + c, c == 0, c == CPT - 1)
                    if c in (1, 3):
                        x_group(which, 2 + c // 2)
                    yield c
                at[0], at[1] = s + CPT, t + 1

            def rows_to(p, use, src, count):
                pe.wait_ge(row_ready, count)
                transposes(p, use, src)

            def level(half, k):
                use = P1_HG[half] + k
                pair_free(1, use)
                if k < 8:
                    pe.wait_ge(z_ready, 8 * half + k + 1)
                if k < LEVELS:
                    h = CHUNK >> k
                    z = Z[k % 2].rearrange("p (b t) -> p b t", t=P)
                    for b in range(2 * HG):
                        q = z[:, b, :].rearrange("p (g u r) -> p g u r", u=2, r=h)[:, :, 1, :]
                        ins = pe.matmul(pair[1][:, b * CHUNK:(b + 1) * CHUNK], z[:, b, :], q, start=True, stop=True)
                elif k == LEVELS:
                    z = Z[1].rearrange("p (h b t) -> p h b t", b=2, t=P)
                    for h in range(HG):
                        ins = pe.matmul(pair[1][:, h * P:(h + 1) * P], z[:, h, 0, :], z[:, h, 1, :], start=True, stop=True)
                else:
                    for b in range(2 * HG):
                        cols = slice((b % 2) * P, (b % 2) * P + P)
                        ins = pe.matmul(pair[1][:, b * P:(b + 1) * P], kT[:, b // 2, cols], qT[:, b // 2, cols],
                                        start=True, stop=True)
                ins.then_inc(pair_full[1], 1)

            def outputs(half, rows):
                use = P1_HG[half] + 9
                pair_free(1, use)
                pe.wait_ge(row_ready, rows)
                av = A.rearrange("p (h b t) -> p h b t", b=2, t=P)
                axv = Ax.rearrange("p (h t) -> p h t", t=P)
                for h in range(HG):
                    cols = slice(h * DH, (h + 1) * DH)
                    pe.matmul(pair[1][:, cols], av[:, h, 0, :], vrow[:, 0, cols], start=True, stop=True)
                for h in range(HG):
                    cols = slice(h * DH, (h + 1) * DH)
                    o_ = pair[1][:, N + h * DH:N + (h + 1) * DH]
                    pe.matmul(o_, axv[:, h, :], vrow[:, 0, cols], start=True, stop=False)
                    ins = pe.matmul(o_, av[:, h, 1, :], vrow[:, 1, cols], start=False, stop=True)
                ins.then_inc(pair_full[1], 1)

            def behind_even(s):
                if s == 9:
                    rows_to(0, P0["F0"], urow[0], 1)
                if s == 17:
                    rows_to(0, P0["Q0"], urow[1], 2)
                if s == 34:
                    pe.wait_ge(h_ready_row, 1)
                    transposes(0, P0["C0"], urow[1])
                if s == 50:
                    pe.wait_ge(h_ready_row, 2)
                    transposes(0, P0["C1"], urow[1])
                if s == 67:
                    pe.wait_ge(o_ready, 1)
                    transposes(0, P0["O0"], orow.rearrange("p (r n) -> p r n", r=RT))
                if s == 73:
                    rows_to(0, P0["F1"], urow[0], 4)
                if s == 81:
                    rows_to(0, P0["Q1"], urow[1], 5)
                for half, base in ((0, 22), (1, 88)):
                    k = s - base
                    if 0 <= k <= 16 and k % 2 == 0:
                        level(half, k // 2)
                if s == 60:
                    outputs(0, 3)
                if s == 108:
                    outputs(1, 6)
                if s in (90, 94):
                    name = "MEAN" if s == 90 else "VAR"
                    pe.wait_ge(taps_done, 1)
                    if s == 94:
                        pe.wait_ge(csq_ready, 1)
                    pair_free(0, P0[name])
                    src = cv if s == 90 else csq
                    for c in range(8):
                        ins = pe.matmul(pair[0][:, 0:S], meanw, src[:, c, :], start=(c == 0), stop=(c == 7))
                    ins.then_inc(pair_full[0], 1)
                if s == 115:
                    pe.wait_ge(o_ready, 2)
                    transposes(0, P0["O1"], orow.rearrange("p (r n) -> p r n", r=RT))

            def forget_logits():
                pe.wait_ge(wf_ready, 1)
                pair_free(1, P1["FL"])
                for r in range(RT):
                    rows = slice(r * P, (r + 1) * P)
                    o_ = pair[1][:, r * N:r * N + HEADS]
                    for k in range(KT):
                        pe.matmul(o_, x_hi[:, k, rows], wf_hi[:, k, :], start=(k == 0), stop=False)
                        pe.matmul(o_, x_hi[:, k, rows], wf_lo[:, k, :], start=False, stop=False)
                        ins = pe.matmul(o_, x_lo[:, k, rows], wf_hi[:, k, :], start=False, stop=(k == KT - 1))
                ins.then_inc(pair_full[1], 1)

            def forget_sums():
                pe.wait_ge(ls_ready, 1)
                pe.wait_ge(odd_consts, 2)
                pair_free(1, P1["FC"])
                pe.matmul(pair[1][:, 0:HEADS], U2[:, 0:P], ls[:, 0:HEADS], start=True, stop=True)
                pe.matmul(pair[1][:, N:N + HEADS], U2[:, P:S], ls[:, 0:HEADS], start=True, stop=False)
                pe.matmul(pair[1][:, N:N + HEADS], U2[:, 0:P], ls[:, HEADS:], start=False, stop=True
                          ).then_inc(pair_full[1], 1)

            def forget_columns(g):
                pe.wait_ge(ls_ready, g + 1)
                pair_free(1, P1[f"FB{g}"])
                for h in range(HG):
                    pe.matmul(quad[1][:, h, :], lsb[:, 0, h, :], U2, start=True, stop=False, skip_group_check=True)
                    ins = pe.matmul(quad[1][:, h, P:S], lsb[:, 1, h, :], U2[:, 0:P], start=False, stop=True,
                                    skip_group_check=True)
                ins.then_inc(pair_full[1], 1)

            def scores(g):
                pe.wait_ge(qk_ready, 2 * g + 2)
                pair_free(0, P0_ATT + 5 * g + 2)
                pair_free(1, P1[f"S{g}"])
                for h in range(HG):
                    ins = pe.matmul(pair[0][:, h * P:(h + 1) * P], qT[:, h, 0:P], kT[:, h, 0:P], start=True, stop=True)
                ins.then_inc(pair_full[0], 1)
                for h in range(HG):
                    ins = pe.matmul(quad[1][:, h, :], qT[:, h, P:S], kT[:, h, :], start=True, stop=True)
                ins.then_inc(pair_full[1], 1)

            def probs(g):
                pe.wait_ge(prob_ready, g + 1)
                pair_free(0, P0_ATT + 5 * g + 3)
                pair_free(1, P1[f"P{g}"])
                p1 = sm[:, HG * P:].rearrange("p (h k) -> p h k", h=HG)
                for h in range(HG):
                    pe.transpose(quad[0][:, h, 0:P], sm[:, h * P:(h + 1) * P], ident[:, :])
                    ins = pe.transpose(quad[0][:, h, P:S], p1[:, h, 0:P], ident[:, :])
                ins.then_inc(pair_full[0], 1)
                for h in range(HG):
                    ins = pe.transpose(pair[1][:, h * P:(h + 1) * P], p1[:, h, P:S], ident[:, :])
                ins.then_inc(pair_full[1], 1)

            def attend(g):
                pe.wait_ge(pT_act, g + 1)
                pe.wait_ge(pT_dve, g + 1)
                pe.wait_ge(row_ready, 6 + 3 * g + 3)
                pair_free(0, P0_ATT + 5 * g + 4)
                a = pT[:, 0:HG * S].rearrange("p (h q) -> p h q", h=HG)
                b = pT[:, HG * S:].rearrange("p (h q) -> p h q", h=HG)
                for h in range(HG):
                    cols = slice(h * DH, (h + 1) * DH)
                    pe.matmul(quad[0][:, h, :], vrow[:, 0, cols], a[:, h, :], start=True, stop=False,
                              skip_group_check=True)
                    ins = pe.matmul(quad[0][:, h, P:S], vrow[:, 1, cols], b[:, h, :], start=False, stop=True,
                                    skip_group_check=True)
                ins.then_inc(pair_full[0], 1)

            def behind_odd(s):
                for g in range(4):
                    r = s - 24 * g
                    if r == 9:
                        rows_to(0, P0_ATT + 5 * g, urow[0], 6 + 3 * g + 1)
                        if g == 1:
                            forget_columns(1)
                    if r == 17:
                        rows_to(0, P0_ATT + 5 * g + 1, urow[1], 6 + 3 * g + 2)
                    if r == 20:
                        scores(g)
                    if r == 24:
                        probs(g)
                    if r == 26:
                        attend(g)
                if s == 8:
                    forget_logits()
                if s == 12:
                    forget_sums()
                if s == 14:
                    forget_columns(0)

            pe.wait_ge(x_loaded, 16 * RT)
            pe.wait_ge(consts, 2)
            pe.wait_ge(const_loaded, 16 * 6)
            for c in range(8):
                pe.transpose(pair[1][:, 32 * c:32 * c + CONV_W], cw_rows[0:CONV_W, c * P:(c + 1) * P],
                             ident[0:CONV_W, 0:CONV_W])
            pe.transpose(pair[1][:, 8 * 32:8 * 32 + 40], small_rows[0:40, :], ident[0:40, 0:40]
                         ).then_inc(pair_full[1], 1)
            groups = [{8: 1, 0: 2, 12: 3}, {0: 4, 4: 5, 8: 6, 12: 7}]
            for layer in range(DEPTH):
                behind = (behind_even, behind_odd)[layer]
                s0 = SLOT0[layer]
                for c in first_tile(2 * layer):
                    behind(c)
                for i in range(1, 12):
                    s, t = at
                    acc = acquire(layer, i)
                    for c in range(CPT):
                        ins = chunk(acc, X_, (CK * c, CK * c + 1), s + c, c == 0, c == CPT - 1)
                        behind(s + c - s0)
                    at[0], at[1] = s + CPT, t + 1
                for part in (EVEN_OUT, ODD_OUT)[layer]:
                    for j in range(NT):
                        s, t = at
                        acc = acquire(layer, t - TILE0[layer])
                        for i, k in enumerate(part[::CK]):
                            if j == 0 and k in groups[layer]:
                                pe.wait_ge(cat_ready, groups[layer][k])
                            ins = chunk(acc, C_, (k, k + 1), s + i, i == 0, i == len(part) // CK - 1)
                            behind(s + i - s0)
                        at[0], at[1] = s + len(part) // CK, t + 1

                base, tbase, p0base = SLOT_MLP[layer], TILE_MLP[layer], P0_MLP[layer]
                assert at == [base, tbase]

                def mlp_tile(b, i, first_block=False):
                    start = first_block and i == 0
                    t = tbase + i
                    acc = gemm[t % 2]
                    j = (i - 2) % (2 * NT)
                    if j < NT:
                        pe.wait_ge(relu_done, b * NT + (layer * FB * NT + j + 1))
                    else:
                        pe.wait_ge(x_sum, b * NT + (2 * NT * (layer + 1) + FB * NT * layer + j - NT + 1 - NT * (i < 2)))
                    operand = X_ if i < NT else C_
                    if start:
                        x_group(2 * layer + 1, 0)
                        x_group(2 * layer + 1, 1)
                    for c in range(CPT):
                        s = base + i * CPT + c
                        if start and c % 2 == 0:
                            pe.wait_ge(xt_ready, NT * (2 * layer + 1) + c // 2 + 1)
                        if i == NT and c % 2 == 0:
                            pe.wait_ge(h_ready, b * NT + (layer * FB * NT + c // 2 + 1))
                        pe.wait_ge(lo_ready, b * (2 * NT * CPT) + (s + 1))
                        for kk in range(CK):
                            ins = products(acc, operand[0], operand[1], CK * c + kk, kk, s % RING,
                                           c == 0 and kk == 0, c == CPT - 1 and kk == CK - 1)
                        ins.then_inc(chunk_used, 1)
                        if start and c in (1, 3):
                            x_group(2 * layer + 1, 2 + c // 2)
                        if c == 1 and 1 <= i <= NT:
                            pe.wait_ge(h_row, b * NT + (layer * FB * NT + i))
                            if i == 1 and first_block:
                                pair_free(0, p0base)
                            else:
                                pe.wait_ge(h_ready, b * NT + (layer * FB * NT + i - 1))
                            for cc in range(4):
                                for r in range(RT):
                                    ins = pe.transpose(quad[0][:, cc, r * P:(r + 1) * P],
                                                       urow[(i - 1) % 2][:, r, cc * P:(cc + 1) * P], ident[:, :])
                            ins.then_inc(pair_full[0], 1)

                for i in range(2 * NT):
                    mlp_tile(0, i, first_block=True)
                with pe.Fori(1, FB) as b:
                    for i in range(2 * NT):
                        mlp_tile(b, i)
                at[0], at[1] = base + MLP_SLOTS, tbase + MLP_TILES


_INS = ["x", "ev_w_in", "ev_conv_w", "ev_conv_b", "ev_conv_ln_g", "ev_conv_ln_b", "hgrn_lb_logits", "ev_gnorm_g",
        "ev_w_out", "od_w_in", "fox_b_f", "rel_bias", "od_w_out", "ln_mix_g", "ln_mix_b", "mlp_w1", "mlp_w2",
        "ln_mlp_g", "ln_mlp_b"]


def kernel(**inputs):
    import numpy as np
    import concourse.bacc as bacc
    from concourse.bass_utils import run_bass_kernel_spmd

    nc = bacc.Bacc("TRN2", target_bir_lowering=False, num_devices=1)
    arrays, args = {}, []
    for name in _INS:
        a = np.ascontiguousarray(inputs[name])
        arrays[f"in_{name}"] = a
        args.append(nc.dram_tensor(f"in_{name}", a.shape, mybir.dt.from_np(a.dtype), kind="ExternalInput").ap())
    args.append(nc.dram_tensor("out_0", (1, S, D), F32, kind="ExternalOutput").ap())
    trunk(nc, *args)
    r = run_bass_kernel_spmd(nc, [arrays], core_ids=[0])
    return r.results[0]["out_0"]
```

```python
from contextlib import ExitStack

import concourse.bass as bass
from concourse import mybir

F32, F32R, I8 = mybir.dt.float32, mybir.dt.float32r, mybir.dt.int8
ACT, ALU, AX = mybir.ActivationFunctionType, mybir.AluOpType, mybir.AxisListType

D = 2048
S = 256
P = 128
RT = S // P
KT = D // P
N = 512
CK = 2
CPT = KT // CK
DEPTH = 2
ALPHA = float((2 * DEPTH) ** 0.25)
EPS = 1e-5
CONV_CH, CONV_W = D // 2, 31
HEADS, DH = 8, 128
HG = 4
KDIM = HEADS * DH
REL_TABLE = 320
CHUNK = 64
D_FF = 4 * D
FB = D_FF // D
SCALE = float(DH) ** -0.5
NEG = -3.0e38
LEVELS = 7
F_MIN = 2.0 ** -63

F_COL, Q_COL, I_COL, G_COL = 2 * CONV_CH + KDIM, 2 * CONV_CH, 2 * CONV_CH + 2 * KDIM, 2 * CONV_CH + 3 * KDIM
EVEN_TILES = [CONV_CH, 0, F_COL, Q_COL, CONV_CH + N, N, I_COL, G_COL,
              F_COL + N, Q_COL + N, I_COL + N, G_COL + N]
FOX_F = 3 * KDIM
ODD_TILES = [base + third * KDIM for base in (0, N, FOX_F + HEADS, FOX_F + HEADS + N) for third in range(3)]
EVEN_OUT = [[8, 9, 10, 11, 0, 1, 2, 3, 4, 5, 6, 7], [12, 13, 14, 15]]
ODD_OUT = [list(range(12)), list(range(12, 16))]
NT = D // N
IN_SLOTS = 12 * CPT
OUT_A, OUT_B = 12 // CK, 4 // CK
LAYER_SLOTS = IN_SLOTS + NT * (OUT_A + OUT_B)
MLP_SLOTS = FB * 2 * NT * CPT
LAYER_TILES, MLP_TILES = 12 + 2 * NT, FB * 2 * NT
SLOT0 = [0, LAYER_SLOTS + MLP_SLOTS]
SLOT_MLP = [LAYER_SLOTS, 2 * LAYER_SLOTS + MLP_SLOTS]
TILE0 = [0, LAYER_TILES + MLP_TILES]
TILE_MLP = [LAYER_TILES, 2 * LAYER_TILES + MLP_TILES]
SLOTS = 2 * (LAYER_SLOTS + MLP_SLOTS)
RING = 4
PIECES = [(0, 2), (2, 2), (4, 4), (8, 4), (12, 4)]
NP = len(PIECES)

def numbered(*names):
    return {name: i for i, name in enumerate(names)}


def pieces(which, p):
    return [("x", which, i) for i in range(p, NP, 2)]


HIDDEN = [[("h", layer, i) for i in range(FB * NT)] for layer in range(DEPTH)]
USE = [numbered(*pieces(0, 0), "C0", "F0", "Q0", "C1", "O0", "F1", "Q1", "mean", "variance", "O1",
                *pieces(1, 0), *HIDDEN[0], *pieces(2, 0),
                *[(name, g) for g in range(4) for name in ("q", "k", "scores", "probs", "out")],
                *pieces(3, 0), *HIDDEN[1]),
       numbered(*pieces(0, 1), "params", *[("level", half, k) for half in range(2) for k in range(10)],
                *pieces(1, 1), *pieces(2, 1), "logits", "F rows", ("F", 0), ("scores", 0), ("probs", 0), ("F", 1),
                *[(name, g) for g in range(1, 4) for name in ("scores", "probs")], *pieces(3, 1))]


def trunk(nc, x, ev_w_in, ev_conv_w, ev_conv_b, ev_conv_ln_g, ev_conv_ln_b, hgrn_lb_logits, ev_gnorm_g, ev_w_out,
          od_w_in, fox_b_f, rel_bias, od_w_out, ln_mix_g, ln_mix_b, mlp_w1, mlp_w2, ln_mlp_g, ln_mlp_b, out):
    w_in, w_out = [ev_w_in[0], od_w_in[0]], [ev_w_out[0], od_w_out[0]]
    with ExitStack() as ctx:
        def sb(name, shape, dt):
            return ctx.enter_context(nc.sbuf_tensor(name, shape, dt))

        def sem(name):
            return ctx.enter_context(nc.semaphore(name))

        raw = sb("raw", [P, RING, CK, N], F32)
        w_hi = sb("w_hi", [P, RING, CK, N], F32R)
        w_lo = sb("w_lo", [P, RING, CK, N], F32R)
        x_hi = sb("x_hi", [P, KT, S], F32R)
        x_lo = sb("x_lo", [P, KT, S], F32R)
        c_hi = sb("c_hi", [P, KT, S], F32R)
        c_lo = sb("c_lo", [P, KT, S], F32R)
        X = sb("X", [P, RT, D], F32)
        lnp = sb("lnp", [P, 2, D], F32)
        ident = sb("ident", [P, P], F32)
        stats = sb("stats", [P, RT, NT, 6], F32)
        mv = sb("mv", [P, RT, 2], F32)
        rstd = sb("rstd", [P, RT, 1], F32)
        mhalf = sb("mhalf", [P, RT * HG], F32)
        nbias = sb("nbias", [P, RT], F32)
        scr = sb("scr", [P, 14800], F32)
        used = [0]

        def cut(n):
            used[0] += n
            assert used[0] <= 14800, used[0]
            return scr[:, used[0] - n:used[0]]

        urow = [cut(RT * N).rearrange("p (r n) -> p r n", r=RT) for _ in range(2)]
        qT = cut(HG * S).rearrange("p (h t) -> p h t", h=HG)
        kT = cut(HG * S).rearrange("p (h t) -> p h t", h=HG)
        vrow = cut(RT * N).rearrange("p (r n) -> p r n", r=RT)
        both = used[0]
        L = cut(HG * S)
        Dm = cut(HG * S)
        Z = [cut(HG * S) for _ in range(2)]
        A = cut(HG * RT * P)
        Ax = cut(HG * P)
        G = cut(RT * N)
        PADW = CONV_W - 1 + S
        hpad = [cut(4 * PADW).rearrange("p (c t) -> p c t", c=4) for _ in range(2)]
        cw = cut(8 * CONV_W).rearrange("p (c j) -> p c j", c=8)
        small = cut(40)
        cpar = small[:, 0:24].rearrange("p (w c) -> p w c", w=3)
        lbl = small[:, 24:40].rearrange("p (w h) -> p w h", w=2)
        cw_rows, small_rows = Z[0], L[:, 0:P]
        lb = cut(8)
        oml = cut(8)
        ss = cut(8)
        crs = cut(S)
        meanw = cut(P)
        cv = lnp[:, 0, :].rearrange("p (c t) -> p c t", c=8)
        orow = lnp[:, 1, 0:RT * N]
        gn = lnp[:, 1, RT * N:RT * N + KDIM]
        csq = scr[:, both + 6 * 1024 + 512:both + 6 * 1024 + 512 + 2048].rearrange("p (c t) -> p c t", c=8)
        cvar = scr[:, both + 6 * 1024 + 512 + 2048:both + 6 * 1024 + 512 + 2048 + S]
        even_end = used[0]
        used[0] = both
        sm = cut(HG * (P + S))
        pT = cut(HG * (P + S))
        fbias = cut(HG * (P + S))
        rel = cut(HEADS * S).rearrange("p (h j) -> p h j", h=HEADS)
        sel = cut(HEADS * P).rearrange("p (h c) -> p h c", h=HEADS)
        ones = cut(S)
        tri = cut(S)
        WF = KT * HEADS + P - HEADS
        wf = cut(WF)
        bf = cut(1)
        zf = cut(S)
        za = cut(S)
        ls = cut(S)
        Ft = cut(S)
        Fc = cut(RT * HEADS)
        mx = cut(RT * HG)
        sums = cut(RT * HG)
        rs = cut(RT * HG)
        wf_hi = sb("wf_hi", [P, WF], F32R)
        wf_lo = sb("wf_lo", [P, WF], F32R)
        rstm = sb("rstm", [P, HG * S], mybir.dt.bfloat16)
        masks = sb("masks", [P, LEVELS, CHUNK], I8)
        imask = sb("imask", [P, P], I8)

        gemm = [ctx.enter_context(nc.psum_tensor(f"gemm{i}", [P, RT, N], F32)) for i in range(2)]
        pair = [ctx.enter_context(nc.psum_tensor(f"pair{i}", [P, RT * N], F32)) for i in range(2)]
        quad = [p[:, :].rearrange("p (k t) -> p k t", k=4) for p in pair]

        raw_full = [sem(f"raw_full{i}") for i in range(RING)]
        hi_ready, lo_ready = sem("hi_ready"), sem("lo_ready")
        chunk_used = sem("chunk_used")
        relu_done = sem("relu_done")
        pair_full = [sem(f"pair_full{i}") for i in range(2)]
        params_ready = sem("params_ready")
        x_loaded = [sem(f"x_loaded{g}") for g in range(NT)]
        const_loaded, consts, xhat, nb_ready = sem("const_loaded"), sem("consts"), sem("xhat"), sem("nb_ready")
        cvar_ready, croot_ready, F_ready = sem("cvar_ready"), sem("croot_ready"), sem("F_ready")
        odd_loaded, odd_consts, lnp_loaded = sem("odd_loaded"), sem("odd_consts"), sem("lnp_loaded")
        xt_hi, xt_ready = sem("xt_hi"), sem("xt_ready")
        cat_hi, cat_ready = sem("cat_hi"), sem("cat_ready")
        h_row, h_hi, h_ready = sem("h_row"), sem("h_hi"), sem("h_ready")
        act_link, dve_link, pool_link = sem("act_link"), sem("dve_link"), sem("pool_link")
        row_ready = sem("row_ready")
        x_sum, normed, x_scaled = sem("x_sum"), sem("normed"), sem("x_scaled")
        var_ready, rstd_ready = sem("var_ready"), sem("rstd_ready")
        gate_ready, h_ready_row, pad_ready = sem("gate_ready"), sem("h_ready_row"), sem("pad_ready")
        taps_done = sem("taps_done")
        lb_exp, lb_ready, f_ready, lnf_ready, L_ready = (sem("lb_exp"), sem("lb_ready"), sem("f_ready"),
                                                         sem("lnf_ready"), sem("L_ready"))
        sig_ready, q_ready, g_sig = sem("sig_ready"), sem("q_ready"), sem("g_sig")
        diff_ready, exp_ready, z_ready = sem("diff_ready"), sem("exp_ready"), sem("z_ready")
        scores_in, scores_clear, o_row, o_ready = sem("scores_in"), sem("scores_clear"), sem("o_row"), sem("o_ready")
        cen_ready, csq_ready, cn_ready, csig_ready, conv_ready = (sem("cen_ready"), sem("csq_ready"), sem("cn_ready"),
                                                                  sem("csig_ready"), sem("conv_ready"))
        wf_hi_ready, wf_ready, za_ready, zl_ready, ls_ready = (sem("wf_hi_ready"), sem("wf_ready"), sem("za_ready"),
                                                               sem("zl_ready"), sem("ls_ready"))
        max_ready, prob_exp, prob_ready, pT_act, pT_dve = (sem("max_ready"), sem("prob_exp"), sem("prob_ready"),
                                                           sem("pT_act"), sem("pT_dve"))
        qk_ready = sem("qk_ready")
        g_silu, z_sum, Fc_ready, fb_ready, scores_read = (sem("g_silu"), sem("z_sum"), sem("Fc_ready"), sem("fb_ready"),
                                                          sem("scores_read"))
        k_ready, square_ready = sem("k_ready"), sem("square_ready")
        stored = sem("stored")

        block = ctx.enter_context(nc.Block())

        def tile_done(eng, layer, i):
            part_a, part_b = min(max(i - 12, 0), NT), max(i - 12 - NT, 0)
            end = CPT * min(i, 12) + OUT_A * part_a + OUT_B * part_b
            end += CPT if i < 12 else OUT_A if i < 12 + NT else OUT_B
            eng.wait_ge(chunk_used, SLOT0[layer] + end)

        def raw_wait(eng, s):
            eng.wait_ge(raw_full[s % RING], 16 * (s // RING + 1))

        @block.sync
        def _(sp):
            def load(s, wmat, k0, c0):
                if s >= RING:
                    sp.wait_ge(lo_ready, s - RING + 1)
                sp.dma_start(raw[:, s % RING], wmat[k0 * P:(k0 + CK) * P, c0:c0 + N].rearrange("(k p) n -> p k n", p=P)
                             ).then_inc(raw_full[s % RING], 16)

            for layer in range(DEPTH):
                s = SLOT0[layer]
                for c0 in (EVEN_TILES, ODD_TILES)[layer]:
                    for c in range(CPT):
                        if s < 2 * NT and s % 2 == 0:
                            cols = slice(s // 2 * N, (s // 2 + 1) * N)
                            sp.dma_start(X[:, :, cols], x[0, :, cols].rearrange("(r p) n -> p r n", p=P)
                                         ).then_inc(x_loaded[s // 2], 16)
                        load(s, w_in[layer], CK * c, c0)
                        s += 1
                for part in (EVEN_OUT, ODD_OUT)[layer]:
                    for j in range(NT):
                        for k in part[::CK]:
                            load(s, w_out[layer], k, j * N)
                            s += 1
                base = SLOT_MLP[layer]
                assert s == base and base % RING == 0
                w1, w2 = mlp_w1[layer], mlp_w2[layer]
                with sp.Fori(0, FB) as b:
                    with sp.Fori(0, NT) as j:
                        for c in range(CPT):
                            sp.wait_ge(lo_ready, b * (2 * NT * CPT) + j * CPT + (base + c - RING + 1))
                            sp.dma_start(raw[:, c % RING],
                                         w1[CK * c * P:CK * (c + 1) * P, bass.ds(b * D + j * N, N)].rearrange(
                                             "(k p) n -> p k n", p=P)).then_inc(raw_full[c % RING], 16)
                    with sp.Fori(0, NT) as j:
                        for c in range(CPT):
                            sp.wait_ge(lo_ready, b * (2 * NT * CPT) + j * CPT + (base + NT * CPT + c - RING + 1))
                            sp.dma_start(raw[:, c % RING],
                                         w2[bass.ds(b * D + CK * c * P, CK * P), bass.ds(j * N, N)].rearrange(
                                             "(k p) n -> p k n", p=P)).then_inc(raw_full[c % RING], 16)
            for i, (k0, n_) in enumerate(PIECES):
                sp.wait_ge(normed, 3 * NP + i + 1)
                cols = slice(k0 * P, (k0 + n_) * P)
                sp.dma_start(out[0, :, cols].rearrange("(r p) n -> p r n", p=P), X[:, :, cols]).then_inc(stored, 16)
            sp.wait_ge(stored, 16 * NP)

        @block.gpsimd
        def _(pool):
            n = [0]

            def link(ins):
                n[0] += 1
                ins.then_inc(pool_link, 1)
                pool.wait_ge(pool_link, n[0])

            def row(dst, src, width, s):
                pool.dma_start(dst, src.rearrange("(o n) -> o n", o=1).broadcast_to([P, width])).then_inc(s, 16)

            def ln_params(which):
                g, b = [(ln_mix_g[0], ln_mix_b[0]), (ln_mlp_g[0], ln_mlp_b[0]),
                        (ln_mix_g[1], ln_mix_b[1]), (ln_mlp_g[1], ln_mlp_b[1])][which]
                row(lnp[:, 0, :], g, D, lnp_loaded)
                row(lnp[:, 1, :], b, D, lnp_loaded)

            def inverse_root(which):
                pool.wait_ge(var_ready, which + 1)
                pool.tensor_tensor(rstd[:, :, 0], mv[:, :, 1], mhalf[:, 0:RT], ALU.pow).then_inc(rstd_ready, 1)

            link(pool.memset(ident[:, :], 0.0))
            pool.affine_select(out=ident[:, :], in_=ident[:, :], compare_op=ALU.not_equal, fill=1.0, base=0,
                               pattern=[[-1, P]], channel_multiplier=1).then_inc(consts, 1)
            link(pool.memset(imask[:, :], 0))
            link(pool.affine_select(out=imask[:, :], in_=imask[:, :], compare_op=ALU.not_equal, fill=1.0, base=0,
                                    pattern=[[-1, P]], channel_multiplier=1))
            link(pool.memset(masks[:, :, :], 1))
            for lv in range(LEVELS):
                h = CHUNK >> lv
                m = masks[:, lv, :].rearrange("p (g r) -> p g r", r=h)
                link(pool.affine_select(out=m, in_=m, compare_op=ALU.is_ge, fill=0.0, base=0,
                                        pattern=[[-2 * h, CHUNK // h], [0, h]], channel_multiplier=1))
                link(pool.affine_select(out=m, in_=m, compare_op=ALU.is_ge, fill=0.0, base=h - 1,
                                        pattern=[[2 * h, CHUNK // h], [0, h]], channel_multiplier=-1))
            link(pool.memset(rstm[:, :], 1.0))
            link(pool.memset(rstm[:, :].rearrange("p (g t) -> p g t", t=P)[:, :, 0:1], 0.0))
            pool.memset(mhalf[:, :], -0.5)
            pool.memset(meanw, 1.0 / CONV_CH)
            for hp in hpad:
                pool.memset(hp[:, :, 0:CONV_W - 1], 0.0)
            link(pool.memset(A, 0.0))
            pool.dma_start(cw_rows[0:CONV_W, :], ev_conv_w[0]).then_inc(const_loaded, 16)
            for i, v in enumerate((ev_conv_b, ev_conv_ln_g, ev_conv_ln_b)):
                pool.dma_start(small_rows[8 * i:8 * i + 8, :], v[0].rearrange("(c p) -> c p", p=P)
                               ).then_inc(const_loaded, 16)
            pool.dma_start(small_rows[24:40, :], hgrn_lb_logits.rearrange("w (h k) -> (w h) k", k=DH)
                           ).then_inc(const_loaded, 16)
            row(gn, ev_gnorm_g[0], KDIM, const_loaded)
            pool.nop().then_inc(consts, 1)
            for half in range(2):
                if half == 1:
                    pool.wait_ge(pair_full[1], USE[1]["level", 0, 9] + 1)
                    pool.memset(A, 0.0).then_inc(scores_clear, 1)
                pool.wait_ge(var_ready, half + 1)
                pool.tensor_tensor(ss, ss, mhalf[:, 0:8], ALU.pow).then_inc(rstd_ready, 1)
            pool.wait_ge(pair_full[0], USE[0]["O1"] + 1)
            pool.wait_ge(cat_ready, 2)
            ln_params(0)
            pool.wait_ge(cat_ready, 3)
            pool.dma_start(wf[:, 0:KT * HEADS].rearrange("p (k h) -> p k h", k=KT),
                           od_w_in[0, :, FOX_F:FOX_F + HEADS].rearrange("(k p) h -> p k h", p=P)).then_inc(odd_loaded, 16)
            pool.dma_start(bf[0:HEADS, :], fox_b_f.rearrange("o h -> h o")).then_inc(odd_loaded, 16)
            for lo in range(2):
                j0 = CHUNK if lo == 0 else 0
                base = rel_bias[0, 0:1, lo * CHUNK - CHUNK + j0:lo * CHUNK - CHUNK + j0 + 1]
                pool.dma_start(rel[lo * CHUNK:(lo + 1) * CHUNK, :, j0:S],
                               bass.AP(base.tensor, base.offset, [[1, CHUNK], [REL_TABLE, HEADS], [1, S - j0]])
                               ).then_inc(odd_loaded, 16)
            pool.memset(rel[0:CHUNK, :, 0:CHUNK], NEG)
            pool.memset(wf[:, KT * HEADS:], 0.0)
            pool.memset(ones, 1.0)
            link(pool.memset(sel, 0.0))
            link(pool.memset(tri, 0.0))
            pool.affine_select(out=sel, in_=sel, compare_op=ALU.not_equal, fill=1.0, base=0,
                               pattern=[[-1, HEADS], [0, P]], channel_multiplier=1).then_inc(odd_consts, 1)
            pool.affine_select(out=tri[:, P:S], in_=tri[:, P:S], compare_op=ALU.is_ge, fill=NEG, base=0,
                               pattern=[[-1, P]], channel_multiplier=1).then_inc(odd_consts, 1)
            inverse_root(2)
            for which in range(1, 4):
                pool.wait_ge(normed, NP * which)
                ln_params(which)
                inverse_root(2 + which)

        @block.scalar
        def _(act):
            at = [0]
            n = [0]

            def link(ins):
                n[0] += 1
                ins.then_inc(act_link, 1)
                act.wait_ge(act_link, n[0])

            def split(s):
                raw_wait(act, s)
                if s >= RING:
                    act.wait_ge(chunk_used, s - RING + 1)
                act.activation(w_hi[:, s % RING], raw[:, s % RING], ACT.Copy).then_inc(hi_ready, 1)

            def upto(s):
                while at[0] <= s:
                    split(at[0])
                    at[0] += 1

            def evac(layer, i, dst, func, done):
                tile_done(act, layer, i)
                act.activation(dst, gemm[(TILE0[layer] + i) % 2][:, :, :], func).then_inc(done, 1)

            def hi_of(p, name, dst, done):
                act.wait_ge(pair_full[p], USE[p][name] + 1)
                act.activation(dst, quad[p][:, 0:dst.shape[1], :], ACT.Copy).then_inc(done, 1)

            def x_piece_hi(which, i):
                k0, n_ = PIECES[i]
                hi_of(i % 2, ("x", which, i), x_hi[:, k0:k0 + n_, :], xt_hi)

            def layer_norm(which):
                act.wait_ge(nb_ready, which)
                for i in range(1, NP):
                    k0, n_ = PIECES[i]
                    cols = slice(k0 * P, (k0 + n_) * P)
                    for r in range(RT):
                        act.activation(X[:, r, cols], X[:, r, cols], ACT.Identity, scale=rstd[:, r, :],
                                       bias=nbias[:, r:r + 1]).then_inc(xhat, 1)
                    if which < 4 and i >= 1:
                        x_piece_hi(which, i - 1)
                if which < 4:
                    x_piece_hi(which, NP - 1)

            def scale_residual(which):
                for r in range(RT):
                    ins = act.activation(X[:, r, :], X[:, r, :], ACT.Copy, scale=ALPHA)
                ins.then_inc(x_scaled, 1)

            x_piece_hi(0, 0)
            upto(0)
            x_piece_hi(0, 1)
            upto(1)
            x_piece_hi(0, 2)
            upto(3)
            x_piece_hi(0, 3)
            x_piece_hi(0, 4)
            scale_residual(0)

            def forget(half, s0, i):
                upto(s0 + 11)
                act.wait_ge(h_ready_row, half + 1)
                evac(0, i, urow[0], ACT.Copy, row_ready)
                upto(s0 + 13)
                if half == 1:
                    act.wait_ge(z_ready, 8)
                act.wait_ge(pair_full[0], USE[0][f"F{half}"] + 1)
                act.activation(Dm, pair[0][:, :], ACT.Sigmoid).then_inc(sig_ready, 1)
                upto(s0 + 14)
                act.wait_ge(sig_ready, 2 * half + 1)
                act.wait_ge(lb_ready, 1)
                if half == 1:
                    act.wait_ge(pair_full[1], USE[1]["level", 0, 8] + 1)
                for h in range(HG):
                    c = HG * half + h
                    ins = act.activation(L[:, h * S:(h + 1) * S], Dm[:, h * S:(h + 1) * S], ACT.Identity,
                                         scale=oml[:, c:c + 1], bias=lb[:, c:c + 1])
                link(ins)
                act.activation(kT.rearrange("p h t -> p (h t)"), L, ACT.Identity, scale=-1.0, bias=1.0
                               ).then_inc(k_ready, 1)
                upto(s0 + 16)
                act.wait_ge(f_ready, half + 1)
                act.activation(Dm, L, ACT.Ln).then_inc(lnf_ready, 1)

            def query(half, s0, i):
                upto(s0 + 11)
                act.wait_ge(pair_full[0], USE[0][f"C{half}"] + 1)
                evac(0, i, urow[1], ACT.Copy, row_ready)
                upto(s0 + 13)
                act.wait_ge(L_ready, half + 1)
                act.wait_ge(pair_full[0], USE[0][f"Q{half}"] + 1)
                act.activation(Dm, pair[0][:, :], ACT.Sigmoid).then_inc(sig_ready, 1)

            def exps(half, k):
                act.wait_ge(diff_ready, 8 * half + k + 1)
                if k < LEVELS:
                    h = CHUNK >> k
                    v = Dm.rearrange("p (g u r) -> p g u r", u=2, r=h)
                    act.activation(v[:, :, 0, :], v[:, :, 0, :], ACT.Exp, scale=-1.0)
                    act.activation(v[:, :, 1, :], v[:, :, 1, :], ACT.Exp).then_inc(exp_ready, 1)
                else:
                    v = Dm.rearrange("p (h b t) -> p h b t", b=2, t=P)
                    act.activation(v, v, ACT.Exp).then_inc(exp_ready, 1)

            def out_rows(half):
                act.wait_ge(pair_full[1], USE[1]["level", half, 9] + 1)
                if half == 1:
                    act.wait_ge(pair_full[0], USE[0]["O0"] + 1)
                act.activation(orow, pair[1][:, :], ACT.Copy).then_inc(o_row, 1)
                act.wait_ge(o_row, half + 1)
                for b in range(2 * HG):
                    cols = slice(b * DH, (b + 1) * DH)
                    ins = act.activation(Dm[:, cols], orow[:, cols], ACT.Square, accum_out=ss[:, b:b + 1])
                ins.then_inc(square_ready, 1)

            def group_hi(name, k0):
                hi_of(0, name, c_hi[:, k0:k0 + 4, :], cat_hi)

            upto(11)
            evac(0, 0, urow[0], ACT.Sigmoid, gate_ready)
            act.wait_ge(lb_exp, 1)
            act.activation(lbl, lbl, ACT.Exp).then_inc(lb_exp, 1)
            upto(22)
            act.wait_ge(pair_full[0], USE[0]["C0"] + 1)
            act.activation(hpad[0][:, :, CONV_W - 1:], quad[0], ACT.Copy).then_inc(pad_ready, 1)
            forget(0, 16, 2)
            query(0, 24, 3)
            upto(39)
            exps(0, 0)
            upto(41)
            exps(0, 1)
            upto(43)
            act.wait_ge(pair_full[0], USE[0]["F0"] + 1)
            evac(0, 4, urow[0], ACT.Sigmoid, gate_ready)
            for k in range(2, 7):
                upto(39 + 2 * k)
                exps(0, k)
            upto(54)
            exps(0, 7)
            act.wait_ge(pair_full[0], USE[0]["C1"] + 1)
            act.activation(hpad[1][:, :, CONV_W - 1:], quad[0], ACT.Copy).then_inc(pad_ready, 1)
            upto(59)
            evac(0, 6, vrow, ACT.Copy, row_ready)
            upto(64)
            out_rows(0)
            upto(67)
            evac(0, 7, G.rearrange("p (r n) -> p r n", r=RT), ACT.Sigmoid, g_sig)
            upto(71)
            group_hi("O0", 8)
            forget(1, 64, 8)
            query(1, 72, 9)
            upto(89)
            exps(1, 0)
            upto(91)
            exps(1, 1)
            act.wait_ge(pair_full[1], USE[1]["level", 0, 9] + 1)
            evac(0, 10, vrow, ACT.Copy, row_ready)
            upto(93)
            exps(1, 2)
            upto(94)
            act.wait_ge(cen_ready, 1)
            act.activation(csq, cv, ACT.Square).then_inc(csq_ready, 1)
            upto(95)
            exps(1, 3)
            upto(97)
            exps(1, 4)
            act.wait_ge(cvar_ready, 1)
            link(act.activation(crs, cvar, ACT.Ln))
            act.activation(crs, crs, ACT.Exp, scale=-0.5).then_inc(croot_ready, 1)
            upto(99)
            exps(1, 5)
            act.wait_ge(o_ready, 1)
            evac(0, 11, G.rearrange("p (r n) -> p r n", r=RT), ACT.Sigmoid, g_sig)
            act.wait_ge(cn_ready, 1)
            act.wait_ge(pair_full[0], USE[0]["variance"] + 1)
            for c in range(8):
                ins = act.activation(csq[:, c, :], cv[:, c, :], ACT.Sigmoid, scale=cpar[:, 1, c:c + 1],
                                     bias=cpar[:, 2, c:c + 1])
            link(ins)
            for c in range(8):
                ins = act.activation(cv[:, c, :], cv[:, c, :], ACT.Identity, scale=cpar[:, 1, c:c + 1],
                                     bias=cpar[:, 2, c:c + 1])
            ins.then_inc(csig_ready, 1)
            upto(101)
            exps(1, 6)
            act.wait_ge(conv_ready, 1)
            act.activation(c_hi[:, 0:8, :], cv, ACT.Copy).then_inc(cat_hi, 1)
            upto(103)
            exps(1, 7)
            upto(112)
            out_rows(1)
            upto(118)
            group_hi("O1", 12)
            upto(SLOT_MLP[0] + RING - 1)

            def mlp_tile(base, tbase, layer, b, i, last=False):
                first = base + i * CPT + RING
                for c in range(CPT):
                    s = first + c
                    if last and b * (2 * NT * CPT) + s >= SLOTS:
                        break
                    act.wait_ge(raw_full[s % RING], b * (16 * 2 * NT * CPT // RING) + 16 * (s // RING + 1))
                    act.wait_ge(chunk_used, b * (2 * NT * CPT) + (s - RING + 1))
                    act.activation(w_hi[:, s % RING], raw[:, s % RING], ACT.Copy).then_inc(hi_ready, 1)
                    if c == 1 and 1 <= i <= NT:
                        act.wait_ge(pair_full[0], b * NT + (USE[0]["h", layer, 0] + i))
                        act.activation(c_hi[:, 4 * (i - 1):4 * i, :], quad[0], ACT.Copy).then_inc(h_hi, 1)
                if i < NT:
                    t = tbase + i
                    act.wait_ge(chunk_used, b * (2 * NT * CPT) + (base + (i + 1) * CPT))
                    act.activation(urow[i % 2], gemm[t % 2][:, :, :], ACT.Relu).then_inc(relu_done, 1)
                    act.wait_ge(relu_done, b * NT + (layer * FB * NT + i + 1))
                    act.activation(urow[i % 2], urow[i % 2], ACT.Square).then_inc(h_row, 1)

            def mlp(layer):
                base, tbase = SLOT_MLP[layer], TILE_MLP[layer]
                whole = FB if layer == 0 else FB - 1
                with act.Fori(0, whole) as b:
                    for i in range(2 * NT):
                        mlp_tile(base, tbase, layer, b, i)
                if layer == 1:
                    for i in range(2 * NT):
                        mlp_tile(base, tbase, layer, whole, i, last=True)
                at[0] = base + MLP_SLOTS + RING

            layer_norm(1)
            scale_residual(1)
            mlp(0)

            layer_norm(2)
            scale_residual(2)
            o = SLOT0[1]
            act.wait_ge(odd_loaded, 16 * 4)
            act.activation(wf_hi[:, :], wf, ACT.Copy).then_inc(wf_hi_ready, 1)
            for g in range(4):
                s0 = o + 24 * g
                upto(s0 + 6 if g else s0 + 3)
                if g:
                    group_hi(("out", g - 1), 4 * (g - 1))
                upto(s0 + 11)
                evac(1, 3 * g, urow[0], ACT.Copy, row_ready)
                if g == 0:
                    upto(s0 + 12)
                    act.wait_ge(za_ready, 1)
                    link(act.activation(za[0:HEADS, :], za[0:HEADS, :], ACT.Exp, scale=-1.0))
                    act.activation(za[0:HEADS, :], za[0:HEADS, :], ACT.Ln, bias=1.0).then_inc(zl_ready, 1)
                upto(s0 + 13)
                act.wait_ge(pair_full[0], USE[0]["q", g] + 1)
                act.activation(qT, quad[0], ACT.Copy).then_inc(qk_ready, 1)
                upto(s0 + 19)
                evac(1, 3 * g + 1, urow[1], ACT.Copy, row_ready)
                upto(s0 + 21)
                act.wait_ge(pair_full[0], USE[0]["k", g] + 1)
                act.activation(kT, quad[0], ACT.Copy).then_inc(qk_ready, 1)
                upto(s0 + 25)
                act.wait_ge(max_ready, g + 1)
                for q in range(RT):
                    width = (q + 1) * P
                    v = sm[:, q * HG * P:q * HG * P + HG * width].rearrange("p (h k) -> p h k", h=HG)
                    for h in range(HG):
                        i = q * HG + h
                        ins = act.activation(v[:, h, :], v[:, h, :], ACT.Exp, bias=mx[:, i:i + 1],
                                             accum_out=sums[:, i:i + 1])
                ins.then_inc(prob_exp, 1)
                upto(s0 + 27)
                evac(1, 3 * g + 2, vrow, ACT.Copy, row_ready)
                upto(s0 + 28)
                act.wait_ge(pair_full[0], USE[0]["probs", g] + 1)
                act.activation(pT[:, 0:HG * S], pair[0][:, :], ACT.Copy).then_inc(pT_act, 1)
            upto(o + 72 + 30)
            group_hi(("out", 3), 12)
            upto(SLOT_MLP[1] + RING - 1)
            layer_norm(3)
            scale_residual(3)
            mlp(1)
            layer_norm(4)

        @block.vector
        def _(dve):
            at = [0]
            n = [0]

            def mark(ins):
                n[0] += 1
                ins.then_inc(dve_link, 1)
                return n[0]

            def link(ins):
                dve.wait_ge(dve_link, mark(ins))

            def split(s):
                dve.wait_ge(hi_ready, s + 1)
                raw_wait(dve, s)
                if s >= RING:
                    dve.wait_ge(chunk_used, s - RING + 1)
                dve.tensor_tensor(w_lo[:, s % RING], raw[:, s % RING], w_hi[:, s % RING].bitcast(F32), ALU.subtract
                                  ).then_inc(lo_ready, 1)

            def upto(s):
                while at[0] <= s:
                    split(at[0])
                    at[0] += 1

            def lo_of(p, hi, lo, hi_sem, value, ready):
                dve.wait_ge(hi_sem, value)
                dve.tensor_tensor(lo, quad[p][:, 0:lo.shape[1], :], hi.bitcast(F32), ALU.subtract).then_inc(ready, 1)

            def add_tile(layer, i, j):
                tile_done(dve, layer, i)
                Xj = X[:, :, j * N:(j + 1) * N]
                dve.tensor_tensor(Xj, gemm[(TILE0[layer] + i) % 2][:, :, :], Xj, ALU.add).then_inc(x_sum, 1)

            def tile_stats(j):
                for r in range(RT):
                    dve.bn_stats(stats[:, r, j, :], X[:, r, j * N:(j + 1) * N]).then_inc(dve_link, 1)
                n[0] += RT

            def x_piece_lo(which, i):
                k0, n_ = PIECES[i]
                lo_of(i % 2, x_hi[:, k0:k0 + n_, :], x_lo[:, k0:k0 + n_, :], xt_hi, NP * which + i + 1, xt_ready)

            def layer_norm(which):
                dve.wait_ge(dve_link, n[0])
                for r in range(RT):
                    k = mark(dve.bn_aggr(mv[:, r, :], stats[:, r, :, :]))
                dve.wait_ge(dve_link, k)
                dve.tensor_scalar(mv[:, :, 1], mv[:, :, 1], EPS, None, ALU.add).then_inc(var_ready, 1)
                dve.wait_ge(lnp_loaded, 32 * which)
                dve.wait_ge(rstd_ready, 2 + which)

                def gain(i, which=which):
                    k0, n_ = PIECES[i]
                    cols = slice(k0 * P, (k0 + n_) * P)
                    gb = lnp[:, 0, cols].unsqueeze(1).broadcast_to([P, RT, n_ * P])
                    bb = lnp[:, 1, cols].unsqueeze(1).broadcast_to([P, RT, n_ * P])
                    if i:
                        dve.wait_ge(xhat, RT * ((NP - 1) * (which - 1) + i))
                    link(dve.tensor_tensor(X[:, :, cols], X[:, :, cols], gb, ALU.mult))
                    dve.tensor_tensor(X[:, :, cols], X[:, :, cols], bb, ALU.add).then_inc(normed, 1)

                first = slice(0, PIECES[0][1] * P)
                for r in range(RT):
                    k = mark(dve.tensor_scalar(X[:, r, first], X[:, r, first], mv[:, r, 0:1], rstd[:, r, :],
                                               ALU.subtract, ALU.mult))
                dve.scalar_tensor_tensor(out=nbias[:, :], in0=mv[:, :, 0], scalar=-1.0, in1=rstd[:, :, 0],
                                         op0=ALU.mult, op1=ALU.mult).then_inc(nb_ready, 1)
                dve.wait_ge(dve_link, k)
                gain(0)
                gain(1)
                if which == 4:
                    for i in range(2, NP):
                        gain(i)
                    return
                x_piece_lo(which, 0)
                x_piece_lo(which, 1)
                gain(2)
                gain(3)
                x_piece_lo(which, 2)
                gain(4)
                x_piece_lo(which, 3)
                x_piece_lo(which, 4)

            x_piece_lo(0, 0)
            upto(0)
            x_piece_lo(0, 1)
            upto(1)
            x_piece_lo(0, 2)
            upto(3)
            x_piece_lo(0, 3)
            x_piece_lo(0, 4)
            upto(10)
            dve.wait_ge(pair_full[1], USE[1]["params"] + 1)
            dve.tensor_copy(cw, pair[1][:, 0:8 * 32].rearrange("p (c j) -> p c j", c=8)[:, :, 0:CONV_W]
                            ).then_inc(dve_link, 1)
            n[0] += 1
            dve.tensor_copy(small, pair[1][:, 8 * 32:8 * 32 + 40]).then_inc(params_ready, 1)
            dve.wait_ge(params_ready, 1)
            dve.wait_ge(consts, 2)
            link(dve.tensor_tensor(lb, lbl[:, 0, :], lbl[:, 1, :], ALU.max))
            k = mark(dve.tensor_tensor(lbl[:, 0, :], lbl[:, 0, :], lb, ALU.subtract))
            dve.tensor_tensor(lbl[:, 1, :], lbl[:, 1, :], lb, ALU.subtract).then_inc(lb_exp, 1)
            upto(13)
            dve.wait_ge(lb_exp, 2)
            link(dve.tensor_tensor(lb, lbl[:, 0, :], lbl[:, 1, :], ALU.add))
            link(dve.reciprocal(oml, lb))
            link(dve.tensor_tensor(lb, lbl[:, 0, :], oml, ALU.mult))
            dve.tensor_scalar(oml, lb, -1.0, 1.0, ALU.mult, ALU.add).then_inc(lb_ready, 1)

            def forget(half, s0):
                upto(s0 + 15)
                dve.wait_ge(k_ready, half + 1)
                dve.tensor_scalar(L, L, F_MIN, None, ALU.max).then_inc(f_ready, 1)
                upto(s0 + 17)
                dve.wait_ge(lnf_ready, half + 1)
                dve.tensor_tensor_scan(L, rstm[:, :], Dm, 0.0, ALU.mult, ALU.add).then_inc(L_ready, 1)

            def query(half, s0):
                upto(s0 + 13)
                dve.wait_ge(sig_ready, 2 * half + 2)
                dve.tensor_tensor(qT.rearrange("p h t -> p (h t)"), pair[0][:, :], Dm, ALU.mult
                                  ).then_inc(q_ready, 1)

            def diff(half, k):
                if k == 0:
                    dve.wait_ge(q_ready, half + 1)
                    dve.wait_ge(L_ready, half + 1)
                else:
                    dve.wait_ge(z_ready, 8 * half + k)
                if k < LEVELS:
                    h = CHUNK >> k
                    Lv = L.rearrange("p (g t) -> p g t", t=2 * h)
                    mid = Lv[:, :, h - 1:h].broadcast_to([P, HG * S // (2 * h), 2 * h])
                    dve.tensor_tensor(Dm.rearrange("p (g t) -> p g t", t=2 * h), Lv, mid, ALU.subtract
                                      ).then_inc(diff_ready, 1)
                else:
                    Lv = L.rearrange("p (h b t) -> p h b t", b=2, t=P)
                    Dv = Dm.rearrange("p (h b t) -> p h b t", b=2, t=P)
                    end = Lv[:, :, 0, P - 1:P].broadcast_to([P, HG, P])
                    k = mark(dve.tensor_tensor(Dv[:, :, 0, :], end, Lv[:, :, 0, :], ALU.subtract))
                    dve.tensor_copy(Dv[:, :, 1, :], Lv[:, :, 1, :]).then_inc(diff_ready, 1)

            def weigh(half, k):
                dve.wait_ge(exp_ready, 8 * half + k + 1)
                if 8 * half + k >= 2:
                    dve.wait_ge(pair_full[1], USE[1][("level", half, k - 2) if k >= 2 else ("level", 0, 6 + k)] + 1)
                h = CHUNK >> k if k < LEVELS else P
                z = Z[k % 2].rearrange("p (g u r) -> p g u r", u=2, r=h)
                e = Dm.rearrange("p (g u r) -> p g u r", u=2, r=h)
                kv = kT.rearrange("p h t -> p (h t)").rearrange("p (g u r) -> p g u r", u=2, r=h)
                qv = qT.rearrange("p h t -> p (h t)").rearrange("p (g u r) -> p g u r", u=2, r=h)
                dve.tensor_tensor(z[:, :, 0, :], e[:, :, 0, :], kv[:, :, 0, :], ALU.mult)
                dve.tensor_tensor(z[:, :, 1, :], e[:, :, 1, :], qv[:, :, 1, :], ALU.mult).then_inc(z_ready, 1)

            def take(half, k):
                dve.wait_ge(pair_full[1], USE[1]["level", half, k] + 1)
                if k == 0:
                    dve.wait_ge(scores_clear, half)
                Av = A.rearrange("p (b t) -> p b t", t=P)
                if k < LEVELS:
                    h = CHUNK >> k
                    o_ = A.rearrange("p (b g u r) -> p b g u r", b=2 * HG, u=2, r=h)[:, :, :, 1, :]
                    m_ = masks[:, k, :].rearrange("p (g r) -> p g r", r=h).unsqueeze(1).broadcast_to(
                        [P, 2 * HG, CHUNK // h, h])
                    d_ = pair[1][:, 0:N].rearrange("p (b g r) -> p b g r", b=2 * HG, r=h)
                    ins = dve.copy_predicated(o_, m_, d_)
                elif k == LEVELS:
                    ins = dve.tensor_copy(Ax, pair[1][:, 0:N])
                else:
                    ins = dve.copy_predicated(Av, imask[:, :].unsqueeze(1).broadcast_to([P, 2 * HG, P]),
                                              pair[1][:, :].rearrange("p (b t) -> p b t", t=P))
                ins.then_inc(scores_in, 1)

            def gates(half, i):
                dve.wait_ge(g_sig, half + 1)
                gv = G.rearrange("p (r n) -> p r n", r=RT)
                dve.tensor_tensor(gv, gv, gemm[(TILE0[0] + i) % 2][:, :, :], ALU.mult).then_inc(g_silu, 1)
                dve.wait_ge(g_silu, half + 1)
                link(dve.tensor_tensor(gv, gv, gn[:, half * N:(half + 1) * N].unsqueeze(1).broadcast_to([P, RT, N]),
                                       ALU.mult))

            def mean_square(half):
                dve.wait_ge(square_ready, half + 1)
                dve.tensor_scalar(ss, ss, 1.0 / DH, EPS, ALU.mult, ALU.add).then_inc(var_ready, 1)

            def norm_out(half):
                dve.wait_ge(rstd_ready, half + 1)
                ov = orow.rearrange("p (b v) -> p b v", v=DH)
                link(dve.tensor_tensor(ov, ov, ss.unsqueeze(2).broadcast_to([P, 2 * HG, DH]), ALU.mult))
                dve.tensor_tensor(orow, orow, G, ALU.mult).then_inc(o_ready, 1)

            def group_lo(k0, value):
                lo_of(0, c_hi[:, k0:k0 + 4, :], c_lo[:, k0:k0 + 4, :], cat_hi, value, cat_ready)

            tap_mark = {}
            taps = [0]

            def conv(count):
                for _ in range(count):
                    if taps[0] == 8 * CONV_W:
                        return
                    half, rest = divmod(taps[0], 4 * CONV_W)
                    j, c = divmod(rest, 4)
                    if rest == 0:
                        dve.wait_ge(pad_ready, half + 1)
                    ch = 4 * half + c
                    src = hpad[half][:, c, j:j + S]
                    if j == 0:
                        ins = dve.tensor_scalar(cv[:, ch, :], src, cw[:, ch, 0:1], cpar[:, 0, ch:ch + 1], ALU.mult, ALU.add)
                    else:
                        dve.wait_ge(dve_link, tap_mark[ch])
                        ins = dve.scalar_tensor_tensor(out=cv[:, ch, :], in0=src, scalar=cw[:, ch, j:j + 1],
                                                       in1=cv[:, ch, :], op0=ALU.mult, op1=ALU.add)
                    tap_mark[ch] = mark(ins)
                    taps[0] += 1
                    if taps[0] == 8 * CONV_W:
                        dve.wait_ge(dve_link, n[0])
                        dve.nop().then_inc(taps_done, 1)

            def gated(i, half):
                dve.wait_ge(gate_ready, half + 1)
                tile_done(dve, 0, i)
                if half == 1:
                    dve.wait_ge(pair_full[0], USE[0]["Q0"] + 1)
                dve.tensor_tensor(urow[1], gemm[(TILE0[0] + i) % 2][:, :, :], urow[0], ALU.mult
                                  ).then_inc(h_ready_row, 1)

            for s in range(14, SLOT_MLP[0]):
                upto(s)
                for half, k in ((0, s - 38), (1, s - 88)):
                    if k >= 0 and k % 2 == 0 and k // 2 <= 10:
                        k //= 2
                        if 1 <= k <= 8:
                            weigh(half, k - 1)
                        if k <= 7:
                            diff(half, k)
                        if 2 <= k:
                            take(half, k - 2)
                if s == 19:
                    gated(1, 0)
                if s == 31:
                    forget(0, 16)
                if s == 37:
                    query(0, 24)
                if s == 51:
                    gated(5, 1)
                if s == 65:
                    mean_square(0)
                if s == 67:
                    gates(0, 7)
                if s == 68:
                    norm_out(0)
                if s == 71:
                    group_lo(8, 1)
                if s == 79:
                    forget(1, 64)
                if s == 85:
                    query(1, 72)
                if s == 93:
                    conv(8 * CONV_W)
                    dve.wait_ge(pair_full[0], USE[0]["mean"] + 1)
                    dve.tensor_tensor(cv, cv, pair[0][:, 0:S].unsqueeze(1).broadcast_to([P, 8, S]), ALU.subtract
                                      ).then_inc(cen_ready, 1)
                if s == 97:
                    dve.wait_ge(pair_full[0], USE[0]["variance"] + 1)
                    dve.tensor_scalar(cvar, pair[0][:, 0:S], EPS, None, ALU.add).then_inc(cvar_ready, 1)
                if s == 98:
                    dve.wait_ge(croot_ready, 1)
                    link(dve.tensor_tensor(cvar, cvar, crs, ALU.mult))
                    link(dve.tensor_tensor(cvar, cvar, crs, ALU.mult))
                    link(dve.tensor_scalar(cvar, cvar, -0.5, 1.5, ALU.mult, ALU.add))
                    link(dve.tensor_tensor(crs, crs, cvar, ALU.mult))
                    dve.tensor_tensor(cv, cv, crs.unsqueeze(1).broadcast_to([P, 8, S]), ALU.mult).then_inc(cn_ready, 1)
                if s == 99:
                    gates(1, 11)
                if s == 100:
                    dve.wait_ge(csig_ready, 1)
                    dve.tensor_tensor(cv, cv, csq, ALU.mult).then_inc(conv_ready, 1)
                if s == 101:
                    dve.wait_ge(cat_hi, 2)
                    dve.tensor_tensor(c_lo[:, 0:8, :], cv, c_hi[:, 0:8, :].bitcast(F32), ALU.subtract
                                      ).then_inc(cat_ready, 1)
                if s == 113:
                    mean_square(1)
                if s == 114:
                    norm_out(1)
                if s == 118:
                    group_lo(12, 3)
                if 23 <= s < 93:
                    conv(1 if 38 <= s <= 58 and s % 2 == 0 else 2 if 38 <= s <= 58 else 5)
                for j in range(NT):
                    if s == 96 + OUT_A * j + OUT_A - 1 + RING:
                        if j == 0:
                            dve.wait_ge(x_scaled, 1)
                        add_tile(0, 12 + j, j)

            def second_part(layer):
                o = SLOT0[layer] + IN_SLOTS + NT * OUT_A
                for j in range(NT):
                    upto(o + OUT_B * j + OUT_B - 1 + RING)
                    add_tile(layer, 12 + NT + j, j)
                    dve.wait_ge(x_sum, x_sums[0] + NT + j + 1)
                    tile_stats(j)
                x_sums[0] += 2 * NT

            x_sums = [0]
            second_part(0)

            def mlp_tile(layer, b, i, last=False):
                base, tbase = SLOT_MLP[layer], TILE_MLP[layer]
                first = base + i * CPT + RING
                for c in range(CPT):
                    s = first + c
                    if last and b * (2 * NT * CPT) + s >= SLOTS:
                        break
                    dve.wait_ge(hi_ready, b * (2 * NT * CPT) + (s + 1))
                    dve.wait_ge(raw_full[s % RING], b * (16 * 2 * NT * CPT // RING) + 16 * (s // RING + 1))
                    dve.wait_ge(chunk_used, b * (2 * NT * CPT) + (s - RING + 1))
                    dve.tensor_tensor(w_lo[:, s % RING], raw[:, s % RING], w_hi[:, s % RING].bitcast(F32), ALU.subtract
                                      ).then_inc(lo_ready, 1)
                    if c == 1 and 1 <= i <= NT:
                        dve.wait_ge(h_hi, b * NT + (layer * NT * FB + i))
                        dve.tensor_tensor(c_lo[:, 4 * (i - 1):4 * i, :], quad[0],
                                          c_hi[:, 4 * (i - 1):4 * i, :].bitcast(F32), ALU.subtract
                                          ).then_inc(h_ready, 1)
                if i >= NT:
                    j, t = i - NT, tbase + i
                    if j == 0:
                        dve.wait_ge(x_scaled, 2 + 2 * layer)
                    dve.wait_ge(chunk_used, b * (2 * NT * CPT) + (base + (i + 1) * CPT))
                    Xj = X[:, :, j * N:(j + 1) * N]
                    dve.tensor_tensor(Xj, gemm[t % 2][:, :, :], Xj, ALU.add).then_inc(x_sum, 1)
                    dve.wait_ge(x_sum, b * NT + (x_sums[0] + j + 1))
                    for r in range(RT):
                        dve.bn_stats(stats[:, r, j, :], X[:, r, j * N:(j + 1) * N]).then_inc(dve_link, 1)

            def mlp(layer):
                whole = FB if layer == 0 else FB - 1
                with dve.Fori(0, whole) as b:
                    for i in range(2 * NT):
                        mlp_tile(layer, b, i)
                if layer == 1:
                    for i in range(2 * NT):
                        mlp_tile(layer, whole, i, last=True)
                n[0] += RT * NT * FB
                x_sums[0] += NT * FB
                at[0] = SLOT_MLP[layer] + MLP_SLOTS + RING

            layer_norm(1)
            mlp(0)
            layer_norm(2)

            o = SLOT0[1]
            dve.wait_ge(wf_hi_ready, 1)
            dve.tensor_tensor(wf_lo[:, :], wf, wf_hi[:, :].bitcast(F32), ALU.subtract).then_inc(wf_ready, 1)

            def forget_bias(g):
                dve.wait_ge(pair_full[1], USE[1]["F", g] + 1)
                for q in range(RT):
                    width = (q + 1) * P
                    for h in range(HG):
                        o_ = fbias[:, q * HG * P + h * width:q * HG * P + (h + 1) * width]
                        ins = dve.scalar_tensor_tensor(out=o_, in0=tri[:, S - width:S],
                                                       scalar=Fc[:, q * HEADS + HG * g + h:q * HEADS + HG * g + h + 1],
                                                       in1=quad[1][:, h, 0:width], op0=ALU.add, op1=ALU.subtract)
                        ins.then_inc(fb_ready, 1)

            def softmax_in(g):
                dve.wait_ge(pair_full[0], USE[0]["scores", g] + 1)
                dve.wait_ge(pair_full[1], USE[1]["scores", g] + 1)
                if g < 2:
                    dve.wait_ge(fb_ready, RT * HG * (g + 1))
                for q in range(RT):
                    width = (q + 1) * P
                    o_ = sm[:, q * HG * P:q * HG * P + HG * width].rearrange("p (h k) -> p h k", h=HG)
                    src = (pair[0][:, 0:N], pair[1][:, :])[q].rearrange("p (h k) -> p h k", h=HG)
                    if g < 2:
                        bias = fbias[:, q * HG * P:q * HG * P + HG * width].rearrange("p (h k) -> p h k", h=HG)
                    else:
                        last = P * q + 2 * CHUNK - 1
                        lo = last - width
                        heads = rel[:, HG * (g - 2):HG * (g - 1), :]
                        bias = heads[:, :, last::-1] if lo < 0 else heads[:, :, last:lo:-1]
                    dve.scalar_tensor_tensor(out=o_, in0=src, scalar=SCALE, in1=bias, op0=ALU.mult, op1=ALU.add
                                             ).then_inc(scores_read, 1)
                    dve.wait_ge(scores_read, 2 * g + q + 1)
                    link(dve.tensor_reduce(mx[:, q * HG:(q + 1) * HG], o_, AX.X, ALU.max))
                dve.tensor_scalar(mx, mx, -1.0, None, ALU.mult).then_inc(max_ready, 1)

            def softmax_out(g):
                dve.wait_ge(prob_exp, g + 1)
                link(dve.reciprocal(rs, sums))
                for q in range(RT):
                    width = (q + 1) * P
                    v = sm[:, q * HG * P:q * HG * P + HG * width].rearrange("p (h k) -> p h k", h=HG)
                    ins = dve.tensor_tensor(v, v, rs[:, q * HG:(q + 1) * HG].unsqueeze(2).broadcast_to([P, HG, width]),
                                            ALU.mult)
                ins.then_inc(prob_ready, 1)

            for g in range(4):
                s0 = o + 24 * g
                if g:
                    upto(s0 + 6)
                    lo_of(0, c_hi[:, 4 * (g - 1):4 * g, :], c_lo[:, 4 * (g - 1):4 * g, :], cat_hi, 3 + g, cat_ready)
                if g == 0:
                    upto(s0 + 12)
                    dve.wait_ge(pair_full[1], USE[1]["logits"] + 1)
                    dve.tensor_scalar(zf[0:HEADS, :], pair[1][0:HEADS, 0:S], bf[0:HEADS, :], None, ALU.add
                                      ).then_inc(z_sum, 1)
                    dve.wait_ge(z_sum, 1)
                    dve.scalar_tensor_tensor(out=za[0:HEADS, :], in0=zf[0:HEADS, :], scalar=-1.0, in1=zf[0:HEADS, :],
                                             op0=ALU.mult, op1=ALU.max).then_inc(za_ready, 1)
                    upto(s0 + 13)
                    dve.wait_ge(zl_ready, 1)
                    link(dve.scalar_tensor_tensor(out=ls[0:HEADS, :], in0=zf[0:HEADS, :], scalar=0.0,
                                                  in1=za[0:HEADS, :], op0=ALU.min, op1=ALU.subtract))
                    dve.tensor_tensor_scan(Ft[0:HEADS, :], ones[0:HEADS, :], ls[0:HEADS, :], 0.0, ALU.mult, ALU.add
                                           ).then_inc(F_ready, 1)
                    upto(s0 + 16)
                    dve.wait_ge(pair_full[1], USE[1]["F rows"] + 1)
                    dve.tensor_copy(Fc, pair[1][:, 0:RT * HEADS]).then_inc(Fc_ready, 1)
                    dve.wait_ge(Fc_ready, 1)
                    upto(s0 + 18)
                    forget_bias(0)
                if g == 1:
                    upto(s0 + 14)
                    forget_bias(1)
                upto(s0 + 24)
                softmax_in(g)
                upto(s0 + 26)
                softmax_out(g)
                upto(s0 + 28)
                dve.wait_ge(pair_full[1], USE[1]["probs", g] + 1)
                dve.tensor_copy(pT[:, HG * S:], pair[1][:, 0:N]).then_inc(pT_dve, 1)
            upto(o + 102)
            lo_of(0, c_hi[:, 12:16, :], c_lo[:, 12:16, :], cat_hi, 7, cat_ready)
            for j in range(NT):
                upto(o + 96 + OUT_A * j + OUT_A - 1 + RING)
                if j == 0:
                    dve.wait_ge(x_scaled, 3)
                add_tile(1, 12 + j, j)
            second_part(1)
            layer_norm(3)
            mlp(1)
            layer_norm(4)

        @block.tensor
        def _(pe):
            def products(acc, hi, lo, k, c, slot, first, last):
                for r in range(RT):
                    rows = slice(r * P, (r + 1) * P)
                    pe.matmul(acc[:, r, :], hi[:, k, rows], w_hi[:, slot, c, :], start=first, stop=False)
                    pe.matmul(acc[:, r, :], hi[:, k, rows], w_lo[:, slot, c, :], start=False, stop=False)
                    ins = pe.matmul(acc[:, r, :], lo[:, k, rows], w_hi[:, slot, c, :], start=False, stop=last)
                return ins

            def chunk(acc, act_, ks, s, first, last):
                pe.wait_ge(lo_ready, s + 1)
                for c, k in enumerate(ks):
                    ins = products(acc, act_[0], act_[1], k, c, s % RING, first and c == 0, last and c == CK - 1)
                ins.then_inc(chunk_used, 1)
                return ins

            tile_out = [[(gate_ready, 1), (h_ready_row, 1), (row_ready, 1), (row_ready, 2), (gate_ready, 2),
                         (h_ready_row, 2), (row_ready, 3), (g_silu, 1), (row_ready, 4), (row_ready, 5), (row_ready, 6),
                         (g_silu, 2)] + [(x_sum, j + 1) for j in range(2 * NT)],
                        [(row_ready, 7 + i) for i in range(12)] +
                        [(x_sum, 2 * NT + FB * NT + j + 1) for j in range(2 * NT)]]
            read_out = [
                {"C0": (pad_ready, 1), "F0": (sig_ready, 1), "Q0": (q_ready, 1), "C1": (pad_ready, 2),
                 "O0": (cat_ready, 1), "F1": (sig_ready, 3), "Q1": (q_ready, 2), "mean": (cen_ready, 1),
                 "variance": (cvar_ready, 1), "O1": (cat_ready, 3)},
                {"params": (params_ready, 1), "logits": (z_sum, 1), "F rows": (Fc_ready, 1)},
            ]
            for p in range(2):
                for which in range(4):
                    for name in pieces(which, p):
                        read_out[p][name] = (xt_ready, NP * which + name[2] + 1)
            for layer in range(DEPTH):
                for name in HIDDEN[layer]:
                    read_out[0][name] = (h_ready, FB * NT * layer + name[2] + 1)
            for g in range(4):
                read_out[0].update({("q", g): (qk_ready, 2 * g + 1), ("k", g): (qk_ready, 2 * g + 2),
                                    ("scores", g): (scores_read, 2 * g + 1), ("probs", g): (pT_act, g + 1),
                                    ("out", g): (cat_ready, 4 + g)})
                read_out[1].update({("scores", g): (scores_read, 2 * g + 2), ("probs", g): (pT_dve, g + 1)})
            for half in range(2):
                read_out[1]["F", half] = (fb_ready, RT * HG * (half + 1))
                for k in range(9):
                    read_out[1]["level", half, k] = (scores_in, 9 * half + k + 1)
                read_out[1]["level", half, 9] = (o_row, half + 1)
            pair_out = [[read_out[p][name] for name in USE[p]] for p in range(2)]

            def acquire(layer, i):
                if i >= 2:
                    pe.wait_ge(*tile_out[layer][i - 2])
                elif layer:
                    pe.wait_ge(x_sum, 2 * NT + NT * FB - 1 + i)
                return gemm[(TILE0[layer] + i) % 2]

            def pair_free(p, name):
                use = USE[p][name]
                if use:
                    pe.wait_ge(*pair_out[p][use - 1])

            def transposes(p, name, src, count=4):
                pair_free(p, name)
                for c in range(count):
                    for r in range(RT):
                        ins = pe.transpose(quad[p][:, c, r * P:(r + 1) * P], src[:, r, c * P:(c + 1) * P], ident[:, :])
                ins.then_inc(pair_full[p], 1)

            def x_piece(which, i):
                k0, n_ = PIECES[i]
                if which:
                    pe.wait_ge(normed, NP * (which - 1) + i + 1)
                else:
                    pe.wait_ge(x_loaded[k0 * P // N], 16)
                transposes(i % 2, ("x", which, i), X[:, :, k0 * P:(k0 + n_) * P], n_)

            def start_tile(which, c):
                if c == 0:
                    x_piece(which, 0)
                    x_piece(which, 1)
                    pe.wait_ge(xt_ready, NP * which + 1)
                if c == 1:
                    x_piece(which, 2)
                    pe.wait_ge(xt_ready, NP * which + 2)
                if c == 2:
                    pe.wait_ge(xt_ready, NP * which + 3)
                if c == 3:
                    x_piece(which, 3)
                if c == 4:
                    x_piece(which, 4)
                    pe.wait_ge(xt_ready, NP * which + 4)
                if c == 6:
                    pe.wait_ge(xt_ready, NP * which + 5)

            X_ = (x_hi, x_lo)
            C_ = (c_hi, c_lo)
            at = [0, 0]

            def rows_to(p, name, src, count):
                pe.wait_ge(row_ready, count)
                transposes(p, name, src)

            def level(half, k):
                pair_free(1, ("level", half, k))
                if k < 8:
                    pe.wait_ge(z_ready, 8 * half + k + 1)
                if k < LEVELS:
                    h = CHUNK >> k
                    z = Z[k % 2].rearrange("p (b t) -> p b t", t=P)
                    for b in range(2 * HG):
                        q = z[:, b, :].rearrange("p (g u r) -> p g u r", u=2, r=h)[:, :, 1, :]
                        ins = pe.matmul(pair[1][:, b * CHUNK:(b + 1) * CHUNK], z[:, b, :], q, start=True, stop=True)
                elif k == LEVELS:
                    z = Z[1].rearrange("p (h b t) -> p h b t", b=2, t=P)
                    for h in range(HG):
                        ins = pe.matmul(pair[1][:, h * P:(h + 1) * P], z[:, h, 0, :], z[:, h, 1, :], start=True, stop=True)
                else:
                    for b in range(2 * HG):
                        cols = slice((b % 2) * P, (b % 2) * P + P)
                        ins = pe.matmul(pair[1][:, b * P:(b + 1) * P], kT[:, b // 2, cols], qT[:, b // 2, cols],
                                        start=True, stop=True)
                ins.then_inc(pair_full[1], 1)

            def outputs(half, rows):
                pair_free(1, ("level", half, 9))
                pe.wait_ge(row_ready, rows)
                av = A.rearrange("p (h b t) -> p h b t", b=2, t=P)
                axv = Ax.rearrange("p (h t) -> p h t", t=P)
                for h in range(HG):
                    cols = slice(h * DH, (h + 1) * DH)
                    pe.matmul(pair[1][:, cols], av[:, h, 0, :], vrow[:, 0, cols], start=True, stop=True)
                for h in range(HG):
                    cols = slice(h * DH, (h + 1) * DH)
                    o_ = pair[1][:, N + h * DH:N + (h + 1) * DH]
                    pe.matmul(o_, axv[:, h, :], vrow[:, 0, cols], start=True, stop=False)
                    ins = pe.matmul(o_, av[:, h, 1, :], vrow[:, 1, cols], start=False, stop=True)
                ins.then_inc(pair_full[1], 1)

            def behind_even(s):
                if s == 7:
                    pe.wait_ge(const_loaded, 16 * 6)
                    pair_free(1, "params")
                    for c in range(8):
                        pe.transpose(pair[1][:, 32 * c:32 * c + CONV_W], cw_rows[0:CONV_W, c * P:(c + 1) * P],
                                     ident[0:CONV_W, 0:CONV_W])
                    pe.transpose(pair[1][:, 8 * 32:8 * 32 + 40], small_rows[0:40, :], ident[0:40, 0:40]
                                 ).then_inc(pair_full[1], 1)
                if s == 18:
                    pe.wait_ge(h_ready_row, 1)
                    transposes(0, "C0", urow[1])
                if s == 25:
                    rows_to(0, "F0", urow[0], 1)
                if s == 33:
                    rows_to(0, "Q0", urow[1], 2)
                if s == 50:
                    pe.wait_ge(h_ready_row, 2)
                    transposes(0, "C1", urow[1])
                if s == 67:
                    pe.wait_ge(o_ready, 1)
                    transposes(0, "O0", orow.rearrange("p (r n) -> p r n", r=RT))
                if s == 73:
                    rows_to(0, "F1", urow[0], 4)
                if s == 81:
                    rows_to(0, "Q1", urow[1], 5)
                for half, base in ((0, 38), (1, 88)):
                    k = s - base
                    if 0 <= k <= 16 and k % 2 == 0:
                        level(half, k // 2)
                if s == 60:
                    outputs(0, 3)
                if s == 108:
                    outputs(1, 6)
                if s in (90, 94):
                    name = "mean" if s == 90 else "variance"
                    pe.wait_ge(taps_done, 1)
                    if s == 94:
                        pe.wait_ge(csq_ready, 1)
                    pair_free(0, name)
                    src = cv if s == 90 else csq
                    for c in range(8):
                        ins = pe.matmul(pair[0][:, 0:S], meanw, src[:, c, :], start=(c == 0), stop=(c == 7))
                    ins.then_inc(pair_full[0], 1)
                if s == 115:
                    pe.wait_ge(o_ready, 2)
                    transposes(0, "O1", orow.rearrange("p (r n) -> p r n", r=RT))

            def forget_logits():
                pe.wait_ge(wf_ready, 1)
                pair_free(1, "logits")
                o_ = pair[1][:, 0:S]
                for k in range(KT):
                    cols = slice(k * HEADS, k * HEADS + P)
                    pe.matmul(o_, wf_hi[:, cols], x_hi[:, k, :], start=(k == 0), stop=False)
                    pe.matmul(o_, wf_hi[:, cols], x_lo[:, k, :], start=False, stop=False)
                    ins = pe.matmul(o_, wf_lo[:, cols], x_hi[:, k, :], start=False, stop=(k == KT - 1))
                ins.then_inc(pair_full[1], 1)

            def forget_rows():
                pe.wait_ge(F_ready, 1)
                pair_free(1, "F rows")
                for r in range(RT):
                    ins = pe.transpose(pair[1][:, r * HEADS:(r + 1) * HEADS], Ft[0:HEADS, r * P:(r + 1) * P],
                                       ident[0:HEADS, 0:HEADS])
                ins.then_inc(pair_full[1], 1)

            def forget_columns(g):
                pe.wait_ge(odd_consts, 2)
                pair_free(1, ("F", g))
                for h in range(HG):
                    ins = pe.matmul(quad[1][:, h, :], sel[0:HEADS, HG * g + h, :], Ft[0:HEADS, :], start=True, stop=True)
                ins.then_inc(pair_full[1], 1)

            def scores(g):
                pe.wait_ge(qk_ready, 2 * g + 2)
                pair_free(0, ("scores", g))
                pair_free(1, ("scores", g))
                for h in range(HG):
                    ins = pe.matmul(pair[0][:, h * P:(h + 1) * P], qT[:, h, 0:P], kT[:, h, 0:P], start=True, stop=True)
                ins.then_inc(pair_full[0], 1)
                for h in range(HG):
                    ins = pe.matmul(quad[1][:, h, :], qT[:, h, P:S], kT[:, h, :], start=True, stop=True)
                ins.then_inc(pair_full[1], 1)

            def probs(g):
                pe.wait_ge(prob_ready, g + 1)
                pair_free(0, ("probs", g))
                pair_free(1, ("probs", g))
                p1 = sm[:, HG * P:].rearrange("p (h k) -> p h k", h=HG)
                for h in range(HG):
                    pe.transpose(quad[0][:, h, 0:P], sm[:, h * P:(h + 1) * P], ident[:, :])
                    ins = pe.transpose(quad[0][:, h, P:S], p1[:, h, 0:P], ident[:, :])
                ins.then_inc(pair_full[0], 1)
                for h in range(HG):
                    ins = pe.transpose(pair[1][:, h * P:(h + 1) * P], p1[:, h, P:S], ident[:, :])
                ins.then_inc(pair_full[1], 1)

            def attend(g):
                pe.wait_ge(pT_act, g + 1)
                pe.wait_ge(pT_dve, g + 1)
                pe.wait_ge(row_ready, 6 + 3 * g + 3)
                pair_free(0, ("out", g))
                a = pT[:, 0:HG * S].rearrange("p (h q) -> p h q", h=HG)
                b = pT[:, HG * S:].rearrange("p (h q) -> p h q", h=HG)
                for h in range(HG):
                    cols = slice(h * DH, (h + 1) * DH)
                    pe.matmul(quad[0][:, h, :], vrow[:, 0, cols], a[:, h, :], start=True, stop=False,
                              skip_group_check=True)
                    ins = pe.matmul(quad[0][:, h, P:S], vrow[:, 1, cols], b[:, h, :], start=False, stop=True,
                                    skip_group_check=True)
                ins.then_inc(pair_full[0], 1)

            def behind_odd(s):
                for g in range(4):
                    r = s - 24 * g
                    if r == 9:
                        rows_to(0, ("q", g), urow[0], 6 + 3 * g + 1)
                        if g == 1:
                            forget_columns(1)
                    if r == 17:
                        rows_to(0, ("k", g), urow[1], 6 + 3 * g + 2)
                    if r == 20:
                        scores(g)
                    if r == 24:
                        probs(g)
                    if r == 26:
                        attend(g)
                if s == 8:
                    forget_logits()
                if s == 12:
                    forget_rows()
                if s == 14:
                    forget_columns(0)

            pe.wait_ge(consts, 1)
            groups = [{8: 1, 0: 2, 12: 3}, {0: 4, 4: 5, 8: 6, 12: 7}]
            for layer in range(DEPTH):
                behind = (behind_even, behind_odd)[layer]
                s0 = SLOT0[layer]
                for i in range(12):
                    s, t = at
                    acc = acquire(layer, i)
                    for c in range(CPT):
                        if i == 0:
                            start_tile(2 * layer, c)
                        ins = chunk(acc, X_, (CK * c, CK * c + 1), s + c, c == 0, c == CPT - 1)
                        behind(s + c - s0)
                    at[0], at[1] = s + CPT, t + 1
                for part in (EVEN_OUT, ODD_OUT)[layer]:
                    for j in range(NT):
                        s, t = at
                        acc = acquire(layer, t - TILE0[layer])
                        for i, k in enumerate(part[::CK]):
                            if j == 0 and k in groups[layer]:
                                pe.wait_ge(cat_ready, groups[layer][k])
                            ins = chunk(acc, C_, (k, k + 1), s + i, i == 0, i == len(part) // CK - 1)
                            behind(s + i - s0)
                        at[0], at[1] = s + len(part) // CK, t + 1

                base, tbase = SLOT_MLP[layer], TILE_MLP[layer]
                assert at == [base, tbase]

                def mlp_tile(b, i, first_block=False):
                    start = first_block and i == 0
                    t = tbase + i
                    acc = gemm[t % 2]
                    j = (i - 2) % (2 * NT)
                    if j < NT:
                        pe.wait_ge(relu_done, b * NT + (layer * FB * NT + j + 1))
                    else:
                        pe.wait_ge(x_sum, b * NT + (2 * NT * (layer + 1) + FB * NT * layer + j - NT + 1 - NT * (i < 2)))
                    operand = X_ if i < NT else C_
                    for c in range(CPT):
                        s = base + i * CPT + c
                        if start:
                            start_tile(2 * layer + 1, c)
                        if i == NT and c % 2 == 0:
                            pe.wait_ge(h_ready, b * NT + (layer * FB * NT + c // 2 + 1))
                        pe.wait_ge(lo_ready, b * (2 * NT * CPT) + (s + 1))
                        for kk in range(CK):
                            ins = products(acc, operand[0], operand[1], CK * c + kk, kk, s % RING,
                                           c == 0 and kk == 0, c == CPT - 1 and kk == CK - 1)
                        ins.then_inc(chunk_used, 1)
                        if c == 1 and 1 <= i <= NT:
                            pe.wait_ge(h_row, b * NT + (layer * FB * NT + i))
                            if i == 1 and first_block:
                                pair_free(0, ("h", layer, 0))
                            else:
                                pe.wait_ge(h_ready, b * NT + (layer * FB * NT + i - 1))
                            for cc in range(4):
                                for r in range(RT):
                                    ins = pe.transpose(quad[0][:, cc, r * P:(r + 1) * P],
                                                       urow[(i - 1) % 2][:, r, cc * P:(cc + 1) * P], ident[:, :])
                            ins.then_inc(pair_full[0], 1)

                for i in range(2 * NT):
                    mlp_tile(0, i, first_block=True)
                with pe.Fori(1, FB) as b:
                    for i in range(2 * NT):
                        mlp_tile(b, i)
                at[0], at[1] = base + MLP_SLOTS, tbase + MLP_TILES


_INS = ["x", "ev_w_in", "ev_conv_w", "ev_conv_b", "ev_conv_ln_g", "ev_conv_ln_b", "hgrn_lb_logits", "ev_gnorm_g",
        "ev_w_out", "od_w_in", "fox_b_f", "rel_bias", "od_w_out", "ln_mix_g", "ln_mix_b", "mlp_w1", "mlp_w2",
        "ln_mlp_g", "ln_mlp_b"]


def kernel(**inputs):
    import numpy as np
    import concourse.bacc as bacc
    from concourse.bass_utils import run_bass_kernel_spmd

    nc = bacc.Bacc("TRN2", target_bir_lowering=False, num_devices=1)
    arrays, args = {}, []
    for name in _INS:
        a = np.ascontiguousarray(inputs[name])
        arrays[f"in_{name}"] = a
        args.append(nc.dram_tensor(f"in_{name}", a.shape, mybir.dt.from_np(a.dtype), kind="ExternalInput").ap())
    args.append(nc.dram_tensor("out_0", (1, S, D), F32, kind="ExternalOutput").ap())
    trunk(nc, *args)
    r = run_bass_kernel_spmd(nc, [arrays], core_ids=[0])
    return r.results[0]["out_0"]
```

```python
from contextlib import ExitStack

import concourse.bass as bass
from concourse import mybir

F32, F32R, I8 = mybir.dt.float32, mybir.dt.float32r, mybir.dt.int8
ACT, ALU, AX = mybir.ActivationFunctionType, mybir.AluOpType, mybir.AxisListType

D = 2048
S = 256
P = 128
RT = S // P
KT = D // P
N = 512
CK = 2
CPT = KT // CK
DEPTH = 2
ALPHA = float((2 * DEPTH) ** 0.25)
EPS = 1e-5
CONV_CH, CONV_W = D // 2, 31
HEADS, DH = 8, 128
HG = 4
KDIM = HEADS * DH
REL_TABLE = 320
CHUNK = 64
D_FF = 4 * D
FB = D_FF // D
SCALE = float(DH) ** -0.5
NEG = -3.0e38
LEVELS = 7
F_MIN = 2.0 ** -63

F_COL, Q_COL, I_COL, G_COL = 2 * CONV_CH + KDIM, 2 * CONV_CH, 2 * CONV_CH + 2 * KDIM, 2 * CONV_CH + 3 * KDIM
EVEN_TILES = [CONV_CH, 0, F_COL, Q_COL, CONV_CH + N, N, I_COL, G_COL,
              F_COL + N, Q_COL + N, I_COL + N, G_COL + N]
FOX_F = 3 * KDIM
ODD_TILES = [base + third * KDIM for base in (0, N, FOX_F + HEADS, FOX_F + HEADS + N) for third in range(3)]
FORGET_SLOT, LEVEL_SLOT, OUT_SLOT = (16, 64), (39, 90), (71, 120)
MEAN_SLOT, CONV_LO_SLOT = 93, 104


def taps_behind(s):
    return 2 if LEVEL_SLOT[0] <= s <= LEVEL_SLOT[0] + 20 else 4 + (s % 4 == 0)


EVEN_OUT = [[8, 9, 10, 11], list(range(8)), [12, 13, 14, 15]]
ODD_OUT = [list(range(4)), list(range(4, 12)), list(range(12, 16))]
PART_CHUNKS = [len(part) // CK for part in EVEN_OUT]
PARTS = len(PART_CHUNKS)
NT = D // N
IN_SLOTS = 12 * CPT
PART_SLOT = [IN_SLOTS + NT * sum(PART_CHUNKS[:q]) for q in range(PARTS)]
LAYER_SLOTS = IN_SLOTS + NT * KT // CK
MLP_SLOTS = FB * 2 * NT * CPT
LAYER_TILES, MLP_TILES = 12 + PARTS * NT, FB * 2 * NT
SLOT0 = [0, LAYER_SLOTS + MLP_SLOTS]
SLOT_MLP = [LAYER_SLOTS, 2 * LAYER_SLOTS + MLP_SLOTS]
TILE0 = [0, LAYER_TILES + MLP_TILES]
TILE_MLP = [LAYER_TILES, 2 * LAYER_TILES + MLP_TILES]
SLOTS = 2 * (LAYER_SLOTS + MLP_SLOTS)
RING = 4
PIECES = [(0, 2), (2, 2), (4, 4), (8, 4), (12, 4)]
NP = len(PIECES)
X_BEFORE = [0, 1, 2, 3, 5]
LAST_PIECES = [(0, 2), (2, 4), (6, 4), (10, 4), (14, 2)]


def pieces_of(which):
    return LAST_PIECES if which == 4 else PIECES


def numbered(*names):
    return {name: i for i, name in enumerate(names)}


def pieces(which, p):
    return [("x", which, i) for i in range(p, NP, 2)]


HIDDEN = [[("h", layer, i) for i in range(FB * NT)] for layer in range(DEPTH)]
USE = [numbered(*pieces(0, 0), "C0", "F0", "Q0", "C1", "O0", "F1", "Q1", "mean", "variance", "O1",
                *pieces(1, 0), *HIDDEN[0], *pieces(2, 0),
                *[(name, g) for g in range(4) for name in ("q", "k", "scores", "probs", "out")],
                *pieces(3, 0), *HIDDEN[1]),
       numbered(*pieces(0, 1), "params", *[("level", half, k) for half in range(2) for k in range(10)],
                *pieces(1, 1), *pieces(2, 1), "logits", "F rows", ("F", 0), ("scores", 0), ("probs", 0), ("F", 1),
                *[(name, g) for g in range(1, 4) for name in ("scores", "probs")], *pieces(3, 1))]


def trunk(nc, x, ev_w_in, ev_conv_w, ev_conv_b, ev_conv_ln_g, ev_conv_ln_b, hgrn_lb_logits, ev_gnorm_g, ev_w_out,
          od_w_in, fox_b_f, rel_bias, od_w_out, ln_mix_g, ln_mix_b, mlp_w1, mlp_w2, ln_mlp_g, ln_mlp_b, out):
    w_in, w_out = [ev_w_in[0], od_w_in[0]], [ev_w_out[0], od_w_out[0]]
    with ExitStack() as ctx:
        def sb(name, shape, dt):
            return ctx.enter_context(nc.sbuf_tensor(name, shape, dt))

        def sem(name):
            return ctx.enter_context(nc.semaphore(name))

        raw = sb("raw", [P, RING, CK, N], F32)
        w_hi = sb("w_hi", [P, RING, CK, N], F32R)
        w_lo = sb("w_lo", [P, RING, CK, N], F32R)
        x_hi = sb("x_hi", [P, KT, S], F32R)
        x_lo = sb("x_lo", [P, KT, S], F32R)
        c_hi = sb("c_hi", [P, KT, S], F32R)
        c_lo = sb("c_lo", [P, KT, S], F32R)
        X = sb("X", [P, RT, D], F32)
        lnp = sb("lnp", [P, 2, D], F32)
        ident = sb("ident", [P, P], F32)
        stats = sb("stats", [P, RT, NT, 6], F32)
        mv = sb("mv", [P, RT, 2], F32)
        rstd = sb("rstd", [P, RT, 1], F32)
        mhalf = sb("mhalf", [P, RT * HG], F32)
        factor = sb("factor", [P, FB], F32)
        nbias = sb("nbias", [P, RT], F32)
        scr = sb("scr", [P, 14800], F32)
        used = [0]

        def cut(n):
            used[0] += n
            assert used[0] <= 14800, used[0]
            return scr[:, used[0] - n:used[0]]

        urow = [cut(RT * N).rearrange("p (r n) -> p r n", r=RT) for _ in range(2)]
        qT = cut(HG * S).rearrange("p (h t) -> p h t", h=HG)
        kT = cut(HG * S).rearrange("p (h t) -> p h t", h=HG)
        vrow = cut(RT * N).rearrange("p (r n) -> p r n", r=RT)
        both = used[0]
        L = cut(HG * S)
        Dm = cut(HG * S)
        Z = [cut(HG * S) for _ in range(2)]
        A = cut(HG * RT * P)
        Ax = cut(HG * P)
        G = cut(RT * N)
        PADW = CONV_W - 1 + S
        hpad = [cut(4 * PADW).rearrange("p (c t) -> p c t", c=4) for _ in range(2)]
        cw = cut(8 * CONV_W).rearrange("p (c j) -> p c j", c=8)
        small = cut(40)
        cpar = small[:, 0:24].rearrange("p (w c) -> p w c", w=3)
        lbl = small[:, 24:40].rearrange("p (w h) -> p w h", w=2)
        cw_rows, small_rows = Z[0], L[:, 0:P]
        lb = cut(8)
        oml = cut(8)
        ss = cut(8)
        crs = cut(S)
        meanw = cut(P)
        cv = lnp[:, 0, :].rearrange("p (c t) -> p c t", c=8)
        orow = lnp[:, 1, 0:RT * N]
        gn = lnp[:, 1, RT * N:RT * N + KDIM]
        csq = scr[:, both + 6 * 1024 + 512:both + 6 * 1024 + 512 + 2048].rearrange("p (c t) -> p c t", c=8)
        cvar = scr[:, both + 6 * 1024 + 512 + 2048:both + 6 * 1024 + 512 + 2048 + S]
        even_end = used[0]
        used[0] = both
        sm = cut(HG * (P + S))
        pT = cut(HG * (P + S))
        fbias = cut(HG * (P + S))
        rel = cut(HEADS * S).rearrange("p (h j) -> p h j", h=HEADS)
        sel = cut(HEADS * P).rearrange("p (h c) -> p h c", h=HEADS)
        ones = cut(S)
        tri = cut(S)
        WF = KT * HEADS + P - HEADS
        wf = cut(WF)
        bf = cut(1)
        zf = cut(S)
        za = cut(S)
        ls = cut(S)
        Ft = cut(S)
        Fc = cut(RT * HEADS)
        mx = cut(RT * HG)
        sums = cut(RT * HG)
        rs = cut(RT * HG)
        wf_hi = sb("wf_hi", [P, WF], F32R)
        wf_lo = sb("wf_lo", [P, WF], F32R)
        rstm = sb("rstm", [P, HG * S], mybir.dt.bfloat16)
        masks = sb("masks", [P, LEVELS, CHUNK], I8)
        imask = sb("imask", [P, P], I8)

        gemm = [ctx.enter_context(nc.psum_tensor(f"gemm{i}", [P, RT, N], F32)) for i in range(2)]
        pair = [ctx.enter_context(nc.psum_tensor(f"pair{i}", [P, RT * N], F32)) for i in range(2)]
        quad = [p[:, :].rearrange("p (k t) -> p k t", k=4) for p in pair]

        raw_full = [sem(f"raw_full{i}") for i in range(RING)]
        hi_ready, lo_ready = sem("hi_ready"), sem("lo_ready")
        chunk_used = sem("chunk_used")
        rows_done = sem("rows_done")
        act_link, dve_link, pool_link = sem("act_link"), sem("dve_link"), sem("pool_link")
        pair_full = [sem(f"pair_full{i}") for i in range(2)]
        row_ready = sem("row_ready")
        x_loaded = [sem(f"x_loaded{g}") for g in range(NP)]
        const_loaded, odd_loaded, lnp_loaded = sem("const_loaded"), sem("odd_loaded"), sem("lnp_loaded")
        consts, odd_consts, params_ready = sem("consts"), sem("odd_consts"), sem("params_ready")
        x_sum0, x_sum = sem("x_sum0"), sem("x_sum")
        stats_ready, mv_ready = sem("stats_ready"), sem("mv_ready")
        var_ready, rstd_ready = sem("var_ready"), sem("rstd_ready")
        nb_ready, xhat = sem("nb_ready"), sem("xhat")
        normed0, normed = sem("normed0"), sem("normed")
        xt_hi, xt_ready = sem("xt_hi"), sem("xt_ready")
        cat_hi, cat_ready = sem("cat_hi"), sem("cat_ready")
        relu_done, h_row, h_hi, h_ready = sem("relu_done"), sem("h_row"), sem("h_hi"), sem("h_ready")
        gate_ready, h_ready_row, pad_ready = sem("gate_ready"), sem("h_ready_row"), sem("pad_ready")
        taps_done, cen_ready, csq_ready = sem("taps_done"), sem("cen_ready"), sem("csq_ready")
        cvar_ready, croot_ready, cn_ready, conv_ready = (sem("cvar_ready"), sem("croot_ready"), sem("cn_ready"),
                                                         sem("conv_ready"))
        lb_exp, lb_ready, sig_ready, f_ready = sem("lb_exp"), sem("lb_ready"), sem("sig_ready"), sem("f_ready")
        lnf_ready, L_ready, k_ready, q_ready = sem("lnf_ready"), sem("L_ready"), sem("k_ready"), sem("q_ready")
        diff_ready, exp_ready, z_ready = sem("diff_ready"), sem("exp_ready"), sem("z_ready")
        scores_in, scores_clear = sem("scores_in"), sem("scores_clear")
        o_row, square_ready, o_normed = sem("o_row"), sem("square_ready"), sem("o_normed")
        g_silu, o_ready = sem("g_silu"), sem("o_ready")
        wf_hi_ready, wf_ready, z_sum, za_ready = sem("wf_hi_ready"), sem("wf_ready"), sem("z_sum"), sem("za_ready")
        zl_ready, F_ready, Fc_ready, fb_ready = sem("zl_ready"), sem("F_ready"), sem("Fc_ready"), sem("fb_ready")
        qk_ready, scores_read, max_ready = sem("qk_ready"), sem("scores_read"), sem("max_ready")
        prob_exp, prob_ready, pT_act, pT_dve = sem("prob_exp"), sem("prob_ready"), sem("pT_act"), sem("pT_dve")
        stored = sem("stored")

        block = ctx.enter_context(nc.Block())

        def tile_done(eng, layer, i):
            end = CPT * (i + 1)
            if i >= 12:
                part, j = divmod(i - 12, NT)
                end = PART_SLOT[part] + PART_CHUNKS[part] * (j + 1)
            eng.wait_ge(chunk_used, SLOT0[layer] + end)

        def raw_wait(eng, s):
            eng.wait_ge(raw_full[s % RING], 16 * (s // RING + 1))

        @block.sync
        def _(sp):
            def load(s, wmat, k0, c0):
                if s >= RING:
                    sp.wait_ge(lo_ready, s - RING + 1)
                sp.dma_start(raw[:, s % RING], wmat[k0 * P:(k0 + CK) * P, c0:c0 + N].rearrange("(k p) n -> p k n", p=P)
                             ).then_inc(raw_full[s % RING], 16)

            for layer in range(DEPTH):
                s = SLOT0[layer]
                for c0 in (EVEN_TILES, ODD_TILES)[layer]:
                    for c in range(CPT):
                        if s in X_BEFORE:
                            i = X_BEFORE.index(s)
                            cols = slice(PIECES[i][0] * P, sum(PIECES[i]) * P)
                            sp.dma_start(X[:, :, cols], x[0, :, cols].rearrange("(r p) n -> p r n", p=P)
                                         ).then_inc(x_loaded[i], 16)
                        load(s, w_in[layer], CK * c, c0)
                        s += 1
                for part in (EVEN_OUT, ODD_OUT)[layer]:
                    for j in range(NT):
                        for k in part[::CK]:
                            load(s, w_out[layer], k, j * N)
                            s += 1
                base = SLOT_MLP[layer]
                assert s == base and base % RING == 0
                w1, w2 = mlp_w1[layer], mlp_w2[layer]
                with sp.Fori(0, FB) as b:
                    with sp.Fori(0, NT) as j:
                        for c in range(CPT):
                            sp.wait_ge(lo_ready, b * (2 * NT * CPT) + j * CPT + (base + c - RING + 1))
                            sp.dma_start(raw[:, c % RING],
                                         w1[CK * c * P:CK * (c + 1) * P, bass.ds(b * D + j * N, N)].rearrange(
                                             "(k p) n -> p k n", p=P)).then_inc(raw_full[c % RING], 16)
                    with sp.Fori(0, NT) as j:
                        for c in range(CPT):
                            sp.wait_ge(lo_ready, b * (2 * NT * CPT) + j * CPT + (base + NT * CPT + c - RING + 1))
                            sp.dma_start(raw[:, c % RING],
                                         w2[bass.ds(b * D + CK * c * P, CK * P), bass.ds(j * N, N)].rearrange(
                                             "(k p) n -> p k n", p=P)).then_inc(raw_full[c % RING], 16)
            for i, (k0, n_) in enumerate(LAST_PIECES):
                sp.wait_ge(normed, 3 * NP + i + 1)
                cols = slice(k0 * P, (k0 + n_) * P)
                sp.dma_start(out[0, :, cols].rearrange("(r p) n -> p r n", p=P), X[:, :, cols]).then_inc(stored, 16)
            sp.wait_ge(stored, 16 * NP)

        @block.gpsimd
        def _(pool):
            n = [0]

            def link(ins):
                n[0] += 1
                ins.then_inc(pool_link, 1)
                pool.wait_ge(pool_link, n[0])

            def row(dst, src, width, s):
                pool.dma_start(dst, src.rearrange("(o n) -> o n", o=1).broadcast_to([P, width])).then_inc(s, 16)

            def ln_params(which):
                g, b = [(ln_mix_g[0], ln_mix_b[0]), (ln_mlp_g[0], ln_mlp_b[0]),
                        (ln_mix_g[1], ln_mix_b[1]), (ln_mlp_g[1], ln_mlp_b[1])][which]
                row(lnp[:, 0, :], g, D, lnp_loaded)
                row(lnp[:, 1, :], b, D, lnp_loaded)

            def inverse_root(which):
                pool.wait_ge(var_ready, 2 + which)
                pool.tensor_tensor(rstd[:, :, 0], mv[:, :, 1], mhalf[:, 0:RT], ALU.pow).then_inc(rstd_ready, 1)

            link(pool.memset(ident[:, :], 0.0))
            pool.affine_select(out=ident[:, :], in_=ident[:, :], compare_op=ALU.not_equal, fill=1.0, base=0,
                               pattern=[[-1, P]], channel_multiplier=1).then_inc(consts, 1)
            link(pool.memset(imask[:, :], 0))
            link(pool.affine_select(out=imask[:, :], in_=imask[:, :], compare_op=ALU.not_equal, fill=1.0, base=0,
                                    pattern=[[-1, P]], channel_multiplier=1))
            link(pool.memset(masks[:, :, :], 1))
            for lv in range(LEVELS):
                h = CHUNK >> lv
                m = masks[:, lv, :].rearrange("p (g r) -> p g r", r=h)
                link(pool.affine_select(out=m, in_=m, compare_op=ALU.is_ge, fill=0.0, base=0,
                                        pattern=[[-2 * h, CHUNK // h], [0, h]], channel_multiplier=1))
                link(pool.affine_select(out=m, in_=m, compare_op=ALU.is_ge, fill=0.0, base=h - 1,
                                        pattern=[[2 * h, CHUNK // h], [0, h]], channel_multiplier=-1))
            link(pool.memset(rstm[:, :], 1.0))
            link(pool.memset(rstm[:, :].rearrange("p (g t) -> p g t", t=P)[:, :, 0:1], 0.0))
            pool.memset(mhalf[:, :], -0.5)
            pool.memset(factor[:, 0:1], ALPHA)
            pool.memset(factor[:, 1:], 1.0)
            pool.memset(meanw, 1.0 / CONV_CH)
            for hp in hpad:
                pool.memset(hp[:, :, 0:CONV_W - 1], 0.0)
            link(pool.memset(A, 0.0))
            pool.dma_start(cw_rows[0:CONV_W, :], ev_conv_w[0]).then_inc(const_loaded, 16)
            for i, v in enumerate((ev_conv_b, ev_conv_ln_g, ev_conv_ln_b)):
                pool.dma_start(small_rows[8 * i:8 * i + 8, :], v[0].rearrange("(c p) -> c p", p=P)
                               ).then_inc(const_loaded, 16)
            pool.dma_start(small_rows[24:40, :], hgrn_lb_logits.rearrange("w (h k) -> (w h) k", k=DH)
                           ).then_inc(const_loaded, 16)
            row(gn, ev_gnorm_g[0], KDIM, const_loaded)
            pool.nop().then_inc(consts, 1)
            for half in range(2):
                if half == 1:
                    pool.wait_ge(pair_full[1], USE[1]["level", 0, 9] + 1)
                    pool.memset(A, 0.0).then_inc(scores_clear, 1)
                pool.wait_ge(var_ready, half + 1)
                pool.tensor_tensor(ss, ss, mhalf[:, 0:8], ALU.pow).then_inc(rstd_ready, 1)
            pool.wait_ge(pair_full[0], USE[0]["O1"] + 1)
            pool.wait_ge(cat_ready, 2)
            ln_params(0)
            pool.wait_ge(cat_ready, 3)
            pool.dma_start(wf[:, 0:KT * HEADS].rearrange("p (k h) -> p k h", k=KT),
                           od_w_in[0, :, FOX_F:FOX_F + HEADS].rearrange("(k p) h -> p k h", p=P)).then_inc(odd_loaded, 16)
            pool.dma_start(bf[0:HEADS, :], fox_b_f.rearrange("o h -> h o")).then_inc(odd_loaded, 16)
            for lo in range(2):
                j0 = CHUNK if lo == 0 else 0
                base = rel_bias[0, 0:1, lo * CHUNK - CHUNK + j0:lo * CHUNK - CHUNK + j0 + 1]
                pool.dma_start(rel[lo * CHUNK:(lo + 1) * CHUNK, :, j0:S],
                               bass.AP(base.tensor, base.offset, [[1, CHUNK], [REL_TABLE, HEADS], [1, S - j0]])
                               ).then_inc(odd_loaded, 16)
            pool.memset(rel[0:CHUNK, :, 0:CHUNK], NEG)
            pool.memset(wf[:, KT * HEADS:], 0.0)
            pool.memset(ones, 1.0)
            link(pool.memset(sel, 0.0))
            link(pool.memset(tri, 0.0))
            pool.affine_select(out=sel, in_=sel, compare_op=ALU.not_equal, fill=1.0, base=0,
                               pattern=[[-1, HEADS], [0, P]], channel_multiplier=1).then_inc(odd_consts, 1)
            pool.affine_select(out=tri[:, P:S], in_=tri[:, P:S], compare_op=ALU.is_ge, fill=NEG, base=0,
                               pattern=[[-1, P]], channel_multiplier=1).then_inc(odd_consts, 1)
            inverse_root(1)
            for which in range(1, 4):
                pool.wait_ge(normed, NP * which)
                ln_params(which)
                inverse_root(1 + which)

        @block.scalar
        def _(act):
            at = [0]
            n = [0]

            def link(ins):
                n[0] += 1
                ins.then_inc(act_link, 1)
                act.wait_ge(act_link, n[0])

            def split(s):
                raw_wait(act, s)
                if s >= RING:
                    act.wait_ge(chunk_used, s - RING + 1)
                act.activation(w_hi[:, s % RING], raw[:, s % RING], ACT.Copy).then_inc(hi_ready, 1)

            def upto(s):
                while at[0] <= s:
                    split(at[0])
                    at[0] += 1

            def evac(layer, i, dst, func, done):
                tile_done(act, layer, i)
                act.activation(dst, gemm[(TILE0[layer] + i) % 2][:, :, :], func).then_inc(done, 1)

            def hi_of(p, name, dst, done):
                act.wait_ge(pair_full[p], USE[p][name] + 1)
                act.activation(dst, quad[p][:, 0:dst.shape[1], :], ACT.Copy).then_inc(done, 1)

            def x_piece_hi(which, i):
                k0, n_ = PIECES[i]
                hi_of(i % 2, ("x", which, i), x_hi[:, k0:k0 + n_, :], xt_hi)

            def layer_norm(which):
                act.wait_ge(nb_ready, which)
                for i in range(1, NP):
                    k0, n_ = pieces_of(which)[i]
                    cols = slice(k0 * P, (k0 + n_) * P)
                    for r in range(RT):
                        act.activation(X[:, r, cols], X[:, r, cols], ACT.Identity, scale=rstd[:, r, :],
                                       bias=nbias[:, r:r + 1]).then_inc(xhat, 1)
                    if which < 4 and i >= 2:
                        x_piece_hi(which, i - 2)
                if which < 4:
                    x_piece_hi(which, NP - 2)
                    x_piece_hi(which, NP - 1)

            x_piece_hi(0, 0)
            upto(0)
            x_piece_hi(0, 1)
            upto(3)
            x_piece_hi(0, 2)
            upto(4)
            x_piece_hi(0, 3)
            upto(6)
            x_piece_hi(0, 4)

            def forget(half, s0, i):
                upto(s0 + 11)
                act.wait_ge(h_ready_row, half + 1)
                evac(0, i, urow[0], ACT.Copy, row_ready)
                upto(s0 + 13)
                if half == 1:
                    act.wait_ge(z_ready, 8)
                act.wait_ge(pair_full[0], USE[0][f"F{half}"] + 1)
                act.activation(Dm, pair[0][:, :], ACT.Sigmoid).then_inc(sig_ready, 1)
                upto(s0 + 14)
                act.wait_ge(sig_ready, half + 1)
                act.wait_ge(lb_ready, 1)
                if half == 1:
                    act.wait_ge(pair_full[1], USE[1]["level", 0, 8] + 1)
                for h in range(HG):
                    c = HG * half + h
                    ins = act.activation(L[:, h * S:(h + 1) * S], Dm[:, h * S:(h + 1) * S], ACT.Identity,
                                         scale=oml[:, c:c + 1], bias=lb[:, c:c + 1])
                link(ins)
                act.activation(kT.rearrange("p h t -> p (h t)"), L, ACT.Identity, scale=-1.0, bias=1.0
                               ).then_inc(k_ready, 1)
                upto(s0 + 16)
                act.wait_ge(f_ready, half + 1)
                act.activation(Dm, L, ACT.Ln).then_inc(lnf_ready, 1)

            def query(half, s0, i):
                upto(s0 + 11)
                act.wait_ge(pair_full[0], USE[0][f"C{half}"] + 1)
                evac(0, i, urow[1], ACT.Copy, row_ready)
                upto(s0 + 13)
                act.wait_ge(pair_full[0], USE[0][f"Q{half}"] + 1)
                act.activation(qT.rearrange("p h t -> p (h t)"), pair[0][:, :], ACT.Silu).then_inc(q_ready, 1)

            def exps(half, k):
                if k < LEVELS:
                    act.wait_ge(diff_ready, LEVELS * half + k + 1)
                    h = CHUNK >> k
                    v = Dm.rearrange("p (g u r) -> p g u r", u=2, r=h)
                    act.activation(v[:, :, 0, :], v[:, :, 0, :], ACT.Exp, scale=-1.0)
                    act.activation(v[:, :, 1, :], v[:, :, 1, :], ACT.Exp).then_inc(exp_ready, 1)
                else:
                    act.wait_ge(z_ready, 8 * half + LEVELS)
                    v = Dm.rearrange("p (h b t) -> p h b t", b=2, t=P)
                    Lv = L.rearrange("p (h b t) -> p h b t", b=2, t=P)
                    for h in range(HG):
                        act.activation(v[:, h, 0, :], Lv[:, h, 0, :], ACT.Exp, scale=-1.0, bias=Lv[:, h, 0, P - 1:P])
                    act.activation(v[:, :, 1, :], Lv[:, :, 1, :], ACT.Exp).then_inc(exp_ready, 1)

            def out_rows(half):
                act.wait_ge(pair_full[1], USE[1]["level", half, 9] + 1)
                if half == 1:
                    act.wait_ge(pair_full[0], USE[0]["O0"] + 1)
                act.activation(orow, pair[1][:, :], ACT.Copy).then_inc(o_row, 1)
                act.wait_ge(o_row, half + 1)
                for b in range(2 * HG):
                    cols = slice(b * DH, (b + 1) * DH)
                    ins = act.activation(Dm[:, cols], orow[:, cols], ACT.Square, accum_out=ss[:, b:b + 1])
                ins.then_inc(square_ready, 1)

            def norm_rows(half):
                act.wait_ge(rstd_ready, half + 1)
                for b in range(2 * HG):
                    cols = slice(b * DH, (b + 1) * DH)
                    ins = act.activation(orow[:, cols], orow[:, cols], ACT.Identity, scale=ss[:, b:b + 1])
                ins.then_inc(o_normed, 1)

            def group_hi(name, k0):
                hi_of(0, name, c_hi[:, k0:k0 + 4, :], cat_hi)

            upto(11)
            evac(0, 0, urow[0], ACT.Sigmoid, gate_ready)
            act.wait_ge(lb_exp, 1)
            act.activation(lbl, lbl, ACT.Exp).then_inc(lb_exp, 1)
            upto(22)
            act.wait_ge(pair_full[0], USE[0]["C0"] + 1)
            act.activation(hpad[0][:, :, CONV_W - 1:], quad[0], ACT.Copy).then_inc(pad_ready, 1)
            forget(0, FORGET_SLOT[0], 2)
            query(0, FORGET_SLOT[0] + 8, 3)
            for s in range(38, SLOT_MLP[0]):
                if s == FORGET_SLOT[1] + 9:
                    forget(1, FORGET_SLOT[1], 8)
                    query(1, FORGET_SLOT[1] + 8, 9)
                upto(s)
                for half, base in enumerate(LEVEL_SLOT):
                    k = s - base - 1
                    if k >= 0 and k % 2 == 0 and k <= 2 * LEVELS:
                        exps(half, k // 2)
                if s == 43:
                    act.wait_ge(pair_full[0], USE[0]["F0"] + 1)
                    evac(0, 4, urow[0], ACT.Sigmoid, gate_ready)
                if s == 54:
                    act.wait_ge(pair_full[0], USE[0]["C1"] + 1)
                    act.activation(hpad[1][:, :, CONV_W - 1:], quad[0], ACT.Copy).then_inc(pad_ready, 1)
                if s == 59:
                    evac(0, 6, vrow, ACT.Copy, row_ready)
                if s == LEVEL_SLOT[0] + 26:
                    out_rows(0)
                if s == 67:
                    evac(0, 7, G.rearrange("p (r n) -> p r n", r=RT), ACT.Silu, g_silu)
                if s == 71:
                    group_hi("O0", 8)
                if s == 92:
                    act.wait_ge(pair_full[1], USE[1]["level", 0, 9] + 1)
                    evac(0, 10, vrow, ACT.Copy, row_ready)
                if s == MEAN_SLOT + 4:
                    act.wait_ge(cen_ready, 1)
                    act.activation(csq, cv, ACT.Square).then_inc(csq_ready, 1)
                if s == MEAN_SLOT + 7:
                    act.wait_ge(cvar_ready, 1)
                    link(act.activation(crs, cvar, ACT.Ln))
                    act.activation(crs, crs, ACT.Exp, scale=-0.5).then_inc(croot_ready, 1)
                if s == 99:
                    act.wait_ge(o_ready, 1)
                    evac(0, 11, G.rearrange("p (r n) -> p r n", r=RT), ACT.Silu, g_silu)
                if s == MEAN_SLOT + 9:
                    act.wait_ge(cn_ready, 1)
                    act.wait_ge(pair_full[0], USE[0]["variance"] + 1)
                    for c in range(8):
                        ins = act.activation(csq[:, c, :], cv[:, c, :], ACT.Silu, scale=cpar[:, 1, c:c + 1],
                                             bias=cpar[:, 2, c:c + 1])
                    ins.then_inc(conv_ready, 1)
                    act.wait_ge(conv_ready, 1)
                    act.activation(c_hi[:, 0:8, :], csq, ACT.Copy).then_inc(cat_hi, 1)
                for half in range(2):
                    if s == LEVEL_SLOT[half] + 26 + 2 * (1 - half):
                        norm_rows(half)
                if s == LEVEL_SLOT[1] + 24:
                    out_rows(1)
                if s == OUT_SLOT[1]:
                    group_hi("O1", 12)
            upto(SLOT_MLP[0] + RING - 1)

            def mlp_tile(base, tbase, layer, b, i, last=False):
                first = base + i * CPT + RING
                for c in range(CPT):
                    s = first + c
                    if last and b * (2 * NT * CPT) + s >= SLOTS:
                        break
                    act.wait_ge(raw_full[s % RING], b * (16 * 2 * NT * CPT // RING) + 16 * (s // RING + 1))
                    act.wait_ge(chunk_used, b * (2 * NT * CPT) + (s - RING + 1))
                    act.activation(w_hi[:, s % RING], raw[:, s % RING], ACT.Copy).then_inc(hi_ready, 1)
                    if c == 1 and 1 <= i <= NT:
                        act.wait_ge(pair_full[0], b * NT + (USE[0]["h", layer, 0] + i))
                        act.activation(c_hi[:, 4 * (i - 1):4 * i, :], quad[0], ACT.Copy).then_inc(h_hi, 1)
                if i < NT:
                    t = tbase + i
                    act.wait_ge(chunk_used, b * (2 * NT * CPT) + (base + (i + 1) * CPT))
                    act.activation(urow[i % 2], gemm[t % 2][:, :, :], ACT.Relu).then_inc(relu_done, 1)
                    act.wait_ge(relu_done, b * NT + (layer * FB * NT + i + 1))
                    act.activation(urow[i % 2], urow[i % 2], ACT.Square).then_inc(h_row, 1)

            def mlp(layer):
                base, tbase = SLOT_MLP[layer], TILE_MLP[layer]
                whole = FB if layer == 0 else FB - 1
                with act.Fori(0, whole) as b:
                    for i in range(2 * NT):
                        mlp_tile(base, tbase, layer, b, i)
                if layer == 1:
                    for i in range(2 * NT):
                        mlp_tile(base, tbase, layer, whole, i, last=True)
                at[0] = base + MLP_SLOTS + RING

            layer_norm(1)
            mlp(0)

            layer_norm(2)
            o = SLOT0[1]
            act.wait_ge(odd_loaded, 16 * 4)
            act.activation(wf_hi[:, :], wf, ACT.Copy).then_inc(wf_hi_ready, 1)
            for g in range(4):
                s0 = o + 24 * g
                upto(s0 + 6 if g else s0 + 3)
                if g:
                    group_hi(("out", g - 1), 4 * (g - 1))
                upto(s0 + 11)
                evac(1, 3 * g, urow[0], ACT.Copy, row_ready)
                if g == 0:
                    upto(s0 + 12)
                    act.wait_ge(za_ready, 1)
                    link(act.activation(za[0:HEADS, :], za[0:HEADS, :], ACT.Exp, scale=-1.0))
                    act.activation(za[0:HEADS, :], za[0:HEADS, :], ACT.Ln, bias=1.0).then_inc(zl_ready, 1)
                upto(s0 + 13)
                act.wait_ge(pair_full[0], USE[0]["q", g] + 1)
                act.activation(qT, quad[0], ACT.Copy).then_inc(qk_ready, 1)
                upto(s0 + 19)
                evac(1, 3 * g + 1, urow[1], ACT.Copy, row_ready)
                upto(s0 + 21)
                act.wait_ge(pair_full[0], USE[0]["k", g] + 1)
                act.activation(kT, quad[0], ACT.Copy).then_inc(qk_ready, 1)
                upto(s0 + 25)
                act.wait_ge(max_ready, g + 1)
                for q in range(RT):
                    width = (q + 1) * P
                    v = sm[:, q * HG * P:q * HG * P + HG * width].rearrange("p (h k) -> p h k", h=HG)
                    for h in range(HG):
                        i = q * HG + h
                        ins = act.activation(v[:, h, :], v[:, h, :], ACT.Exp, bias=mx[:, i:i + 1],
                                             accum_out=sums[:, i:i + 1])
                ins.then_inc(prob_exp, 1)
                upto(s0 + 27)
                evac(1, 3 * g + 2, vrow, ACT.Copy, row_ready)
                upto(s0 + 28)
                act.wait_ge(pair_full[0], USE[0]["probs", g] + 1)
                act.activation(pT[:, 0:HG * S], pair[0][:, :], ACT.Copy).then_inc(pT_act, 1)
            upto(o + 72 + 30)
            group_hi(("out", 3), 12)
            upto(SLOT_MLP[1] + RING - 1)
            layer_norm(3)
            mlp(1)
            layer_norm(4)

        @block.vector
        def _(dve):
            at = [0]
            n = [0]

            def mark(ins):
                n[0] += 1
                ins.then_inc(dve_link, 1)
                return n[0]

            def link(ins):
                dve.wait_ge(dve_link, mark(ins))

            def split(s):
                dve.wait_ge(hi_ready, s + 1)
                raw_wait(dve, s)
                if s >= RING:
                    dve.wait_ge(chunk_used, s - RING + 1)
                dve.tensor_tensor(w_lo[:, s % RING], raw[:, s % RING], w_hi[:, s % RING].bitcast(F32), ALU.subtract
                                  ).then_inc(lo_ready, 1)

            def upto(s):
                while at[0] <= s:
                    add_before(at[0])
                    split(at[0])
                    at[0] += 1

            def lo_of(p, hi, lo, hi_sem, value, ready):
                dve.wait_ge(hi_sem, value)
                dve.tensor_tensor(lo, quad[p][:, 0:lo.shape[1], :], hi.bitcast(F32), ALU.subtract).then_inc(ready, 1)

            def add_tile(layer, part, j):
                i = 12 + NT * part + j
                t = TILE0[layer] + i
                for r, done in enumerate((x_sum0, x_sum)):
                    if r == 0:
                        dve.wait_ge(rows_done, t + 1)
                    else:
                        tile_done(dve, layer, i)
                    Xj, tile = X[:, r, j * N:(j + 1) * N], gemm[t % 2][:, r, :]
                    if part == 0:
                        dve.scalar_tensor_tensor(out=Xj, in0=Xj, scalar=ALPHA, in1=tile, op0=ALU.mult, op1=ALU.add
                                                 ).then_inc(done, 1)
                    else:
                        dve.tensor_tensor(Xj, tile, Xj, ALU.add).then_inc(done, 1)
                    if part == PARTS - 1:
                        dve.wait_ge(done, NT * ((PARTS + FB) * layer + part) + j + 1)
                        tile_stats(j, r)
                if part == PARTS - 1 and j == NT - 1:
                    statistics((1 + FB) * NT * layer + NT, 2 * layer + 1)

            def add_before(s):
                for layer in range(DEPTH):
                    for part in range(PARTS):
                        for j in range(NT):
                            if s == SLOT0[layer] + PART_SLOT[part] + PART_CHUNKS[part] * (j + 1) - 1 + RING:
                                add_tile(layer, part, j)

            def tile_stats(j, r):
                dve.bn_stats(stats[:, r, j, :], X[:, r, j * N:(j + 1) * N]).then_inc(stats_ready, 1)

            def x_piece_lo(which, i):
                k0, n_ = PIECES[i]
                lo_of(i % 2, x_hi[:, k0:k0 + n_, :], x_lo[:, k0:k0 + n_, :], xt_hi, NP * which + i + 1, xt_ready)

            def statistics(tiles, norms):
                dve.wait_ge(stats_ready, tiles * RT)
                for r in range(RT):
                    dve.bn_aggr(mv[:, r, :], stats[:, r, :, :]).then_inc(mv_ready, 1)
                dve.wait_ge(mv_ready, norms * RT)
                dve.tensor_scalar(mv[:, :, 1], mv[:, :, 1], EPS, None, ALU.add).then_inc(var_ready, 1)

            def layer_norm(which):
                dve.wait_ge(lnp_loaded, 32 * which)
                dve.wait_ge(rstd_ready, 2 + which)

                def gain(i, which=which):
                    k0, n_ = pieces_of(which)[i]
                    cols = slice(k0 * P, (k0 + n_) * P)
                    gb = lnp[:, 0, cols].unsqueeze(1).broadcast_to([P, RT, n_ * P])
                    bb = lnp[:, 1, cols].unsqueeze(1).broadcast_to([P, RT, n_ * P])
                    dve.wait_ge(xhat, RT * ((NP - 1) * (which - 1) + i))
                    link(dve.tensor_tensor(X[:, :, cols], X[:, :, cols], gb, ALU.mult))
                    dve.tensor_tensor(X[:, :, cols], X[:, :, cols], bb, ALU.add).then_inc(normed, 1)

                first = slice(0, PIECES[0][1] * P)
                for r in range(RT):
                    link(dve.tensor_scalar(X[:, r, first], X[:, r, first], mv[:, r, 0:1], rstd[:, r, :],
                                           ALU.subtract, ALU.mult))
                    if r == 0:
                        dve.scalar_tensor_tensor(out=nbias[:, :], in0=mv[:, :, 0], scalar=-1.0, in1=rstd[:, :, 0],
                                                 op0=ALU.mult, op1=ALU.mult).then_inc(nb_ready, 1)
                    link(dve.tensor_tensor(X[:, r, first], X[:, r, first], lnp[:, 0, first], ALU.mult))
                    ins = dve.tensor_tensor(X[:, r, first], X[:, r, first], lnp[:, 1, first], ALU.add)
                    ins.then_inc(normed if r else normed0, 1)
                gain(1)
                if which == 4:
                    for i in range(2, NP):
                        gain(i)
                    return
                x_piece_lo(which, 0)
                x_piece_lo(which, 1)
                gain(2)
                gain(3)
                gain(4)
                x_piece_lo(which, 2)
                x_piece_lo(which, 3)
                x_piece_lo(which, 4)

            x_piece_lo(0, 0)
            upto(0)
            x_piece_lo(0, 1)
            upto(3)
            x_piece_lo(0, 2)
            upto(4)
            x_piece_lo(0, 3)
            upto(6)
            x_piece_lo(0, 4)
            upto(10)
            dve.wait_ge(pair_full[1], USE[1]["params"] + 1)
            dve.tensor_copy(cw, pair[1][:, 0:8 * 32].rearrange("p (c j) -> p c j", c=8)[:, :, 0:CONV_W]
                            ).then_inc(dve_link, 1)
            n[0] += 1
            dve.tensor_copy(small, pair[1][:, 8 * 32:8 * 32 + 40]).then_inc(params_ready, 1)
            dve.wait_ge(params_ready, 1)
            dve.wait_ge(consts, 2)
            link(dve.tensor_tensor(lb, lbl[:, 0, :], lbl[:, 1, :], ALU.max))
            k = mark(dve.tensor_tensor(lbl[:, 0, :], lbl[:, 0, :], lb, ALU.subtract))
            dve.tensor_tensor(lbl[:, 1, :], lbl[:, 1, :], lb, ALU.subtract).then_inc(lb_exp, 1)
            upto(13)
            dve.wait_ge(lb_exp, 2)
            link(dve.tensor_tensor(lb, lbl[:, 0, :], lbl[:, 1, :], ALU.add))
            link(dve.reciprocal(oml, lb))
            link(dve.tensor_tensor(lb, lbl[:, 0, :], oml, ALU.mult))
            dve.tensor_scalar(oml, lb, -1.0, 1.0, ALU.mult, ALU.add).then_inc(lb_ready, 1)

            def forget(half, s0):
                upto(s0 + 15)
                dve.wait_ge(k_ready, half + 1)
                dve.tensor_scalar(L, L, F_MIN, None, ALU.max).then_inc(f_ready, 1)
                upto(s0 + 17)
                dve.wait_ge(lnf_ready, half + 1)
                dve.tensor_tensor_scan(L, rstm[:, :], Dm, 0.0, ALU.mult, ALU.add).then_inc(L_ready, 1)

            def diff(half, k):
                if k == 0:
                    dve.wait_ge(q_ready, half + 1)
                    dve.wait_ge(L_ready, half + 1)
                else:
                    dve.wait_ge(z_ready, 8 * half + k)
                h = CHUNK >> k
                Lv = L.rearrange("p (g t) -> p g t", t=2 * h)
                mid = Lv[:, :, h - 1:h].broadcast_to([P, HG * S // (2 * h), 2 * h])
                dve.tensor_tensor(Dm.rearrange("p (g t) -> p g t", t=2 * h), Lv, mid, ALU.subtract
                                  ).then_inc(diff_ready, 1)

            def weigh(half, k):
                dve.wait_ge(exp_ready, 8 * half + k + 1)
                if 8 * half + k >= 2:
                    dve.wait_ge(pair_full[1], USE[1][("level", half, k - 2) if k >= 2 else ("level", 0, 6 + k)] + 1)
                h = CHUNK >> k if k < LEVELS else P
                z = Z[k % 2].rearrange("p (g u r) -> p g u r", u=2, r=h)
                e = Dm.rearrange("p (g u r) -> p g u r", u=2, r=h)
                kv = kT.rearrange("p h t -> p (h t)").rearrange("p (g u r) -> p g u r", u=2, r=h)
                qv = qT.rearrange("p h t -> p (h t)").rearrange("p (g u r) -> p g u r", u=2, r=h)
                dve.tensor_tensor(z[:, :, 0, :], e[:, :, 0, :], kv[:, :, 0, :], ALU.mult)
                dve.tensor_tensor(z[:, :, 1, :], e[:, :, 1, :], qv[:, :, 1, :], ALU.mult).then_inc(z_ready, 1)

            def take(half, k):
                dve.wait_ge(pair_full[1], USE[1]["level", half, k] + 1)
                if k == 0:
                    dve.wait_ge(scores_clear, half)
                Av = A.rearrange("p (b t) -> p b t", t=P)
                if k < LEVELS:
                    h = CHUNK >> k
                    o_ = A.rearrange("p (b g u r) -> p b g u r", b=2 * HG, u=2, r=h)[:, :, :, 1, :]
                    m_ = masks[:, k, :].rearrange("p (g r) -> p g r", r=h).unsqueeze(1).broadcast_to(
                        [P, 2 * HG, CHUNK // h, h])
                    d_ = pair[1][:, 0:N].rearrange("p (b g r) -> p b g r", b=2 * HG, r=h)
                    ins = dve.copy_predicated(o_, m_, d_)
                elif k == LEVELS:
                    ins = dve.tensor_copy(Ax, pair[1][:, 0:N])
                else:
                    ins = dve.copy_predicated(Av, imask[:, :].unsqueeze(1).broadcast_to([P, 2 * HG, P]),
                                              pair[1][:, :].rearrange("p (b t) -> p b t", t=P))
                ins.then_inc(scores_in, 1)

            def gates(half):
                dve.wait_ge(g_silu, half + 1)
                gv = G.rearrange("p (r n) -> p r n", r=RT)
                link(dve.tensor_tensor(gv, gv, gn[:, half * N:(half + 1) * N].unsqueeze(1).broadcast_to([P, RT, N]),
                                       ALU.mult))

            def mean_square(half):
                dve.wait_ge(square_ready, half + 1)
                dve.tensor_scalar(ss, ss, 1.0 / DH, EPS, ALU.mult, ALU.add).then_inc(var_ready, 1)

            def gate_out(half):
                dve.wait_ge(o_normed, half + 1)
                dve.tensor_tensor(orow, orow, G, ALU.mult).then_inc(o_ready, 1)

            def group_lo(k0, value):
                lo_of(0, c_hi[:, k0:k0 + 4, :], c_lo[:, k0:k0 + 4, :], cat_hi, value, cat_ready)

            tap_mark = {}
            taps = [0]

            def conv(count):
                for _ in range(count):
                    if taps[0] == 8 * CONV_W:
                        return
                    half, rest = divmod(taps[0], 4 * CONV_W)
                    j, c = divmod(rest, 4)
                    if rest == 0:
                        dve.wait_ge(pad_ready, half + 1)
                    ch = 4 * half + c
                    src = hpad[half][:, c, j:j + S]
                    if j == 0:
                        ins = dve.tensor_scalar(cv[:, ch, :], src, cw[:, ch, 0:1], cpar[:, 0, ch:ch + 1], ALU.mult, ALU.add)
                    else:
                        dve.wait_ge(dve_link, tap_mark[ch])
                        ins = dve.scalar_tensor_tensor(out=cv[:, ch, :], in0=src, scalar=cw[:, ch, j:j + 1],
                                                       in1=cv[:, ch, :], op0=ALU.mult, op1=ALU.add)
                    tap_mark[ch] = mark(ins)
                    taps[0] += 1
                    if taps[0] == 8 * CONV_W:
                        dve.wait_ge(dve_link, n[0])
                        dve.nop().then_inc(taps_done, 1)

            def gated(i, half):
                dve.wait_ge(gate_ready, half + 1)
                tile_done(dve, 0, i)
                if half == 1:
                    dve.wait_ge(pair_full[0], USE[0]["Q0"] + 1)
                dve.tensor_tensor(urow[1], gemm[(TILE0[0] + i) % 2][:, :, :], urow[0], ALU.mult
                                  ).then_inc(h_ready_row, 1)

            for s in range(14, SLOT_MLP[0]):
                upto(s)
                for half, k in enumerate((s - LEVEL_SLOT[0], s - LEVEL_SLOT[1])):
                    if k >= 0 and k % 2 == 0 and k // 2 <= 10:
                        k //= 2
                        if 1 <= k <= 8:
                            weigh(half, k - 1)
                        if k < LEVELS:
                            diff(half, k)
                        if 2 <= k:
                            take(half, k - 2)
                if s == 19:
                    gated(1, 0)
                if s == 31:
                    forget(0, FORGET_SLOT[0])
                if s == 51:
                    gated(5, 1)
                if s == 65:
                    mean_square(0)
                if s == 67:
                    gates(0)
                if s == 68:
                    gate_out(0)
                if s == 71:
                    group_lo(8, 1)
                if s == 79:
                    forget(1, FORGET_SLOT[1])
                if s == MEAN_SLOT + 3:
                    conv(8 * CONV_W)
                    dve.wait_ge(pair_full[0], USE[0]["mean"] + 1)
                    dve.tensor_tensor(cv, cv, pair[0][:, 0:S].unsqueeze(1).broadcast_to([P, 8, S]), ALU.subtract
                                      ).then_inc(cen_ready, 1)
                if s == MEAN_SLOT + 7:
                    dve.wait_ge(pair_full[0], USE[0]["variance"] + 1)
                    dve.tensor_scalar(cvar, pair[0][:, 0:S], EPS, None, ALU.add).then_inc(cvar_ready, 1)
                if s == MEAN_SLOT + 8:
                    dve.wait_ge(croot_ready, 1)
                    link(dve.tensor_tensor(cvar, cvar, crs, ALU.mult))
                    link(dve.tensor_tensor(cvar, cvar, crs, ALU.mult))
                    link(dve.tensor_scalar(cvar, cvar, -0.5, 1.5, ALU.mult, ALU.add))
                    link(dve.tensor_tensor(crs, crs, cvar, ALU.mult))
                    dve.tensor_tensor(cv, cv, crs.unsqueeze(1).broadcast_to([P, 8, S]), ALU.mult).then_inc(cn_ready, 1)
                if s == 101:
                    gates(1)
                if s == CONV_LO_SLOT:
                    dve.wait_ge(cat_hi, 2)
                    dve.tensor_tensor(c_lo[:, 0:8, :], csq, c_hi[:, 0:8, :].bitcast(F32), ALU.subtract
                                      ).then_inc(cat_ready, 1)
                if s == LEVEL_SLOT[1] + 25:
                    mean_square(1)
                if s == LEVEL_SLOT[1] + 27:
                    gate_out(1)
                if s == OUT_SLOT[1]:
                    group_lo(12, 3)
                if 22 <= s < MEAN_SLOT + 3:
                    conv(taps_behind(s))

            def last_part(layer):
                upto(SLOT_MLP[layer] + RING - 1)
                x_sums[0] += PARTS * NT

            x_sums = [0]
            last_part(0)

            def add_block(layer, b, j, t, end, last):
                for r, done in enumerate((x_sum0, x_sum)):
                    if r == 0:
                        dve.wait_ge(rows_done, b * (2 * NT) + (t + 1))
                    else:
                        dve.wait_ge(chunk_used, b * (2 * NT * CPT) + end)
                    Xj = X[:, r, j * N:(j + 1) * N]
                    dve.scalar_tensor_tensor(out=Xj, in0=Xj, scalar=factor[:, bass.ds(b, 1)], in1=gemm[t % 2][:, r, :],
                                             op0=ALU.mult, op1=ALU.add).then_inc(done, 1)
                    dve.wait_ge(done, b * NT + (x_sums[0] + j + 1))
                    tile_stats(j, r)
                if last and j == NT - 1:
                    statistics((1 + FB) * NT * (layer + 1), 2 * layer + 2)

            def mlp_tile(layer, b, i, last=False):
                base, tbase = SLOT_MLP[layer], TILE_MLP[layer]
                first = base + i * CPT + RING
                for c in range(CPT):
                    s = first + c
                    if c == CPT - 1 and i >= NT:
                        add_block(layer, b, i - NT, tbase + i, base + (i + 1) * CPT, last)
                    if last and b * (2 * NT * CPT) + s >= SLOTS:
                        continue
                    dve.wait_ge(hi_ready, b * (2 * NT * CPT) + (s + 1))
                    dve.wait_ge(raw_full[s % RING], b * (16 * 2 * NT * CPT // RING) + 16 * (s // RING + 1))
                    dve.wait_ge(chunk_used, b * (2 * NT * CPT) + (s - RING + 1))
                    dve.tensor_tensor(w_lo[:, s % RING], raw[:, s % RING], w_hi[:, s % RING].bitcast(F32), ALU.subtract
                                      ).then_inc(lo_ready, 1)
                    if c == 1 and 1 <= i <= NT:
                        dve.wait_ge(h_hi, b * NT + (layer * NT * FB + i))
                        dve.tensor_tensor(c_lo[:, 4 * (i - 1):4 * i, :], quad[0],
                                          c_hi[:, 4 * (i - 1):4 * i, :].bitcast(F32), ALU.subtract
                                          ).then_inc(h_ready, 1)

            def mlp(layer):
                with dve.Fori(0, FB - 1) as b:
                    for i in range(2 * NT):
                        mlp_tile(layer, b, i)
                for i in range(2 * NT):
                    mlp_tile(layer, FB - 1, i, last=True)
                x_sums[0] += NT * FB
                at[0] = SLOT_MLP[layer] + MLP_SLOTS + RING

            layer_norm(1)
            mlp(0)
            layer_norm(2)

            o = SLOT0[1]
            dve.wait_ge(wf_hi_ready, 1)
            dve.tensor_tensor(wf_lo[:, :], wf, wf_hi[:, :].bitcast(F32), ALU.subtract).then_inc(wf_ready, 1)

            def forget_bias(g):
                dve.wait_ge(pair_full[1], USE[1]["F", g] + 1)
                for q in range(RT):
                    width = (q + 1) * P
                    for h in range(HG):
                        o_ = fbias[:, q * HG * P + h * width:q * HG * P + (h + 1) * width]
                        ins = dve.scalar_tensor_tensor(out=o_, in0=tri[:, S - width:S],
                                                       scalar=Fc[:, q * HEADS + HG * g + h:q * HEADS + HG * g + h + 1],
                                                       in1=quad[1][:, h, 0:width], op0=ALU.add, op1=ALU.subtract)
                        ins.then_inc(fb_ready, 1)

            def softmax_in(g):
                dve.wait_ge(pair_full[0], USE[0]["scores", g] + 1)
                dve.wait_ge(pair_full[1], USE[1]["scores", g] + 1)
                if g < 2:
                    dve.wait_ge(fb_ready, RT * HG * (g + 1))
                for q in range(RT):
                    width = (q + 1) * P
                    o_ = sm[:, q * HG * P:q * HG * P + HG * width].rearrange("p (h k) -> p h k", h=HG)
                    src = (pair[0][:, 0:N], pair[1][:, :])[q].rearrange("p (h k) -> p h k", h=HG)
                    if g < 2:
                        bias = fbias[:, q * HG * P:q * HG * P + HG * width].rearrange("p (h k) -> p h k", h=HG)
                    else:
                        last = P * q + 2 * CHUNK - 1
                        lo = last - width
                        heads = rel[:, HG * (g - 2):HG * (g - 1), :]
                        bias = heads[:, :, last::-1] if lo < 0 else heads[:, :, last:lo:-1]
                    dve.scalar_tensor_tensor(out=o_, in0=src, scalar=SCALE, in1=bias, op0=ALU.mult, op1=ALU.add
                                             ).then_inc(scores_read, 1)
                    dve.wait_ge(scores_read, 2 * g + q + 1)
                    link(dve.tensor_reduce(mx[:, q * HG:(q + 1) * HG], o_, AX.X, ALU.max))
                dve.tensor_scalar(mx, mx, -1.0, None, ALU.mult).then_inc(max_ready, 1)

            def softmax_out(g):
                dve.wait_ge(prob_exp, g + 1)
                link(dve.reciprocal(rs, sums))
                for q in range(RT):
                    width = (q + 1) * P
                    v = sm[:, q * HG * P:q * HG * P + HG * width].rearrange("p (h k) -> p h k", h=HG)
                    ins = dve.tensor_tensor(v, v, rs[:, q * HG:(q + 1) * HG].unsqueeze(2).broadcast_to([P, HG, width]),
                                            ALU.mult)
                ins.then_inc(prob_ready, 1)

            for g in range(4):
                s0 = o + 24 * g
                if g:
                    upto(s0 + 6)
                    lo_of(0, c_hi[:, 4 * (g - 1):4 * g, :], c_lo[:, 4 * (g - 1):4 * g, :], cat_hi, 3 + g, cat_ready)
                if g == 0:
                    upto(s0 + 12)
                    dve.wait_ge(pair_full[1], USE[1]["logits"] + 1)
                    dve.tensor_scalar(zf[0:HEADS, :], pair[1][0:HEADS, 0:S], bf[0:HEADS, :], None, ALU.add
                                      ).then_inc(z_sum, 1)
                    dve.wait_ge(z_sum, 1)
                    dve.scalar_tensor_tensor(out=za[0:HEADS, :], in0=zf[0:HEADS, :], scalar=-1.0, in1=zf[0:HEADS, :],
                                             op0=ALU.mult, op1=ALU.max).then_inc(za_ready, 1)
                    upto(s0 + 13)
                    dve.wait_ge(zl_ready, 1)
                    link(dve.scalar_tensor_tensor(out=ls[0:HEADS, :], in0=zf[0:HEADS, :], scalar=0.0,
                                                  in1=za[0:HEADS, :], op0=ALU.min, op1=ALU.subtract))
                    dve.tensor_tensor_scan(Ft[0:HEADS, :], ones[0:HEADS, :], ls[0:HEADS, :], 0.0, ALU.mult, ALU.add
                                           ).then_inc(F_ready, 1)
                    upto(s0 + 16)
                    dve.wait_ge(pair_full[1], USE[1]["F rows"] + 1)
                    dve.tensor_copy(Fc, pair[1][:, 0:RT * HEADS]).then_inc(Fc_ready, 1)
                    dve.wait_ge(Fc_ready, 1)
                    upto(s0 + 18)
                    forget_bias(0)
                if g == 1:
                    upto(s0 + 14)
                    forget_bias(1)
                upto(s0 + 24)
                softmax_in(g)
                upto(s0 + 26)
                softmax_out(g)
                upto(s0 + 28)
                dve.wait_ge(pair_full[1], USE[1]["probs", g] + 1)
                dve.tensor_copy(pT[:, HG * S:], pair[1][:, 0:N]).then_inc(pT_dve, 1)
            upto(o + 102)
            lo_of(0, c_hi[:, 12:16, :], c_lo[:, 12:16, :], cat_hi, 7, cat_ready)
            last_part(1)
            layer_norm(3)
            mlp(1)
            layer_norm(4)

        @block.tensor
        def _(pe):
            def products(acc, hi, lo, k, slot, first, last):
                for r in range(RT):
                    rows = slice(r * P, (r + 1) * P)
                    for c in range(CK):
                        begin, end = first and c == 0, last and c == CK - 1
                        pe.matmul(acc[:, r, :], hi[:, k + c, rows], w_hi[:, slot, c, :], start=begin, stop=False)
                        pe.matmul(acc[:, r, :], hi[:, k + c, rows], w_lo[:, slot, c, :], start=False, stop=False)
                        ins = pe.matmul(acc[:, r, :], lo[:, k + c, rows], w_hi[:, slot, c, :], start=False, stop=end)
                    if last and r == 0:
                        ins.then_inc(rows_done, 1)
                ins.then_inc(chunk_used, 1)

            def chunk(acc, act_, k, s, first, last):
                pe.wait_ge(lo_ready, s + 1)
                products(acc, act_[0], act_[1], k, s % RING, first, last)

            tile_out = [[(gate_ready, 1), (h_ready_row, 1), (row_ready, 1), (row_ready, 2), (gate_ready, 2),
                         (h_ready_row, 2), (row_ready, 3), (g_silu, 1), (row_ready, 4), (row_ready, 5), (row_ready, 6),
                         (g_silu, 2)] + [(x_sum, j + 1) for j in range(PARTS * NT)],
                        [(row_ready, 7 + i) for i in range(12)] +
                        [(x_sum, (PARTS + FB) * NT + j + 1) for j in range(PARTS * NT)]]
            read_out = [
                {"C0": (pad_ready, 1), "F0": (sig_ready, 1), "Q0": (q_ready, 1), "C1": (pad_ready, 2),
                 "O0": (cat_ready, 1), "F1": (sig_ready, 2), "Q1": (q_ready, 2), "mean": (cen_ready, 1),
                 "variance": (cvar_ready, 1), "O1": (cat_ready, 3)},
                {"params": (params_ready, 1), "logits": (z_sum, 1), "F rows": (Fc_ready, 1)},
            ]
            for p in range(2):
                for which in range(4):
                    for name in pieces(which, p):
                        read_out[p][name] = (xt_ready, NP * which + name[2] + 1)
            for layer in range(DEPTH):
                for name in HIDDEN[layer]:
                    read_out[0][name] = (h_ready, FB * NT * layer + name[2] + 1)
            for g in range(4):
                read_out[0].update({("q", g): (qk_ready, 2 * g + 1), ("k", g): (qk_ready, 2 * g + 2),
                                    ("scores", g): (scores_read, 2 * g + 1), ("probs", g): (pT_act, g + 1),
                                    ("out", g): (cat_ready, 4 + g)})
                read_out[1].update({("scores", g): (scores_read, 2 * g + 2), ("probs", g): (pT_dve, g + 1)})
            for half in range(2):
                read_out[1]["F", half] = (fb_ready, RT * HG * (half + 1))
                for k in range(9):
                    read_out[1]["level", half, k] = (scores_in, 9 * half + k + 1)
                read_out[1]["level", half, 9] = (o_row, half + 1)
            pair_out = [[read_out[p][name] for name in USE[p]] for p in range(2)]

            def acquire(layer, i):
                if i >= 2:
                    pe.wait_ge(*tile_out[layer][i - 2])
                elif layer:
                    pe.wait_ge(x_sum, (PARTS + FB) * NT - 1 + i)
                return gemm[(TILE0[layer] + i) % 2]

            def pair_free(p, name):
                use = USE[p][name]
                if use:
                    pe.wait_ge(*pair_out[p][use - 1])

            def transposes(p, name, src, count=4):
                pair_free(p, name)
                for c in range(count):
                    for r in range(RT):
                        ins = pe.transpose(quad[p][:, c, r * P:(r + 1) * P], src[:, r, c * P:(c + 1) * P], ident[:, :])
                ins.then_inc(pair_full[p], 1)

            def x_piece(which, i):
                k0, n_ = PIECES[i]
                pair_free(i % 2, ("x", which, i))
                for r in range(RT):
                    if not which:
                        pe.wait_ge(x_loaded[i], 16)
                    elif i == 0 and r == 0:
                        pe.wait_ge(normed0, which)
                    else:
                        pe.wait_ge(normed, NP * (which - 1) + i + 1)
                    for c in range(n_):
                        ins = pe.transpose(quad[i % 2][:, c, r * P:(r + 1) * P], X[:, r, (k0 + c) * P:(k0 + c + 1) * P],
                                           ident[:, :])
                ins.then_inc(pair_full[i % 2], 1)

            def start_tile(which, c):
                if c == 0:
                    x_piece(which, 0)
                    x_piece(which, 1)
                    pe.wait_ge(xt_ready, NP * which + 1)
                if c == 1:
                    x_piece(which, 2)
                    pe.wait_ge(xt_ready, NP * which + 2)
                if c == (2 if which else 3):
                    x_piece(which, 3)
                if c == (2 if which else 5):
                    x_piece(which, 4)
                if c == 2:
                    pe.wait_ge(xt_ready, NP * which + 3)
                if c == 4:
                    pe.wait_ge(xt_ready, NP * which + 4)
                if c == 6:
                    pe.wait_ge(xt_ready, NP * which + 5)

            X_ = (x_hi, x_lo)
            C_ = (c_hi, c_lo)
            at = [0, 0]

            def rows_to(p, name, src, count):
                pe.wait_ge(row_ready, count)
                transposes(p, name, src)

            def level(half, k):
                pair_free(1, ("level", half, k))
                if k < 8:
                    pe.wait_ge(z_ready, 8 * half + k + 1)
                if k < LEVELS:
                    h = CHUNK >> k
                    z = Z[k % 2].rearrange("p (b t) -> p b t", t=P)
                    for b in range(2 * HG):
                        q = z[:, b, :].rearrange("p (g u r) -> p g u r", u=2, r=h)[:, :, 1, :]
                        ins = pe.matmul(pair[1][:, b * CHUNK:(b + 1) * CHUNK], z[:, b, :], q, start=True, stop=True)
                elif k == LEVELS:
                    z = Z[1].rearrange("p (h b t) -> p h b t", b=2, t=P)
                    for h in range(HG):
                        ins = pe.matmul(pair[1][:, h * P:(h + 1) * P], z[:, h, 0, :], z[:, h, 1, :], start=True, stop=True)
                else:
                    for b in range(2 * HG):
                        cols = slice((b % 2) * P, (b % 2) * P + P)
                        ins = pe.matmul(pair[1][:, b * P:(b + 1) * P], kT[:, b // 2, cols], qT[:, b // 2, cols],
                                        start=True, stop=True)
                ins.then_inc(pair_full[1], 1)

            def outputs(half, rows):
                pair_free(1, ("level", half, 9))
                pe.wait_ge(row_ready, rows)
                av = A.rearrange("p (h b t) -> p h b t", b=2, t=P)
                axv = Ax.rearrange("p (h t) -> p h t", t=P)
                for h in range(HG):
                    cols = slice(h * DH, (h + 1) * DH)
                    pe.matmul(pair[1][:, cols], av[:, h, 0, :], vrow[:, 0, cols], start=True, stop=True)
                for h in range(HG):
                    cols = slice(h * DH, (h + 1) * DH)
                    o_ = pair[1][:, N + h * DH:N + (h + 1) * DH]
                    pe.matmul(o_, axv[:, h, :], vrow[:, 0, cols], start=True, stop=False)
                    ins = pe.matmul(o_, av[:, h, 1, :], vrow[:, 1, cols], start=False, stop=True)
                ins.then_inc(pair_full[1], 1)

            def behind_even(s):
                if s == 7:
                    pe.wait_ge(const_loaded, 16 * 6)
                    pair_free(1, "params")
                    for c in range(8):
                        pe.transpose(pair[1][:, 32 * c:32 * c + CONV_W], cw_rows[0:CONV_W, c * P:(c + 1) * P],
                                     ident[0:CONV_W, 0:CONV_W])
                    pe.transpose(pair[1][:, 8 * 32:8 * 32 + 40], small_rows[0:40, :], ident[0:40, 0:40]
                                 ).then_inc(pair_full[1], 1)
                if s == 18:
                    pe.wait_ge(h_ready_row, 1)
                    transposes(0, "C0", urow[1])
                if s == 25:
                    rows_to(0, "F0", urow[0], 1)
                if s == 33:
                    rows_to(0, "Q0", urow[1], 2)
                if s == 50:
                    pe.wait_ge(h_ready_row, 2)
                    transposes(0, "C1", urow[1])
                if s == 67:
                    pe.wait_ge(o_ready, 1)
                    transposes(0, "O0", orow.rearrange("p (r n) -> p r n", r=RT))
                if s == 73:
                    rows_to(0, "F1", urow[0], 4)
                if s == 82:
                    rows_to(0, "Q1", urow[1], 5)
                for half, base in enumerate(LEVEL_SLOT):
                    k = s - base - 1
                    if 0 <= k <= 16 and k % 2 == 0:
                        level(half, k // 2)
                if s == 60:
                    outputs(0, 3)
                if s == LEVEL_SLOT[1] + 20:
                    outputs(1, 6)
                if s in (MEAN_SLOT, MEAN_SLOT + 4):
                    name = "mean" if s == MEAN_SLOT else "variance"
                    pe.wait_ge(taps_done, 1)
                    if s == MEAN_SLOT + 4:
                        pe.wait_ge(csq_ready, 1)
                    pair_free(0, name)
                    src = cv if s == MEAN_SLOT else csq
                    for c in range(8):
                        ins = pe.matmul(pair[0][:, 0:S], meanw, src[:, c, :], start=(c == 0), stop=(c == 7))
                    ins.then_inc(pair_full[0], 1)
                if s == OUT_SLOT[1] - 3:
                    pe.wait_ge(o_ready, 2)
                    transposes(0, "O1", orow.rearrange("p (r n) -> p r n", r=RT))

            def forget_logits():
                pe.wait_ge(wf_ready, 1)
                pair_free(1, "logits")
                o_ = pair[1][:, 0:S]
                for k in range(KT):
                    cols = slice(k * HEADS, k * HEADS + P)
                    pe.matmul(o_, wf_hi[:, cols], x_hi[:, k, :], start=(k == 0), stop=False)
                    pe.matmul(o_, wf_hi[:, cols], x_lo[:, k, :], start=False, stop=False)
                    ins = pe.matmul(o_, wf_lo[:, cols], x_hi[:, k, :], start=False, stop=(k == KT - 1))
                ins.then_inc(pair_full[1], 1)

            def forget_rows():
                pe.wait_ge(F_ready, 1)
                pair_free(1, "F rows")
                for r in range(RT):
                    ins = pe.transpose(pair[1][:, r * HEADS:(r + 1) * HEADS], Ft[0:HEADS, r * P:(r + 1) * P],
                                       ident[0:HEADS, 0:HEADS])
                ins.then_inc(pair_full[1], 1)

            def forget_columns(g):
                pe.wait_ge(odd_consts, 2)
                pair_free(1, ("F", g))
                for h in range(HG):
                    ins = pe.matmul(quad[1][:, h, :], sel[0:HEADS, HG * g + h, :], Ft[0:HEADS, :], start=True, stop=True)
                ins.then_inc(pair_full[1], 1)

            def scores(g):
                pe.wait_ge(qk_ready, 2 * g + 2)
                pair_free(0, ("scores", g))
                pair_free(1, ("scores", g))
                for h in range(HG):
                    ins = pe.matmul(pair[0][:, h * P:(h + 1) * P], qT[:, h, 0:P], kT[:, h, 0:P], start=True, stop=True)
                ins.then_inc(pair_full[0], 1)
                for h in range(HG):
                    ins = pe.matmul(quad[1][:, h, :], qT[:, h, P:S], kT[:, h, :], start=True, stop=True)
                ins.then_inc(pair_full[1], 1)

            def probs(g):
                pe.wait_ge(prob_ready, g + 1)
                pair_free(0, ("probs", g))
                pair_free(1, ("probs", g))
                p1 = sm[:, HG * P:].rearrange("p (h k) -> p h k", h=HG)
                for h in range(HG):
                    pe.transpose(quad[0][:, h, 0:P], sm[:, h * P:(h + 1) * P], ident[:, :])
                    ins = pe.transpose(quad[0][:, h, P:S], p1[:, h, 0:P], ident[:, :])
                ins.then_inc(pair_full[0], 1)
                for h in range(HG):
                    ins = pe.transpose(pair[1][:, h * P:(h + 1) * P], p1[:, h, P:S], ident[:, :])
                ins.then_inc(pair_full[1], 1)

            def attend(g):
                pe.wait_ge(pT_act, g + 1)
                pe.wait_ge(pT_dve, g + 1)
                pe.wait_ge(row_ready, 6 + 3 * g + 3)
                pair_free(0, ("out", g))
                a = pT[:, 0:HG * S].rearrange("p (h q) -> p h q", h=HG)
                b = pT[:, HG * S:].rearrange("p (h q) -> p h q", h=HG)
                for h in range(HG):
                    cols = slice(h * DH, (h + 1) * DH)
                    pe.matmul(quad[0][:, h, :], vrow[:, 0, cols], a[:, h, :], start=True, stop=False,
                              skip_group_check=True)
                    ins = pe.matmul(quad[0][:, h, P:S], vrow[:, 1, cols], b[:, h, :], start=False, stop=True,
                                    skip_group_check=True)
                ins.then_inc(pair_full[0], 1)

            def behind_odd(s):
                for g in range(4):
                    r = s - 24 * g
                    if r == 9:
                        rows_to(0, ("q", g), urow[0], 6 + 3 * g + 1)
                        if g == 1:
                            forget_columns(1)
                    if r == 17:
                        rows_to(0, ("k", g), urow[1], 6 + 3 * g + 2)
                    if r == 20:
                        scores(g)
                    if r == 25:
                        probs(g)
                    if r == 27:
                        attend(g)
                if s == 8:
                    forget_logits()
                if s == 12:
                    forget_rows()
                if s == 14:
                    forget_columns(0)

            pe.wait_ge(consts, 1)
            groups = [{8: 1, 0: 2, 12: 3}, {0: 4, 4: 5, 8: 6, 12: 7}]
            for layer in range(DEPTH):
                behind = (behind_even, behind_odd)[layer]
                s0 = SLOT0[layer]
                for i in range(12):
                    s, t = at
                    acc = acquire(layer, i)
                    for c in range(CPT):
                        if i == 0:
                            start_tile(2 * layer, c)
                        chunk(acc, X_, CK * c, s + c, c == 0, c == CPT - 1)
                        behind(s + c - s0)
                    at[0], at[1] = s + CPT, t + 1
                for part in (EVEN_OUT, ODD_OUT)[layer]:
                    for j in range(NT):
                        s, t = at
                        acc = acquire(layer, t - TILE0[layer])
                        for i, k in enumerate(part[::CK]):
                            if j == 0 and k in groups[layer]:
                                pe.wait_ge(cat_ready, groups[layer][k])
                            chunk(acc, C_, k, s + i, i == 0, i == len(part) // CK - 1)
                            behind(s + i - s0)
                        at[0], at[1] = s + len(part) // CK, t + 1

                base, tbase = SLOT_MLP[layer], TILE_MLP[layer]
                assert at == [base, tbase]

                def mlp_tile(b, i, first_block=False):
                    start = first_block and i == 0
                    t = tbase + i
                    acc = gemm[t % 2]
                    j = (i - 2) % (2 * NT)
                    if j < NT:
                        pe.wait_ge(relu_done, b * NT + (layer * FB * NT + j + 1))
                    else:
                        done = PARTS * NT * (layer + 1) + FB * NT * layer - NT * (i < 2)
                        pe.wait_ge(x_sum, b * NT + (done + j - NT + 1))
                    operand = X_ if i < NT else C_
                    for c in range(CPT):
                        s = base + i * CPT + c
                        if start:
                            start_tile(2 * layer + 1, c)
                        if i == NT and c % 2 == 0:
                            pe.wait_ge(h_ready, b * NT + (layer * FB * NT + c // 2 + 1))
                        pe.wait_ge(lo_ready, b * (2 * NT * CPT) + (s + 1))
                        products(acc, operand[0], operand[1], CK * c, s % RING, c == 0, c == CPT - 1)
                        if c == 1 and 1 <= i <= NT:
                            pe.wait_ge(h_row, b * NT + (layer * FB * NT + i))
                            if i == 1 and first_block:
                                pair_free(0, ("h", layer, 0))
                            else:
                                pe.wait_ge(h_ready, b * NT + (layer * FB * NT + i - 1))
                            for cc in range(4):
                                for r in range(RT):
                                    ins = pe.transpose(quad[0][:, cc, r * P:(r + 1) * P],
                                                       urow[(i - 1) % 2][:, r, cc * P:(cc + 1) * P], ident[:, :])
                            ins.then_inc(pair_full[0], 1)

                for i in range(2 * NT):
                    mlp_tile(0, i, first_block=True)
                with pe.Fori(1, FB) as b:
                    for i in range(2 * NT):
                        mlp_tile(b, i)
                at[0], at[1] = base + MLP_SLOTS, tbase + MLP_TILES


_INS = ["x", "ev_w_in", "ev_conv_w", "ev_conv_b", "ev_conv_ln_g", "ev_conv_ln_b", "hgrn_lb_logits", "ev_gnorm_g",
        "ev_w_out", "od_w_in", "fox_b_f", "rel_bias", "od_w_out", "ln_mix_g", "ln_mix_b", "mlp_w1", "mlp_w2",
        "ln_mlp_g", "ln_mlp_b"]


def kernel(**inputs):
    import numpy as np
    import concourse.bacc as bacc
    from concourse.bass_utils import run_bass_kernel_spmd

    nc = bacc.Bacc("TRN2", target_bir_lowering=False, num_devices=1)
    arrays, args = {}, []
    for name in _INS:
        a = np.ascontiguousarray(inputs[name])
        arrays[f"in_{name}"] = a
        args.append(nc.dram_tensor(f"in_{name}", a.shape, mybir.dt.from_np(a.dtype), kind="ExternalInput").ap())
    args.append(nc.dram_tensor("out_0", (1, S, D), F32, kind="ExternalOutput").ap())
    trunk(nc, *args)
    r = run_bass_kernel_spmd(nc, [arrays], core_ids=[0])
    return r.results[0]["out_0"]
```
